# Optimizing a Trainium2 kernel written in Bass

```python
import numpy as np
import jax
import jax.numpy as jnp
from jax import lax

D_MODEL = 1024
BATCH = 1
SEQ = 256
DEPTH = 2

N_BRANCH = 4
BRANCH_WIDTH = 256
Q_BLOCK = 128
EPS = 1e-6
NEG_BIG = -1e30

DSA_HEADS = 4
DSA_HEAD_DIM = 64
DSA_Q_LATENT = 128
DSA_KV_LATENT = 128
IDX_HEADS = 8
IDX_DIM = 32
TOPK_MAX = 256

RWKV_HEADS = 4
RWKV_HEAD_DIM = 64
RWKV_LORA_W = 64
RWKV_LORA_A = 64
RWKV_LORA_G = 128
RWKV_GN_EPS = 64e-5

MLSTM_HEADS = 4
MLSTM_QK_DIM = 32
MLSTM_V_DIM = 64
MLSTM_CHUNK = 64
CONV_WIDTH = 4
GATE_SOFTCAP = 15.0

FOX_HEADS = 4
FOX_HEAD_DIM = 64

D_FF_DENSE = 2816
N_EXPERTS = 8
TOP_K_EXPERTS = 2
D_FF_EXPERT = 3584
N_DENSE_LAYERS = (DEPTH + 1) // 2
N_MOE_LAYERS = DEPTH // 2

DSA_SPLITS = (DSA_Q_LATENT, DSA_KV_LATENT, IDX_DIM, IDX_HEADS)
RWKV_WIDTH = RWKV_HEADS * RWKV_HEAD_DIM
RWKV_SPLITS = (RWKV_WIDTH, RWKV_WIDTH, RWKV_WIDTH, RWKV_LORA_W, RWKV_LORA_A, RWKV_LORA_G)
MLSTM_SPLITS = (MLSTM_HEADS * MLSTM_QK_DIM, MLSTM_HEADS * MLSTM_QK_DIM, MLSTM_HEADS * MLSTM_V_DIM, MLSTM_HEADS * MLSTM_V_DIM, MLSTM_HEADS, MLSTM_HEADS)
FOX_SPLITS = (FOX_HEADS * FOX_HEAD_DIM,) * 3 + (FOX_HEADS,)
GATE_SPLITS = (D_MODEL,) * N_BRANCH
GROUP_SPLITS = (sum(DSA_SPLITS), sum(RWKV_SPLITS), sum(MLSTM_SPLITS), sum(FOX_SPLITS), sum(GATE_SPLITS))
D_IN = sum(GROUP_SPLITS)

kernel_name = 'hybrid_gated_dsa_rwkv7_mlstm_fox_moe'

def _split(z, sizes):
    return jnp.split(z, np.cumsum(sizes)[:-1].tolist(), axis=-1)

def rmsnorm(x, g, eps=EPS):
    xf = x.astype(jnp.float32)
    y = xf * lax.rsqrt(jnp.mean(xf * xf, axis=-1, keepdims=True) + eps)
    return (y * g.astype(jnp.float32)).astype(x.dtype)

def head_rmsnorm(y, g, eps=EPS):
    b, s, nh, d = y.shape
    yf = y.astype(jnp.float32)
    yf = yf * lax.rsqrt(jnp.mean(yf * yf, axis=-1, keepdims=True) + eps)
    return yf.reshape(b, s, nh * d) * g.astype(jnp.float32)

def softcap(t, cap):
    return cap * jnp.tanh(t / cap)

def causal_conv(x, w, bias):
    s = x.shape[1]
    xp = jnp.pad(x, ((0, 0), (w.shape[0] - 1, 0), (0, 0)))
    y = bias
    for j in range(w.shape[0]):
        y = y + xp[:, j:j + s] * w[j]
    return y

def _block_starts(s):
    return jnp.arange(s // Q_BLOCK) * Q_BLOCK

def dsa_mixer(c_q, c_kv, k_idx, w_idx, g_cq, g_ckv, g_kidx, w_uq, w_qidx, w_uv):
    b, s, _ = c_q.shape
    topk = min(TOPK_MAX, s // 4)
    cq = rmsnorm(c_q, g_cq)
    ckv = rmsnorm(c_kv, g_ckv)
    q = jnp.einsum('bsc,chl->bshl', cq, w_uq)
    qi = jnp.einsum('bsc,chd->bshd', cq, w_qidx)
    ki = rmsnorm(k_idx, g_kidx)
    wi = w_idx.astype(jnp.float32) * IDX_HEADS ** -0.5
    spos = jnp.arange(s)

    def block(q0):
        qb = lax.dynamic_slice_in_dim(q, q0, Q_BLOCK, axis=1)
        qib = lax.dynamic_slice_in_dim(qi, q0, Q_BLOCK, axis=1)
        wib = lax.dynamic_slice_in_dim(wi, q0, Q_BLOCK, axis=1)
        tpos = q0 + jnp.arange(Q_BLOCK)
        dots = jnp.einsum('bqhd,bsd->bqhs', qib, ki).astype(jnp.float32) * IDX_DIM ** -0.5
        score = jnp.einsum('bqh,bqhs->bqs', wib, jax.nn.relu(dots))
        score = jnp.where(spos[None, None, :] <= tpos[None, :, None], score, -jnp.inf)
        _, sel = lax.top_k(score, topk)
        valid = sel <= tpos[None, :, None]
        kv_sel = jax.vmap(lambda c, i: c[i])(ckv, sel)
        logits = jnp.einsum('bqhl,bqkl->bhqk', qb, kv_sel).astype(jnp.float32) * DSA_KV_LATENT ** -0.5
        logits = jnp.where(valid[:, None], logits, -jnp.inf)
        p = jax.nn.softmax(logits, axis=-1).astype(ckv.dtype)
        return jnp.einsum('bhqk,bqkl->bqhl', p, kv_sel)

    o = lax.map(block, _block_starts(s))
    o = jnp.moveaxis(o, 0, 1).reshape(b, s, DSA_HEADS, DSA_KV_LATENT)
    y = jnp.einsum('bshl,hld->bshd', o, w_uv)
    return y.reshape(b, s, DSA_HEADS * DSA_HEAD_DIM)

def rwkv7_mixer(z, mu, w0, w_up, a0, a_up, g_up, k_k, k_a, r_k, ln_g, ln_b):
    b, s, _ = z.shape
    nh, n = RWKV_HEADS, RWKV_HEAD_DIM
    z_prev = jnp.pad(z[:, :-1], ((0, 0), (1, 0), (0, 0)))
    z = z + mu * (z_prev - z)
    r, k, v, wd, ad, gd = _split(z, RWKV_SPLITS)
    w_log = -jax.nn.softplus(-(w0 + jnp.tanh(wd) @ w_up)) - 0.5
    decay = jnp.exp(-jnp.exp(w_log.astype(jnp.float32)))
    a = jax.nn.sigmoid((a0 + ad @ a_up).astype(jnp.float32))
    g = jax.nn.sigmoid(gd) @ g_up
    heads = lambda t: t.astype(jnp.float32).reshape(b, s, nh, n)
    kk = heads(k * k_k)
    kk = kk / jnp.maximum(jnp.linalg.norm(kk, axis=-1, keepdims=True), 1e-12)
    k = k * (1.0 + (a - 1.0) * k_a)
    rh, kh, vh, wh, ah = heads(r), heads(k), heads(v), heads(decay), heads(a)

    def step(state, inp):
        r_t, w_t, k_t, v_t, kk_t, a_t = inp
        sa = jnp.einsum('bhvk,bhk->bhv', state, -kk_t)
        state = state * w_t[:, :, None, :] + sa[..., None] * (kk_t * a_t)[:, :, None, :] + v_t[..., None] * k_t[:, :, None, :]
        return state, jnp.einsum('bhvk,bhk->bhv', state, r_t)

    xs = tuple(jnp.moveaxis(t, 1, 0) for t in (rh, wh, kh, vh, kk, ah))
    _, y = lax.scan(step, jnp.zeros((b, nh, n, n), jnp.float32), xs)
    y = jnp.moveaxis(y, 0, 1)
    mean = jnp.mean(y, axis=-1, keepdims=True)
    var = jnp.mean(jnp.square(y - mean), axis=-1, keepdims=True)
    y = ((y - mean) * lax.rsqrt(var + RWKV_GN_EPS)).reshape(b, s, nh * n) * ln_g + ln_b
    bonus = (jnp.sum(rh * kh * r_k, axis=-1, keepdims=True) * vh).reshape(b, s, nh * n)
    return ((y + bonus) * g).astype(z.dtype)

def mlstm_mixer(q, k, v, o, i_pre, f_pre, conv_w, conv_b, b_i, b_f, norm_g):
    b, s, _ = q.shape
    nh, dk, dv, lc = MLSTM_HEADS, MLSTM_QK_DIM, MLSTM_V_DIM, MLSTM_CHUNK
    nc = s // lc
    qk = jax.nn.silu(causal_conv(jnp.concatenate([q, k], axis=-1), conv_w, conv_b))
    q, k = jnp.split(qk, 2, axis=-1)

    def chunked(t, d):
        return t.reshape(b, nc, lc, nh, d).transpose(0, 3, 1, 2, 4).astype(jnp.float32)

    def gate_chunks(t):
        return t.astype(jnp.float32).reshape(b, nc, lc, nh).transpose(0, 3, 1, 2)

    qc = chunked(q, dk) * dk ** -0.5
    kc = chunked(k, dk)
    vc = chunked(v, dv)
    li = gate_chunks(softcap(i_pre + b_i, GATE_SOFTCAP))
    lf = jax.nn.log_sigmoid(gate_chunks(softcap(f_pre + b_f, GATE_SOFTCAP)))
    bcum = jnp.cumsum(lf, axis=-1)
    gtot = bcum[..., -1]
    a_log = gtot[..., None] - bcum + li
    a_max = jnp.max(a_log, axis=-1)
    a_w = jnp.exp(a_log - a_max[..., None])
    kv_chunk = jnp.einsum('bhcl,bhclv,bhcld->bhcvd', a_w, vc, kc)
    n_chunk = jnp.einsum('bhcl,bhcld->bhcd', a_w, kc)

    def step(carry, inp):
        c_st, n_st, m_st = carry
        g_c, am_c, kv_c, nk_c = inp
        m_new = jnp.maximum(g_c + m_st, am_c)
        s_old = jnp.exp(g_c + m_st - m_new)
        s_new = jnp.exp(am_c - m_new)
        c_new = s_old[..., None, None] * c_st + s_new[..., None, None] * kv_c
        n_new = s_old[..., None] * n_st + s_new[..., None] * nk_c
        return (c_new, n_new, m_new), (c_st, n_st, m_st)

    init = (jnp.zeros((b, nh, dv, dk), jnp.float32), jnp.zeros((b, nh, dk), jnp.float32), jnp.full((b, nh), NEG_BIG, jnp.float32))
    xs = (jnp.moveaxis(gtot, 2, 0), jnp.moveaxis(a_max, 2, 0), jnp.moveaxis(kv_chunk, 2, 0), jnp.moveaxis(n_chunk, 2, 0))
    _, (c_prev, n_prev, m_prev) = lax.scan(step, init, xs)
    c_prev = jnp.moveaxis(c_prev, 0, 2)
    n_prev = jnp.moveaxis(n_prev, 0, 2)
    m_prev = jnp.moveaxis(m_prev, 0, 2)
    causal = jnp.tril(jnp.ones((lc, lc), dtype=bool))
    d_intra = jnp.where(causal, bcum[..., :, None] - bcum[..., None, :] + li[..., None, :], NEG_BIG)
    m_inter = bcum + m_prev[..., None]
    m_t = jnp.maximum(m_inter, jnp.max(d_intra, axis=-1))
    w_intra = jnp.exp(d_intra - m_t[..., None]) * jnp.einsum('bhctd,bhcsd->bhcts', qc, kc)
    s_inter = jnp.exp(m_inter - m_t)
    num = jnp.einsum('bhcts,bhcsv->bhctv', w_intra, vc) + s_inter[..., None] * jnp.einsum('bhcvd,bhctd->bhctv', c_prev, qc)
    den = jnp.sum(w_intra, axis=-1) + s_inter * jnp.einsum('bhcd,bhctd->bhct', n_prev, qc)
    hcell = num / jnp.maximum(jnp.abs(den), jnp.exp(-m_t))[..., None]
    hcell = hcell.transpose(0, 2, 3, 1, 4).reshape(b, s, nh, dv)
    y = head_rmsnorm(hcell, norm_g) * jax.nn.sigmoid(o.astype(jnp.float32))
    return y.astype(v.dtype)

def fox_mixer(q, k, v, f_pre, b_f):
    b, s, _ = q.shape
    nh, d = FOX_HEADS, FOX_HEAD_DIM
    qh = q.reshape(b, s, nh, d)
    kh = k.reshape(b, s, nh, d)
    vh = v.reshape(b, s, nh, d)
    lf = jax.nn.log_sigmoid((f_pre + b_f).astype(jnp.float32))
    fcum = jnp.cumsum(lf, axis=1).transpose(0, 2, 1)
    spos = jnp.arange(s)

    def block(q0):
        qb = lax.dynamic_slice_in_dim(qh, q0, Q_BLOCK, axis=1)
        fq = lax.dynamic_slice_in_dim(fcum, q0, Q_BLOCK, axis=2)
        tpos = q0 + jnp.arange(Q_BLOCK)
        logits = jnp.einsum('bqhd,bshd->bhqs', qb, kh).astype(jnp.float32) * d ** -0.5
        logits = logits + fq[..., None] - fcum[:, :, None, :]
        logits = jnp.where(spos[None, None, None, :] <= tpos[None, None, :, None], logits, -jnp.inf)
        p = jax.nn.softmax(logits, axis=-1).astype(vh.dtype)
        return jnp.einsum('bhqs,bshd->bqhd', p, vh)

    o = lax.map(block, _block_starts(s))
    return jnp.moveaxis(o, 0, 1).reshape(b, s, nh * d)

def swiglu(t, w1, w3, w2):
    return (jax.nn.silu(t @ w1) * (t @ w3)) @ w2

def moe_swiglu(h, router, w1, w3, w2):
    b, s, d = h.shape
    t = h.reshape(b * s, d)
    logits = (t @ router).astype(jnp.float32)
    top_v, top_i = lax.top_k(logits, TOP_K_EXPERTS)
    top_p = jax.nn.softmax(top_v, axis=-1)
    gate = jnp.sum(jax.nn.one_hot(top_i, N_EXPERTS, dtype=jnp.float32) * top_p[..., None], axis=1).astype(h.dtype)
    y = jnp.zeros_like(t)
    for e in range(N_EXPERTS):
        y = y + gate[:, e:e + 1] * swiglu(t, w1[e], w3[e], w2[e])
    return y.reshape(b, s, d)

def setup_inputs(seed: int = 0) -> dict:
    key = jax.random.key(seed)
    ks = iter(jax.random.split(key, 64))

    def nrm(shape, scale):
        return jax.random.normal(next(ks), shape, jnp.float32) * scale

    def unif(shape, lo, hi):
        return jax.random.uniform(next(ks), shape, jnp.float32, lo, hi)

    def gain(shape):
        return 1.0 + nrm(shape, 0.02)

    L = DEPTH
    qk_conv = 2 * MLSTM_HEADS * MLSTM_QK_DIM
    return {
        'x': nrm((BATCH, SEQ, D_MODEL), 1.0),
        'norm_mix_g': gain((L, D_MODEL)),
        'w_in': nrm((L, D_MODEL, D_IN), D_MODEL ** -0.5),
        'dsa_g_cq': gain((L, DSA_Q_LATENT)),
        'dsa_g_ckv': gain((L, DSA_KV_LATENT)),
        'dsa_g_kidx': gain((L, IDX_DIM)),
        'dsa_w_uq': nrm((L, DSA_Q_LATENT, DSA_HEADS, DSA_KV_LATENT), DSA_Q_LATENT ** -0.5),
        'dsa_w_qidx': nrm((L, DSA_Q_LATENT, IDX_HEADS, IDX_DIM), DSA_Q_LATENT ** -0.5),
        'dsa_w_uv': nrm((L, DSA_HEADS, DSA_KV_LATENT, DSA_HEAD_DIM), DSA_KV_LATENT ** -0.5),
        'rwkv_mu': unif((L, sum(RWKV_SPLITS)), 0.0, 1.0),
        'rwkv_w0': unif((L, RWKV_WIDTH), -5.0, -1.0),
        'rwkv_w_up': nrm((L, RWKV_LORA_W, RWKV_WIDTH), 0.1),
        'rwkv_a0': nrm((L, RWKV_WIDTH), 0.1),
        'rwkv_a_up': nrm((L, RWKV_LORA_A, RWKV_WIDTH), 0.1),
        'rwkv_g_up': nrm((L, RWKV_LORA_G, RWKV_WIDTH), RWKV_LORA_G ** -0.5),
        'rwkv_k_k': 0.85 + nrm((L, RWKV_WIDTH), 0.05),
        'rwkv_k_a': 1.0 + nrm((L, RWKV_WIDTH), 0.05),
        'rwkv_r_k': nrm((L, RWKV_HEADS, RWKV_HEAD_DIM), 0.1),
        'rwkv_ln_g': gain((L, RWKV_WIDTH)),
        'rwkv_ln_b': nrm((L, RWKV_WIDTH), 0.02),
        'mlstm_conv_w': nrm((L, CONV_WIDTH, qk_conv), 0.5),
        'mlstm_conv_b': nrm((L, qk_conv), 0.02),
        'mlstm_b_i': nrm((L, MLSTM_HEADS), 0.1),
        'mlstm_b_f': 3.0 + nrm((L, MLSTM_HEADS), 0.5),
        'mlstm_norm_g': gain((L, MLSTM_HEADS * MLSTM_V_DIM)),
        'fox_b_f': 4.0 + nrm((L, FOX_HEADS), 0.5),
        'w_branch': nrm((L, N_BRANCH, BRANCH_WIDTH, D_MODEL), BRANCH_WIDTH ** -0.5),
        'w_out': nrm((L, D_MODEL, D_MODEL), D_MODEL ** -0.5),
        'norm_ffn_g': gain((L, D_MODEL)),
        'ffn_w1': nrm((N_DENSE_LAYERS, D_MODEL, D_FF_DENSE), D_MODEL ** -0.5),
        'ffn_w3': nrm((N_DENSE_LAYERS, D_MODEL, D_FF_DENSE), D_MODEL ** -0.5),
        'ffn_w2': nrm((N_DENSE_LAYERS, D_FF_DENSE, D_MODEL), D_FF_DENSE ** -0.5),
        'moe_router': nrm((N_MOE_LAYERS, D_MODEL, N_EXPERTS), D_MODEL ** -0.5),
        'moe_w1': nrm((N_MOE_LAYERS, N_EXPERTS, D_MODEL, D_FF_EXPERT), D_MODEL ** -0.5),
        'moe_w3': nrm((N_MOE_LAYERS, N_EXPERTS, D_MODEL, D_FF_EXPERT), D_MODEL ** -0.5),
        'moe_w2': nrm((N_MOE_LAYERS, N_EXPERTS, D_FF_EXPERT, D_MODEL), D_FF_EXPERT ** -0.5),
        'final_norm_g': gain((D_MODEL,)),
    }

def reference(x, norm_mix_g, w_in, dsa_g_cq, dsa_g_ckv, dsa_g_kidx, dsa_w_uq, dsa_w_qidx, dsa_w_uv, rwkv_mu, rwkv_w0, rwkv_w_up, rwkv_a0, rwkv_a_up, rwkv_g_up, rwkv_k_k, rwkv_k_a, rwkv_r_k, rwkv_ln_g, rwkv_ln_b, mlstm_conv_w, mlstm_conv_b, mlstm_b_i, mlstm_b_f, mlstm_norm_g, fox_b_f, w_branch, w_out, norm_ffn_g, ffn_w1, ffn_w3, ffn_w2, moe_router, moe_w1, moe_w3, moe_w2, final_norm_g):
    for l in range(DEPTH):
        h = rmsnorm(x, norm_mix_g[l])
        z = h @ w_in[l]
        z_dsa, z_rwkv, z_mlstm, z_fox, z_gate = _split(z, GROUP_SPLITS)
        y_dsa = dsa_mixer(*_split(z_dsa, DSA_SPLITS), dsa_g_cq[l], dsa_g_ckv[l], dsa_g_kidx[l], dsa_w_uq[l], dsa_w_qidx[l], dsa_w_uv[l])
        y_rwkv = rwkv7_mixer(z_rwkv, rwkv_mu[l], rwkv_w0[l], rwkv_w_up[l], rwkv_a0[l], rwkv_a_up[l], rwkv_g_up[l], rwkv_k_k[l], rwkv_k_a[l], rwkv_r_k[l], rwkv_ln_g[l], rwkv_ln_b[l])
        y_mlstm = mlstm_mixer(*_split(z_mlstm, MLSTM_SPLITS), mlstm_conv_w[l], mlstm_conv_b[l], mlstm_b_i[l], mlstm_b_f[l], mlstm_norm_g[l])
        y_fox = fox_mixer(*_split(z_fox, FOX_SPLITS), fox_b_f[l])
        gates = _split(jax.nn.sigmoid(z_gate.astype(jnp.float32)).astype(x.dtype), GATE_SPLITS)
        merged = jnp.zeros_like(x)
        for n, y_n in enumerate((y_dsa, y_rwkv, y_mlstm, y_fox)):
            merged = merged + gates[n] * (y_n.astype(x.dtype) @ w_branch[l, n])
        x = x + merged @ w_out[l]
        h = rmsnorm(x, norm_ffn_g[l])
        j = l // 2
        if l % 2 == 0:
            x = x + swiglu(h, ffn_w1[j], ffn_w3[j], ffn_w2[j])
        else:
            x = x + moe_swiglu(h, moe_router[j], moe_w1[j], moe_w3[j], moe_w2[j])
    return rmsnorm(x, final_norm_g)


_drawn_inputs = setup_inputs


def setup_inputs(seed=0):
    import zlib

    import numpy as np

    out = dict(_drawn_inputs(seed))
    spreads = {}
    factors = {'dsa_g_ckv': 5.774,
     'rwkv_ln_g': 2.944,
     'mlstm_b_i': 8.0,
     'mlstm_norm_g': 2.955,
     'final_norm_g': 2.688}
    for name, (base, spread) in spreads.items():
        noise = np.random.default_rng([zlib.crc32(name.encode()), seed]).standard_normal(out[name].shape)
        drawn = base * np.exp(spread * noise) if base else spread * noise
        out[name] = jnp.asarray(drawn.astype(out[name].dtype))
    for name, factor in factors.items():
        out[name] = (out[name] * factor).astype(out[name].dtype)
    return out
```

```python
import numpy as np

import concourse.bass as bass
import concourse.mybir as mybir

F32 = mybir.dt.float32
F32R = mybir.dt.float32r
ALU = mybir.AluOpType
ACT = mybir.ActivationFunctionType
AX = mybir.AxisListType

P = 128
D = 1024
T = 256
TT = T // P
KC = D // P
LAYERS = 2
FF_DENSE = 2816
FF_EXPERT = 3584
EXPERTS = 8
TOPK = 64
EPS = 1e-6
GN_EPS = 64e-5
NEG = -1e30
TAKEN = -3e38
ABSENT = -3.2e38
DECAY = float(np.exp(-0.5))

Z_RWKV, Z_ML, Z_FOX, Z_GATE = 296, 1320, 2096, 2868
GROUPS = {
    "z_ml": [(Z_ML, 256, 0), (Z_ML + 768, 4, 256), (Z_ML + 772, 4, 288), (Z_FOX + 768, 4, 320), (256, 40, 352)],
    "z_lat": [(0, 256, 0), (Z_FOX + 512, 256, 256)],
    "z_mvo": [(Z_ML + 256, 512, 0)],
    "z_fox": [(Z_FOX, 512, 0)],
    "z_rw0": [(Z_RWKV, 512, 0)],
    "z_rw1": [(Z_RWKV + 512, 512, 0)],
}
BRANCH_ORDER = [3, 2, 0, 1]
for _b, _n in enumerate(BRANCH_ORDER):
    for _h in range(2):
        GROUPS[f"gate{_b}{_h}"] = [(Z_GATE + _n * D + _h * 512, 512, 0)]

SCHEDULE = [
    "norm_mix", "z_ml", "z_lat", "ml_in", "ds_norm", "z_mvo", "ds_tr", "z_fox", "ds_q", "ml_gate", "z_rw0", "ds_dot0",
    "ml_D", "z_rw1", "ds_dot1", "ml_qk", "fx_L", "gate00", "fx_T", "ds_topk", "fx_O", "ml_T", "gate01", "ml_N",
    "br0", "ds_L", "gate10", "ml_Y", "ds_T", "gate11", "ds_O", "ds_Y",
    "rw_mix", "br1", "rw_lora", "gate20", "rw_fm", "gate21", "rw_tr", "rw_prod", "br2", "rw_x0",
    "rw_m1", "gate30", "rw_m2", "gate31", "rw_m3", "rw_m4", "rw_m5", "rw_app", "rw_state", "rw_Y", "rw_gn", "br3",
    "mrg_tr", "out0", "out1", "norm_ffn",
]

def _episodes():
    eps, alt = [], 0
    own = {
        "ds_tr": [("dT", 4), ("dTk", 5)],
        "ds_q": [("dQ0", 6), ("dQ1", 7), ("dQi", 4)],
        "ds_dot0": [("dD0_%d" % b, 4 + b) for b in range(4)],
        "ds_dot1": [("dD1_%d" % b, 4 + b) for b in range(4)],
        "ml_D": [("mD0", 4), ("mD1", 5), ("mD2", 6)],
        "ml_qk": [("mQ%d" % h, 4 + h) for h in range(4)],
        "fx_L": [("fL%d" % i, 4 + i) for i in range(4)],
        "fx_T": [("fT%d" % i, 4 + i) for i in range(3)],
        "fx_O": [("fO", 7)],
        "ml_T": [("mT%d" % i, 4 + i) for i in range(3)],
        "ml_N": [("mN", 7)],
        "ml_Y": [("mY", 4)],
        "ds_L": [("dL%d" % i, 4 + i) for i in range(4)],
        "ds_T": [("dP%d" % i, 4 + i) for i in range(3)],
        "ds_O": [("dO0", 7), ("dO1", 4)],
        "ds_Y": [("dY", 5)],
        "rw_lora": [("rKK", 7), ("rW", 4), ("rA", 5), ("rG", 6)],
        "rw_tr": [("rtV", 4), ("rtA", 5), ("rtB", 6), ("rtK", 7), ("rBon", 4)],
        "rw_prod": [("rLT%d" % h, 4 + (1 + h) % 4) for h in range(4)] + [("rKT%d" % h, 4 + (1 + h) % 4) for h in range(4)],
        "rw_x0": [("rX0_0", 4), ("rX0_1", 5)],
        "rw_app": [("rLkV", 4), ("rXA0", 5), ("rXA1", 6)],
        "rw_state": [("rRp", 7), ("rP0", 4), ("rP1", 5), ("rG0", 6), ("rG1", 7), ("rS2", 4), ("rS3", 5)],
        "rw_Y": [("rY", 6)],
        "rw_gn": [("rMean", 7), ("rVar", 4)],
    }
    for j in range(1, 6):
        own["rw_m%d" % j] = [(f"rZ{j}_0", 4), (f"rZ{j}_1", 5), (f"rX{j}_0", 6), (f"rT{j}_0", 7), (f"rX{j}_1", 4), (f"rT{j}_1", 5)]
    for s in SCHEDULE:
        if s in ("norm_mix", "norm_ffn", "mrg_tr"):
            eps += [(f"{s}{b}", b) for b in range(4)]
        elif s in GROUPS or s.startswith("out"):
            eps += [(s + "a", alt), (s + "b", alt + 1)]
            alt = 2 - alt
        elif s.startswith("br"):
            for h in range(2):
                eps += [(f"{s}{h}a", alt), (f"{s}{h}b", alt + 1)]
                alt = 2 - alt
        else:
            eps += own.get(s, [])
    return eps

EPISODES = _episodes()
EP_BANK = dict(EPISODES)
EP_IN_BANK = [[n for n, b in EPISODES if b == k] for k in range(8)]
EP_NO = {n: EP_IN_BANK[b].index(n) for n, b in EPISODES}

RING = 6
PIECE = 2048
MIX_PIECES = sum(2 if (s in GROUPS or s.startswith("out")) else 1 if s.startswith("br") else 0 for s in SCHEDULE)
DENSE_BLOCKS = FF_DENSE // P
DENSE_GROUPS = -(-DENSE_BLOCKS // 4)
DENSE_PIECES = 4 * DENSE_GROUPS + DENSE_BLOCKS // 2
EXP_GROUPS = FF_EXPERT // 512
EXP_BLOCKS = FF_EXPERT // P
EXP_PIECES = 4 * EXP_GROUPS + EXP_BLOCKS // 2
FIRST_DENSE = MIX_PIECES
FIRST_MIX = [0, MIX_PIECES + DENSE_PIECES]
FIRST_EXPERT = 2 * MIX_PIECES + DENSE_PIECES
PIECES = FIRST_EXPERT + EXPERTS * EXP_PIECES

SPLIT = 3
SPLIT_RANGES = [(FIRST_DENSE, DENSE_PIECES), (FIRST_EXPERT, EXPERTS * EXP_PIECES)]

def _columns(spec):
    at, out = 0, {}
    for name, n in spec:
        out[name] = (at, n)
        at += n
    return out, at

CONST, N_CONST = _columns([("ident", 128), ("pair_ones", 128), ("pair_mean", 128), ("negtri", 128), ("masks", 256),
                           ("level", 768), ("ident64", 64), ("reset", 256), ("ones", 256), ("before", 128),
                           ("iota", 256), ("pick", 8), ("eps", 1), ("gn_eps", 1), ("one", 1), ("is_f", 1), ("is_i", 1)])
SMALL, N_SMALL = _columns([("w_uq", 512), ("w_qidx", 256), ("w_uv", 256), ("wa_up", 256), ("g_up", 256), ("router", 64),
                           ("g_mix", 8), ("g_ffn", 8), ("mu", 8), ("w0", 2), ("a0", 2), ("k_k", 2), ("k_a", 2), ("r_k", 2),
                           ("ln_g", 2), ("ln_b", 2), ("conv_w", 8), ("conv_b", 2), ("gate_b", 1)])
ROW, N_ROW = _columns([("g_cq", 128), ("g_ckv", 128), ("g_kidx", 32), ("ml_g", 256)])


def constants():
    c = np.zeros((P, N_CONST), np.float32)
    i, j = np.arange(P)[:, None], np.arange(P)[None, :]

    def put(name, value):
        at, n = CONST[name]
        c[:, at:at + n] = value

    put("ident", i == j)
    put("pair_ones", i // 64 == j // 64)
    put("pair_mean", (i // 64 == j // 64) / 64.0)
    put("negtri", np.where(j <= i, 0.0, NEG))
    chunk = i // 64 == j // 64
    put("masks", np.concatenate([(i < j) & chunk, (i <= j) & chunk], 1))
    put("level", np.concatenate([(i < j) & (i // 2 ** (n + 1) == j // 2 ** (n + 1)) & (i // 2 ** n != j // 2 ** n)
                                 for n in range(6)], 1))
    put("ident64", (i % 64) == np.arange(64)[None, :])
    put("reset", (np.arange(256) % 64 != 0)[None, :])
    put("ones", 1.0)
    put("before", i < j)
    put("iota", np.arange(256)[None, :])
    for h in range(4):
        c[[h, 32 + h], CONST["pick"][0] + h] = 1.0
        c[64 + h, CONST["pick"][0] + 4 + h] = 1.0
    put("eps", EPS)
    put("gn_eps", GN_EPS)
    put("one", 1.0)
    put("is_f", i >= 32)
    put("is_i", i < 32)
    return c


def build(nc, x_in, stream, small_in, row_in, const_in, final_in, out):
    sems = {}

    def sem(name):
        if name not in sems:
            sems[name] = nc.alloc_semaphore(name)
        return sems[name]

    def sb(name, shape):
        return nc.alloc_sbuf_tensor(name, shape, F32)

    ring = sb("ring", [P, RING, PIECE])
    x = sb("resid", [P, TT, D])
    xn = sb("xn", [P, TT, D])
    const = sb("consts", [P, N_CONST])
    small = [sb(f"smalls{l}", [P, N_SMALL]) for l in range(LAYERS)]
    row = [sb(f"rows{l}", [P, N_ROW]) for l in range(LAYERS)]
    stat = sb("stat", [P, 256])
    over_i = nc.alloc_sbuf_tensor("over_i", [P, 1], mybir.dt.int32)
    slab_at = -(-nc.sbuf_base // 32) * 32
    SLAB = (nc.sbuf_top - slab_at) // 32 * 8
    nc.alloc_sbuf_tensor("slab", [P, SLAB], F32)
    placed = [0]

    def place(name, shape, dtype):
        n = int(np.prod(shape[1:]))
        t = nc.alloc_sbuf_tensor_at(name, shape, dtype, offset=slab_at + 4 * placed[0])
        placed[0] += n
        assert placed[0] <= SLAB, (name, placed[0], SLAB)
        return t

    ARENA = 27400
    arena = place("arena", [P, ARENA], F32)
    hT = place("hT", [P, KC, T], F32)
    placed[0] = 0
    w_h = place("w_h", [P, SPLIT, PIECE], F32R)
    w_l = place("w_l", [P, SPLIT, PIECE], F32R)
    phase = placed[0]
    hT_h = place("hT_h", [P, KC, T], F32R)
    hT_l = place("hT_l", [P, KC, T], F32R)
    denseT_h = place("denseT_h", [P, DENSE_BLOCKS, T], F32R)
    denseT_l = place("denseT_l", [P, DENSE_BLOCKS, T], F32R)
    dsil = place("dsil", [P, 4, T], F32)
    placed[0] = phase
    actT_h = place("actT_h", [P, EXP_BLOCKS, P], F32R)
    actT_l = place("actT_l", [P, EXP_BLOCKS, P], F32R)
    hsel_h = place("hsel_h", [P, KC, P], F32R)
    hsel_l = place("hsel_l", [P, KC, P], F32R)
    experts_at = placed[0]
    pb = [nc.alloc_psum_tensor(f"bank{i}", [P, 512], F32) for i in range(8)]

    def c_(name):
        at, n = CONST[name]
        return const[:, at:at + n]

    def s_(l, name):
        at, n = SMALL[name]
        return small[l][:, at:at + n]

    def r_(l, name):
        at, n = ROW[name]
        return row[l][:, at:at + n]

    top = [0]

    def area(*shape):
        n = int(np.prod(shape))
        a = arena[:, top[0]:top[0] + n]
        top[0] += n
        assert top[0] <= ARENA, top[0]
        if len(shape) == 2:
            a = a.rearrange("p (a b) -> p a b", a=shape[0])
        if len(shape) == 3:
            a = a.rearrange("p (a b c) -> p a b c", a=shape[0], b=shape[1])
        if len(shape) == 4:
            a = a.rearrange("p (a b c d) -> p a b c d", a=shape[0], b=shape[1], c=shape[2])
        return a

    yT = area(4, 2, T)
    gates = area(2, TT, D)
    Zr = area(8, T + 1)
    shared = top[0]
    z_lat = area(TT, 512)
    z_mvo = area(TT, 512)
    z_idx = area(TT, 40)
    conv_in = area(2, T + 3)
    conv = area(2, T)
    conv_s = area(2, T)
    g_pre, g_tmp, g_exp, g_cum, g_pos, g_key = (area(T) for _ in range(6))
    foxq, foxk = area(2, T), area(2, T)
    probs = area(TT, 4, T)
    probsT = area(12, P)
    relu = area(8, T)
    mlP = area(TT, 4, T)
    lat_n = area(TT, 2, P)
    lat_sq = area(TT, 2, P)
    ki4 = area(TT, 4, 32)
    ki_sq = area(TT, 32)
    latT = area(2, T)
    kiT = area(T)
    dsq = area(4, T)
    qiT = area(2, T)
    score = area(TT, T)
    best = area(TT, 8)
    dsO = relu[:, 0:4, :]
    cell = area(TT, 256)
    cell_sq = lat_sq.rearrange("p a b c -> p a (b c)")
    osig = conv_s
    attn_top = top[0]
    top[0] = shared
    kkn, t0, lw, cum, cml, Wf, sa, k2 = (area(2, T) for _ in range(8))
    AR = area(2, 2, T)
    tanh_w = area(T)
    sig_g = area(T)
    gout = area(2, T)
    Vtm, Atm, Btm, Ktm = (Zr.rearrange("p a b -> p (a b)")[:, 512 * n:512 * n + 512].rearrange("p (a b) -> p a b", a=TT) for n in range(4))
    LQ = area(4, TT, 256)
    KQ = area(4, TT, 256)
    lev = area(2, 8, P)
    X, XT, Z = area(8, P), area(8, P), area(8, P)
    Xf, Zf = X.rearrange("p a b -> p (a b)"), Z.rearrange("p a b -> p (a b)")
    RpT = Xf[:, 0:512].rearrange("p (a b) -> p a b", a=2)
    PT = Xf[:, 512:1024].rearrange("p (c a t k) -> p c a t k", c=2, a=2, t=TT)
    GW = Zf[:, 0:512].rearrange("p (c a t k) -> p c a t k", c=2, a=2, t=TT)
    S2, S3 = (Zf[:, 512 + 128 * n:640 + 128 * n].rearrange("p (a b) -> p a b", a=2) for n in range(2))
    ALV, XALV = lev[:, 0, :, :], lev[:, 1, :, :]
    Zm = area(8, T)
    bon = area(2, T)
    Ys, Yc, Yq = Wf, t0, cml
    rwkv_top = top[0]
    top[0] = max(attn_top, rwkv_top)
    mtmp = area(512)
    top[0] = experts_at
    sil = area(2, 512)
    act = area(2, 512)
    pickT = area(T)
    pick = area(TT, P)
    pickg = area(TT, P)
    yexp = area(D)
    rank = area(TT, EXPERTS + 1)
    took = area(TT, EXPERTS + 1)
    weight = area(TT, EXPERTS + 1)
    rtmp = area(TT, 64)
    over = area(8)
    assert top[0] < ARENA - D
    final_g = arena[:, ARENA - D:ARENA]

    def bank2(name, n=T):
        return pb[EP_BANK[name]][:, :].rearrange("p (a b) -> p a b", a=512 // n)

    def bank(name):
        return pb[EP_BANK[name]]

    def full(eng, l, name):
        b = EP_BANK[name]
        eng.wait_ge(sem(f"bank{b}_full"), l * len(EP_IN_BANK[b]) + EP_NO[name] + 1)

    def drained(eng, l, name):
        b = EP_BANK[name]
        eng.wait_ge(sem(f"bank{b}_free"), l * len(EP_IN_BANK[b]) + EP_NO[name] + 1)

    def freed(name):
        return sem(f"bank{EP_BANK[name]}_free")

    def begin(eng, l, name):
        b = EP_BANK[name]
        before = l * len(EP_IN_BANK[b]) + EP_NO[name]
        if before:
            eng.wait_ge(sem(f"bank{b}_free"), before)

    def filled(name):
        return sem(f"bank{EP_BANK[name]}_full")

    HEADS = [(h, h // 2, slice(64 * (h % 2), 64 * (h % 2) + 64)) for h in range(4)]

    def tsl(tt):
        return slice(tt * P, tt * P + P)

    ctx_block = nc.Block()
    block = ctx_block.__enter__()

    @block.sync
    def _(sp):
        def load(n, i=None):
            step = 0 if i is None else i * RING
            if n >= RING:
                split_before = 0
                is_split = False
                for at, count in SPLIT_RANGES:
                    if n - RING >= at + count:
                        split_before += count
                    elif n - RING >= at:
                        split_before += n - RING - at
                        is_split = True
                if is_split:
                    sp.wait_ge(sem("split_lo"), step + (split_before + 1))
                else:
                    sp.wait_ge(sem("piece_used"), step + (n - RING + 1))
            src = stream[n] if i is None else stream[bass.ds(step + n, 1)].rearrange("a p n -> (a p) n")
            sp.dma_start(ring[:, n % RING, :], src).then_inc(sem(f"piece{n % RING}_in"), 16)

        for n in range(RING):
            load(n)
        edges = sorted({at + d + RING for at, count in SPLIT_RANGES for d in (0, count)} | {RING})
        for lo, hi in zip(edges, edges[1:]):
            hi = min(hi, PIECES)
            rounds = (hi - lo) // RING
            with sp.Fori(0, rounds) as i:
                for s in range(RING):
                    load(lo + s, i)
            for n in range(lo + rounds * RING, hi):
                load(n)

        sp.wait_ge(sem("over_known"), 1)
        more = sp.value_load(over_i[0:1, 0:1], min_val=0, max_val=1)
        with sp.If(more > 0):
            with sp.Fori(0, EXPERTS) as e:
                for j in range(EXP_PIECES):
                    n = PIECES + j
                    sp.wait_ge(sem("split_lo"), e * EXP_PIECES + (DENSE_PIECES + EXPERTS * EXP_PIECES + j + 1 - RING))
                    sp.dma_start(ring[:, n % RING, :],
                                 stream[bass.ds(e * EXP_PIECES + (FIRST_EXPERT + j), 1)].rearrange("a p n -> (a p) n"))\
                      .then_inc(sem(f"piece{n % RING}_in"), 16)
        sp.wait_ge(sem("out_ready"), 1)
        sp.dma_start(out.rearrange("b (t p) d -> p (b t) d", p=P), xn[:, :, :]).then_inc(sem("out_stored"), 16)
        sp.wait_ge(sem("out_stored"), 16)

    @block.tensor
    def _(pe):
        mm = nc.tensor.matmul
        pend = [0]
        ident = c_("ident")

        def smm(o, lhsT, rhs, start, stop):
            ins = mm(o, lhsT, rhs, start=start, stop=stop)
            if pend[0]:
                ins.then_inc(sem("piece_used"), pend[0])
                pend[0] = 0
            return ins

        def arrived(n):
            pe.wait_ge(sem(f"piece{n % RING}_in"), 16 * (n // RING + 1))

        def slot(n):
            return ring[:, n % RING, :].rearrange("p (k n) -> p k n", k=4)

        def slot2(n):
            return ring[:, n % RING, :].rearrange("p (k n) -> p k n", k=2)

        nxt = [0]

        def tm_group(outs, lhs, n0, at=0, width=512):
            for tt in range(TT):
                for k in range(KC):
                    if tt == 0 and k % 4 == 0:
                        arrived(n0 + k // 4)
                    ins = smm(outs[tt], lhs[:, k, tsl(tt)], slot(n0 + k // 4)[:, k % 4, at:at + width], k == 0, k == KC - 1)
                    if tt == TT - 1 and k == 3:
                        ins.then_inc(sem("piece_used"), 1)
            return ins

        def fm_block(o, n0, at, width, last=False):
            for k in range(KC):
                if k % 4 == 0:
                    arrived(n0 + k // 4)
                ins = smm(o, slot(n0 + k // 4)[:, k % 4, at:at + width], hT[:, k, :], k == 0, k == KC - 1)
                if last and k == 3:
                    ins.then_inc(sem("piece_used"), 1)
            return ins

        def norm_transposes(l, step, j):
            for b in range(4):
                begin(pe, l, f"{step}{b}")
                for kk in range(2):
                    for tt in range(TT):
                        if b == 0 and kk == 0:
                            pe.wait_ge(sem("normed"), TT * j + tt + 1)
                        ins = nc.tensor.transpose(pb[b][:, kk * T + tt * P:kk * T + tt * P + P],
                                                  xn[:, tt, (2 * b + kk) * P:(2 * b + kk + 1) * P], ident)
                ins.then_inc(filled(f"{step}{b}"), 1)

        def z_group(l, step):
            n0 = nxt[0]
            nxt[0] += 2
            a, b = step + "a", step + "b"
            fm_layout = step in ("z_ml", "z_fox", "z_rw0", "z_rw1")
            if step == "z_ml":
                drained(pe, l, "norm_mix3")
                drained(pe, l, "norm_mix1")
            begin(pe, l, a)
            if not fm_layout:
                for tt, ep in ((0, a), (1, b)):
                    if tt:
                        begin(pe, l, b)
                    for k in range(KC):
                        if tt == 0 and k % 4 == 0:
                            arrived(n0 + k // 4)
                        ins = smm(bank(ep)[:, :], hT[:, k, tsl(tt)], slot(n0 + k // 4)[:, k % 4, :], k == 0, k == KC - 1)
                        if tt == 1 and k == 3:
                            ins.then_inc(sem("piece_used"), 1)
                    ins.then_inc(filled(ep), 1)
                pend[0] = 1
                return
            fm_block(bank2(a)[:, 0, :], n0, 0, P)
            fm_block(bank2(a)[:, 1, :], n0, P, P).then_inc(filled(a), 1)
            begin(pe, l, b)
            if step == "z_ml":
                fm_block(bank(b)[0:96, 0:T], n0, 256, 96)
                for tt in range(TT):
                    for k in range(KC):
                        ins = smm(bank(b)[:, T + 40 * tt:T + 40 * tt + 40], hT[:, k, tsl(tt)],
                                  slot(n0 + k // 4)[:, k % 4, 352:392], k == 0, k == KC - 1)
                        if tt == 1 and k == 3:
                            ins.then_inc(sem("piece_used"), 1)
                ins.then_inc(filled(b), 1)
            else:
                fm_block(bank2(b)[:, 0, :], n0, 2 * P, P)
                fm_block(bank2(b)[:, 1, :], n0, 3 * P, P, last=True).then_inc(filled(b), 1)
            pend[0] = 1

        def branch(l, bi):
            n = nxt[0]
            nxt[0] += 1
            yi = BRANCH_ORDER[bi]
            arrived(n)
            drained(pe, l, {3: "fO", 2: "mY", 0: "dY", 1: "rVar"}[yi])
            if yi == 1:
                pe.wait_ge(sem("rwkv_out"), l + 1)
            for half in range(2):
                for tt, ep in ((0, f"br{bi}{half}a"), (1, f"br{bi}{half}b")):
                    begin(pe, l, ep)
                    for k in range(2):
                        ins = smm(bank(ep)[:, :], yT[:, yi, k, tsl(tt)], slot2(n)[:, k, half * 512:half * 512 + 512], k == 0, k == 1)
                    ins.then_inc(filled(ep), 1)
            pend[0] = 1

        def merged_transposes(l):
            pe.wait_ge(sem("merged"), l + 1)
            for b in range(4):
                begin(pe, l, f"mrg_tr{b}")
                for kk in range(2):
                    for tt in range(TT):
                        ins = nc.tensor.transpose(pb[b][:, kk * T + tt * P:kk * T + tt * P + P],
                                                  xn[:, tt, (2 * b + kk) * P:(2 * b + kk + 1) * P], ident)
                ins.then_inc(filled(f"mrg_tr{b}"), 1)

        def out_group(l, half):
            n0 = nxt[0]
            nxt[0] += 2
            if half == 0:
                drained(pe, l, "mrg_tr1")
                drained(pe, l, "mrg_tr3")
            for tt, ep in ((0, f"out{half}a"), (1, f"out{half}b")):
                begin(pe, l, ep)
                for k in range(KC):
                    if tt == 0 and k % 4 == 0:
                        arrived(n0 + k // 4)
                    ins = smm(bank(ep)[:, :], hT[:, k, tsl(tt)], slot(n0 + k // 4)[:, k % 4, :], k == 0, k == KC - 1)
                    if tt == 1 and k == 3:
                        ins.then_inc(sem("piece_used"), 1)
                ins.then_inc(filled(ep), 1)
            pend[0] = 1

        def ds_tr(l):
            pe.wait_ge(sem("lat_normed"), l + 1)
            begin(pe, l, "dT")
            for w in range(2):
                for tt in range(TT):
                    ins = nc.tensor.transpose(bank("dT")[:, w * T + tt * P:w * T + tt * P + P], lat_n[:, tt, w, :], ident)
            ins.then_inc(filled("dT"), 1)
            begin(pe, l, "dTk")
            for tt in range(TT):
                ins = nc.tensor.transpose(bank("dTk")[:, tsl(tt)], ki4[:, tt, :, :].rearrange("p a b -> p (a b)"), ident)
            ins.then_inc(filled("dTk"), 1)

        def ds_q(l):
            drained(pe, l, "dT")
            for i in range(2):
                begin(pe, l, f"dQ{i}")
                for j in range(2):
                    h = 2 * i + j
                    ins = mm(bank2(f"dQ{i}")[:, j, :], s_(l, "w_uq")[:, h * P:h * P + P], latT[:, 0, :], start=True, stop=True)
                ins.then_inc(filled(f"dQ{i}"), 1)
            begin(pe, l, "dQi")
            for j in range(2):
                ins = mm(bank2("dQi")[:, j, :], s_(l, "w_qidx")[:, j * P:j * P + P], latT[:, 0, :], start=True, stop=True)
            ins.then_inc(filled("dQi"), 1)

        def ds_dot(l, tt):
            drained(pe, l, "dQi")
            drained(pe, l, "dTk")
            for b in range(4):
                ep = f"dD{tt}_{b}"
                begin(pe, l, ep)
                for j in range(2):
                    ins = mm(bank2(ep)[:, j, 0:P * (tt + 1)], qiT[32 * b:32 * b + 32, j, tsl(tt)],
                             kiT[32 * b:32 * b + 32, 0:P * (tt + 1)], start=True, stop=True, tile_position=(32 * b, 0))
                ins.then_inc(filled(ep), 1)

        def causal(o, tt):
            return mm(o[:, tt * P:tt * P + P], ident, c_("negtri"), start=False, stop=True)

        def ds_L(l):
            pe.wait_ge(sem("topk_mask"), l + 1)
            drained(pe, l, "dQ1")
            for i in range(4):
                tt, ns = i // 2, P * (i // 2 + 1)
                begin(pe, l, f"dL{i}")
                for j in range(2):
                    h = 2 * (i % 2) + j
                    o = bank2(f"dL{i}")[:, j, 0:ns]
                    mm(o, dsq[:, h, tsl(tt)], latT[:, 1, 0:ns], start=True, stop=False)
                    ins = mm(o, ident, score[:, tt, 0:ns], start=False, stop=True)
                ins.then_inc(filled(f"dL{i}"), 1)

        def probs_transposes(l, eps, src):
            for i, ep in enumerate(eps):
                begin(pe, l, ep)
                for j in range(4):
                    h, tt, sblk = (j, 0, 0) if i == 0 else (2 * (i - 1) + j // 2, 1, j % 2)
                    ins = nc.tensor.transpose(bank(ep)[:, j * P:j * P + P], src[:, tt, h, sblk * P:sblk * P + P], ident)
                ins.then_inc(filled(ep), 1)

        def pT(h, tt, sblk):
            return probsT[:, h if tt == 0 else 4 + 2 * h + sblk, :]

        def ds_O(l):
            drained(pe, l, "dP0")
            drained(pe, l, "dP1")
            drained(pe, l, "dP2")
            for i in range(2):
                begin(pe, l, f"dO{i}")
                for j in range(2):
                    h = 2 * i + j
                    for tt in range(TT):
                        for sblk in range(tt + 1):
                            ins = mm(bank2(f"dO{i}")[:, j, tsl(tt)], lat_n[:, sblk, 1, :], pT(h, tt, sblk),
                                     start=sblk == 0, stop=sblk == tt)
                ins.then_inc(filled(f"dO{i}"), 1)

        def ds_Y(l):
            drained(pe, l, "dO0")
            drained(pe, l, "dO1")
            begin(pe, l, "dY")
            for h, blk, ps in HEADS:
                ins = mm(bank2("dY")[ps, blk, :], s_(l, "w_uv")[:, h * 64:h * 64 + 64], dsO[:, h, :], start=True, stop=True)
            ins.then_inc(filled("dY"), 1)

        def decay_logits(o, row_, tt, ns):
            pk = const[0:96, CONST["pick"][0] + row_:CONST["pick"][0] + row_ + 1]
            mm(o, g_pos[0:96, tsl(tt)], pk.broadcast_to([96, ns]), start=False, stop=False)
            mm(o, pk.broadcast_to([96, P]), g_key[0:96, 0:ns], start=False, stop=False)

        def ml_D(l):
            pe.wait_ge(sem("gate_sums"), l + 1)
            for i in range(3):
                tt = 0 if i == 0 else 1
                ns = P * (tt + 1)
                begin(pe, l, f"mD{i}")
                for j in range(512 // ns):
                    h = j if i == 0 else 2 * (i - 1) + j
                    o = bank(f"mD{i}")[:, j * ns:j * ns + ns]
                    pk = const[0:96, CONST["pick"][0] + h:CONST["pick"][0] + h + 1]
                    mm(o, g_pos[0:96, tsl(tt)], pk.broadcast_to([96, ns]), start=True, stop=False)
                    mm(o, pk.broadcast_to([96, P]), g_key[0:96, 0:ns], start=False, stop=False)
                    ins = causal(o, tt)
                ins.then_inc(filled(f"mD{i}"), 1)

        def ml_qk(l):
            pe.wait_ge(sem("conv_done"), l + 1)
            for h in range(4):
                ep = f"mQ{h}"
                begin(pe, l, ep)
                hs = slice(32 * h, 32 * h + 32)
                mm(bank(ep)[:, 0:P], conv[hs, 0, 0:P], conv[hs, 1, 0:P], start=True, stop=True, tile_position=(32 * h, 0))
                mm(bank(ep)[:, P:P + T], conv[hs, 0, P:T], conv[hs, 1, :], start=True, stop=True, tile_position=(32 * h, 0))\
                    .then_inc(filled(ep), 1)

        def ml_N(l):
            for i in range(3):
                drained(pe, l, f"mT{i}")
            begin(pe, l, "mN")
            for tt in range(TT):
                for h in range(4):
                    for sblk in range(tt + 1):
                        ins = mm(bank("mN")[:, tt * 256 + h * 64:tt * 256 + h * 64 + 64], pT(h, tt, sblk),
                                 z_mvo[:, sblk, h * 64:h * 64 + 64], start=sblk == 0, stop=sblk == tt)
            ins.then_inc(filled("mN"), 1)

        def ml_Y(l):
            pe.wait_ge(sem("ml_cell"), l + 1)
            begin(pe, l, "mY")
            for blk in range(2):
                for tt in range(TT):
                    ins = nc.tensor.transpose(bank2("mY")[:, blk, tsl(tt)], cell[:, tt, blk * P:blk * P + P], ident)
            ins.then_inc(filled("mY"), 1)

        def fx_L(l):
            pe.wait_ge(sem("gate_sums"), l + 1)
            drained(pe, l, "z_foxa")
            drained(pe, l, "z_foxb")
            for i in range(4):
                tt, ns = i // 2, P * (i // 2 + 1)
                begin(pe, l, f"fL{i}")
                for j in range(2):
                    h = i % 2 + 2 * j
                    ps = HEADS[h][2]
                    o = bank2(f"fL{i}")[:, j, 0:ns]
                    mm(o, foxq[ps, j, tsl(tt)], foxk[ps, j, 0:ns], start=True, stop=False)
                    decay_logits(o, 4 + h, tt, ns)
                    ins = causal(o, tt)
                ins.then_inc(filled(f"fL{i}"), 1)

        def fx_O(l):
            for i in range(3):
                drained(pe, l, f"fT{i}")
            begin(pe, l, "fO")
            for h, blk, ps in HEADS:
                for tt in range(TT):
                    for sblk in range(tt + 1):
                        ins = mm(bank2("fO")[ps, blk, tsl(tt)], z_lat[:, sblk, 256 + h * 64:256 + h * 64 + 64], pT(h, tt, sblk),
                                 start=sblk == 0, stop=sblk == tt)
            ins.then_inc(filled("fO"), 1)

        def rw_lora(l):
            pe.wait_ge(sem("rw_kksq"), l + 1)
            begin(pe, l, "rKK")
            mm(bank("rKK")[:, :], c_("pair_ones"), t0.rearrange("p a b -> p (a b)"), start=True, stop=True)\
                .then_inc(filled("rKK"), 1)
            pe.wait_ge(sem("rw_lora_in"), l + 1)
            for ep, w, rhs in (("rW", s_(l, "wa_up")[0:64, :], tanh_w[0:64, :]),
                               ("rA", s_(l, "wa_up")[64:128, :], Zm[64:128, 6, :]),
                               ("rG", s_(l, "g_up"), sig_g)):
                begin(pe, l, ep)
                for blk in range(2):
                    ins = mm(bank2(ep)[:, blk, :], w[:, blk * P:blk * P + P], rhs, start=True, stop=True)
                ins.then_inc(filled(ep), 1)

        def rw_tr(l):
            def turn(ep, src):
                begin(pe, l, ep)
                for tt in range(TT):
                    for blk in range(2):
                        ins = nc.tensor.transpose(bank(ep)[:, tt * 256 + blk * P:tt * 256 + blk * P + P], src(blk, tt), ident)
                ins.then_inc(filled(ep), 1)
            turn("rtV", lambda blk, tt: Zm[:, 4 + blk, tsl(tt)])
            pe.wait_ge(sem("rw_fm_done"), l + 1)
            turn("rtA", lambda blk, tt: AR[:, blk, 0, tsl(tt)])
            turn("rtB", lambda blk, tt: sa[:, blk, tsl(tt)])
            turn("rtK", lambda blk, tt: k2[:, blk, tsl(tt)])
            begin(pe, l, "rBon")
            mm(bank("rBon")[:, :], c_("pair_ones"), t0.rearrange("p a b -> p (a b)"), start=True, stop=True)\
                .then_inc(filled("rBon"), 1)

        def rw_prod(l):
            for pre, src in (("rLT", sa), ("rKT", k2)):
                for h, blk, ps in HEADS:
                    ep = f"{pre}{h}"
                    begin(pe, l, ep)
                    for tt in range(TT):
                        ins = mm(bank2(ep)[:, tt, :].rearrange("p (a b) -> p a b", a=2), src[ps, blk, tsl(tt)],
                                 AR[ps, blk, :, tsl(tt)], start=True, stop=True)
                    ins.then_inc(filled(ep), 1)

        def rw_x0(l):
            pe.wait_ge(sem("rw_xt0"), l + 1)
            for i in range(2):
                begin(pe, l, f"rX0_{i}")
                for j in range(4):
                    ins = nc.tensor.transpose(bank(f"rX0_{i}")[:, j * P:j * P + P], XT[:, 4 * i + j, :], ident)
                ins.then_inc(filled(f"rX0_{i}"), 1)

        def rw_merge(l, j):
            pe.wait_ge(sem("rw_level"), 5 * l + j)
            for i in range(2):
                drained(pe, l, f"rX{j - 1}_{i}")
                if j > 1:
                    drained(pe, l, f"rT{j - 1}_{i}")
                ep = f"rZ{j}_{i}"
                begin(pe, l, ep)
                for q in range(4 * i, 4 * i + 4):
                    ins = mm(bank(ep)[:, (q % 4) * P:(q % 4) * P + P], lev[:, j % 2, q, :], X[:, q, :], start=True, stop=True)
                ins.then_inc(filled(ep), 1)
            for i in range(2):
                drained(pe, l, f"rZ{j}_{i}")
                for ep, lhs, rhs in ((f"rX{j}_{i}", XT, Z), (f"rT{j}_{i}", Z, XT)):
                    begin(pe, l, ep)
                    for q in range(4 * i, 4 * i + 4):
                        ins = mm(bank(ep)[:, (q % 4) * P:(q % 4) * P + P], lhs[:, q, :], rhs[:, q, :], start=True, stop=True)
                    ins.then_inc(filled(ep), 1)

        def rw_app(l):
            drained(pe, l, "rtV")
            drained(pe, l, "rKT3")
            begin(pe, l, "rLkV")
            for h in range(4):
                for tt in range(TT):
                    q = 2 * h + tt
                    ins = mm(bank("rLkV")[:, q * 64:q * 64 + 64], KQ[:, h, tt, 0:P], Vtm[:, tt, h * 64:h * 64 + 64],
                             start=True, stop=True)
            ins.then_inc(filled("rLkV"), 1)
            pe.wait_ge(sem("rw_alv"), l + 1)
            for i in range(2):
                drained(pe, l, f"rT5_{i}")
                begin(pe, l, f"rXA{i}")
                for q in range(4 * i, 4 * i + 4):
                    ins = mm(bank(f"rXA{i}")[:, (q % 4) * P:(q % 4) * P + P], XT[:, q, :], ALV[:, q, :], start=True, stop=True)
                ins.then_inc(filled(f"rXA{i}"), 1)

        def rw_state(l):
            drained(pe, l, "rtB")
            drained(pe, l, "rtK")
            drained(pe, l, "rXA0")
            drained(pe, l, "rXA1")
            begin(pe, l, "rRp")
            for h, blk, ps in HEADS:
                for tt in range(TT):
                    ins = mm(bank2("rRp")[ps, blk, tsl(tt)], XALV[:, 2 * h + tt, 0:64], LQ[:, h, tt, P:2 * P], start=True, stop=True)
            ins.then_inc(filled("rRp"), 1)
            for c in range(2):
                cs = slice(64 * c, 64 * c + 64)
                begin(pe, l, f"rP{c}")
                for h, blk, ps in HEADS:
                    for tt in range(TT):
                        at = (blk * 2 + tt) * 64
                        ins = mm(bank(f"rP{c}")[ps, at:at + 64], XALV[cs, 2 * h + tt, 0:64], Btm[cs, tt, h * 64:h * 64 + 64],
                                 start=True, stop=True)
                ins.then_inc(filled(f"rP{c}"), 1)
            for c in range(2):
                cs = slice(64 * c, 64 * c + 64)
                begin(pe, l, f"rG{c}")
                for h, blk, ps in HEADS:
                    for tt in range(TT):
                        at = (blk * 2 + tt) * 64
                        o = bank(f"rG{c}")[ps, at:at + 64]
                        mm(o, Btm[cs, tt, h * 64:h * 64 + 64], XALV[cs, 2 * h + tt, 64:128], start=True, stop=False)
                        ins = mm(o, Ktm[cs, tt, h * 64:h * 64 + 64], Vtm[cs, tt, h * 64:h * 64 + 64], start=False, stop=True)
                ins.then_inc(filled(f"rG{c}"), 1)
            drained(pe, l, "rP1")
            drained(pe, l, "rG0")
            drained(pe, l, "rG1")
            for ep, c, tt, prev in (("rS2", 1, 0, lambda blk: GW[:, 0, blk, 0, :]), ("rS3", 0, 1, lambda blk: S2[:, blk, :])):
                if ep == "rS3":
                    drained(pe, l, "rS2")
                begin(pe, l, ep)
                for h, blk, ps in HEADS:
                    ins = mm(bank(ep)[ps, blk * 64:blk * 64 + 64], PT[ps, c, blk, tt, :], prev(blk)[ps, :], start=True, stop=True)
                ins.then_inc(filled(ep), 1)

        def rw_Y(l):
            drained(pe, l, "rRp")
            drained(pe, l, "rS3")
            begin(pe, l, "rY")
            entering = {1: lambda blk: GW[:, 0, blk, 0, :], 2: lambda blk: S2[:, blk, :], 3: lambda blk: S3[:, blk, :]}
            for h, blk, ps in HEADS:
                for tt in range(TT):
                    q = 2 * h + tt
                    o = bank2("rY")[ps, blk, tsl(tt)]
                    mm(o, XALV[:, q, 64:128], LQ[:, h, tt, P:2 * P], start=True, stop=False)
                    mm(o, Vtm[:, tt, h * 64:h * 64 + 64], KQ[:, h, tt, P:2 * P], start=False, stop=False)
                    for c in range(2):
                        n = 2 * tt + c
                        if n:
                            ins = mm(bank2("rY")[ps, blk, n * 64:n * 64 + 64], entering[n](blk)[ps, :],
                                     RpT[ps, blk, n * 64:n * 64 + 64], start=False, stop=c == 1)
            ins.then_inc(filled("rY"), 1)

        def rw_gn(l):
            drained(pe, l, "rY")
            begin(pe, l, "rMean")
            mm(bank("rMean")[:, :], c_("pair_mean"), Ys.rearrange("p a b -> p (a b)"), start=True, stop=True)\
                .then_inc(filled("rMean"), 1)
            pe.wait_ge(sem("rw_ysq"), l + 1)
            begin(pe, l, "rVar")
            mm(bank("rVar")[:, :], c_("pair_mean"), Yq.rearrange("p a b -> p (a b)"), start=True, stop=True)\
                .then_inc(filled("rVar"), 1)

        def mixer(l):
            nxt[0] = FIRST_MIX[l]
            for step in SCHEDULE:
                if step == "norm_mix":
                    norm_transposes(l, step, 2 * l)
                elif step == "norm_ffn":
                    norm_transposes(l, step, 2 * l + 1)
                elif step in GROUPS:
                    z_group(l, step)
                elif step[:2] == "br":
                    branch(l, int(step[2]))
                elif step == "mrg_tr":
                    merged_transposes(l)
                elif step[:3] == "out":
                    out_group(l, int(step[3]))
                elif step == "ds_tr":
                    ds_tr(l)
                elif step == "ds_q":
                    ds_q(l)
                elif step[:6] == "ds_dot":
                    ds_dot(l, int(step[6]))
                elif step == "ds_L":
                    ds_L(l)
                elif step == "ds_T":
                    pe.wait_ge(sem("ds_probs"), l + 1)
                    probs_transposes(l, ["dP0", "dP1", "dP2"], probs)
                elif step == "ds_O":
                    ds_O(l)
                elif step == "ds_Y":
                    ds_Y(l)
                elif step == "ml_D":
                    ml_D(l)
                elif step == "ml_qk":
                    ml_qk(l)
                elif step == "ml_T":
                    drained(pe, l, "mQ3")
                    probs_transposes(l, ["mT0", "mT1", "mT2"], mlP)
                elif step == "ml_N":
                    ml_N(l)
                elif step == "ml_Y":
                    ml_Y(l)
                elif step == "fx_L":
                    fx_L(l)
                elif step == "fx_T":
                    pe.wait_ge(sem("fx_probs"), l + 1)
                    probs_transposes(l, ["fT0", "fT1", "fT2"], probs)
                elif step == "fx_O":
                    fx_O(l)
                elif step == "rw_lora":
                    rw_lora(l)
                elif step == "rw_tr":
                    rw_tr(l)
                elif step == "rw_prod":
                    rw_prod(l)
                elif step == "rw_x0":
                    rw_x0(l)
                elif step[:4] == "rw_m" and step[4:].isdigit():
                    rw_merge(l, int(step[4]))
                elif step == "rw_app":
                    rw_app(l)
                elif step == "rw_state":
                    rw_state(l)
                elif step == "rw_Y":
                    rw_Y(l)
                elif step == "rw_gn":
                    rw_gn(l)

        def parts(o, lhs, rhs, first, last):
            (lh, ll), (rh, rl) = lhs, rhs
            a = smm(o, lh, rh, first, False)
            smm(o, lh, rl, False, False)
            return a, smm(o, ll, rh, False, last)

        def wparts(n, k, width, cols):
            return tuple(w[:, n % SPLIT, :].rearrange("p (k n) -> p k n", n=width)[:, k, cols] for w in (w_h, w_l))

        def dense():
            drained(pe, 0, "norm_ffn3")
            for g in range(DENSE_GROUPS):
                base = 0 if g % 2 else 4
                blocks = range(4 * g, min(4 * g + 4, DENSE_BLOCKS))
                for w in range(2):
                    n0 = FIRST_DENSE + 4 * g + 2 * w
                    for b in blocks:
                        if w == 0 and b >= 8:
                            pe.wait_ge(sem("dense_mul"), b - 7)
                        for k in range(KC):
                            if b == blocks[0] and k % 4 == 0:
                                pe.wait_ge(sem("split_lo"), n0 - FIRST_DENSE + k // 4 + 1)
                            c = (b - 4 * g) * P
                            first, last = parts(pb[base + b % 4][:, w * T:w * T + T], wparts(n0 + k // 4, k % 4, 512, slice(c, c + P)),
                                                (hT_h[:, k, :], hT_l[:, k, :]), k == 0, k == KC - 1)
                            if b == blocks[-1] and k == 4:
                                first.then_inc(sem("piece_used"), 1)
                        if w == 1:
                            last.then_inc(sem("dense_up"), 1)
                    pend[0] = 1
            for c in range(DENSE_BLOCKS // 2):
                n = FIRST_DENSE + 4 * DENSE_GROUPS + c
                pe.wait_ge(sem("split_lo"), 4 * DENSE_GROUPS + c + 1)
                if c == 0:
                    pe.wait_ge(sem("dense_mul"), 4 * (DENSE_GROUPS - 1))
                pe.wait_ge(sem("dense_act"), 2 * c + 2)
                for k in range(2):
                    b = 2 * c + k
                    for tt in range(TT):
                        for half in range(2):
                            _, last = parts(pb[4 + 2 * tt + half][:, :], (denseT_h[:, b, tsl(tt)], denseT_l[:, b, tsl(tt)]),
                                            wparts(n, k, D, slice(half * 512, half * 512 + 512)), b == 0, b == DENSE_BLOCKS - 1)
                pend[0] = 1
            last.then_inc(sem("dense_down"), 1)

        pe.wait_ge(sem("const_in"), 16)
        pe.wait_ge(sem("small_in"), 32 * LAYERS)
        mixer(0)
        dense()
        mixer(1)

        def route():
            drained(pe, 1, "norm_ffn1")
            drained(pe, 1, "norm_ffn3")
            for tt in range(TT):
                for k in range(KC):
                    ins = mm(pb[4][:, tt * 8:tt * 8 + 8], hT[:, k, tsl(tt)], s_(1, "router")[:, k * 8:k * 8 + 8], start=k == 0, stop=k == KC - 1)
            ins.then_inc(sem("router_logits"), 1)
            pe.wait_ge(sem("took_done"), 1)
            E1 = EXPERTS + 1
            mm(pb[5][:, 0:E1], c_("before"), took[:, 0, :], start=True, stop=True)
            mm(pb[5][:, E1:2 * E1], c_("ones")[:, 0:P], took[:, 0, :], start=True, stop=False)
            mm(pb[5][:, E1:2 * E1], c_("before"), took[:, 1, :], start=False, stop=True)
            mm(pb[5][:, 2 * E1:3 * E1], c_("ones")[:, 0:P], took[:, 0, :], start=True, stop=False)
            mm(pb[5][:, 2 * E1:3 * E1], c_("ones")[:, 0:P], took[:, 1, :], start=False, stop=True).then_inc(sem("ranks"), 1)

        def gather(tag):
            for b in range(2):
                for j in range(4):
                    k = 4 * b + j
                    for tt in range(TT):
                        ins = mm(pb[2 + b][:, j * P:j * P + P], xn[:, tt, k * P:k * P + P], pick[:, tt, :], start=tt == 0, stop=tt == 1)
                ins.then_inc(sem(tag + "gathered"), 1)
            for tt in range(TT):
                ins = nc.tensor.transpose(pb[7][:, tsl(tt)], pickg[:, tt, :], ident)
            ins.then_inc(sem(tag + "gathered"), 1)

        def experts(tag, first):
            split0 = DENSE_PIECES + first - FIRST_EXPERT
            pe.wait_ge(sem(tag + "ready"), 1)
            pe.wait_ge(sem(tag + "pick"), 1)
            gather(tag)
            for half in range(2):
                ins = mm(pb[4 + half][:, :], yexp[:, 0:P], yexp[:, 0:512], start=True, stop=True)
            ins.then_inc(sem(tag + "down"), 1)
            with pe.Fori(0, EXPERTS) as e:
                def up(g):
                    for w in range(2):
                        n0 = first + 4 * g + 2 * w
                        b = 2 * (g % 2) + w
                        if w == 0 and g >= 2:
                            pe.wait_ge(sem(tag + "act"), e * EXP_GROUPS + (g - 1))
                        for k in range(KC):
                            if k % 4 == 0:
                                pe.wait_ge(sem("split_lo"), e * EXP_PIECES + (split0 + 4 * g + 2 * w + k // 4 + 1))
                            a, last = parts(pb[b][:, :], (hsel_h[:, k, :], hsel_l[:, k, :]),
                                            wparts(n0 + k // 4, k % 4, 512, slice(0, 512)), k == 0, k == KC - 1)
                            if k == 4:
                                a.then_inc(sem("piece_used"), 1)
                        if w == 1:
                            last.then_inc(sem(tag + "up"), 1)
                        pend[0] = 1

                def turn(g):
                    pe.wait_ge(sem(tag + "act"), e * EXP_GROUPS + (g + 1))
                    if g >= 1:
                        pe.wait_ge(sem(tag + "actT"), e * EXP_GROUPS + g)
                    for j in range(4):
                        ins = nc.tensor.transpose(pb[6][:, j * P:j * P + P], act[:, g % 2, j * P:j * P + P], ident)
                    ins.then_inc(sem(tag + "turned"), 1)

                def scatter(tt):
                    for half in range(2):
                        if tt == 1:
                            pe.wait_ge(sem(tag + "added"), e * 4 + (half + 1))
                        mm(pb[4 + half][:, :], pickT[:, tsl(tt)], yexp[:, half * 512:half * 512 + 512], start=True, stop=True)\
                            .then_inc(sem(tag + "scattered"), 1)

                pend[0] = 1
                pe.wait_ge(sem(tag + "hsel"), e + 1)
                up(0)
                pe.wait_ge(sem(tag + "yexp"), e + 1)
                scatter(0)
                up(1)
                turn(0)
                scatter(1)
                for g in range(2, EXP_GROUPS):
                    up(g)
                    turn(g - 1)
                pe.wait_ge(sem(tag + "pick"), e + 2)
                pe.wait_ge(sem(tag + "pickT"), e + 1)
                gather(tag)
                turn(EXP_GROUPS - 1)
                pe.wait_ge(sem(tag + "added"), e * 4 + 4)
                for c in range(EXP_BLOCKS // 2):
                    n = first + 4 * EXP_GROUPS + c
                    pe.wait_ge(sem("split_lo"), e * EXP_PIECES + (split0 + 4 * EXP_GROUPS + c + 1))
                    if c % 2 == 0:
                        pe.wait_ge(sem(tag + "actT"), e * EXP_GROUPS + (c // 2 + 1))
                    for k in range(2):
                        b = 2 * c + k
                        for half in range(2):
                            _, last = parts(pb[4 + half][:, :], (actT_h[:, b, :], actT_l[:, b, :]),
                                            wparts(n, k, D, slice(half * 512, half * 512 + 512)), b == 0, b == EXP_BLOCKS - 1)
                    pend[0] = 1
                last.then_inc(sem(tag + "down"), 1)
            pend[0] = 0
            pe.wait_ge(sem(tag + "yexp"), EXPERTS + 1)
            for tt in range(TT):
                for half in range(2):
                    if tt == 1:
                        pe.wait_ge(sem(tag + "added"), EXPERTS * 4 + half + 1)
                    mm(pb[4 + half][:, :], pickT[:, tsl(tt)], yexp[:, half * 512:half * 512 + 512], start=True, stop=True)\
                        .then_inc(sem(tag + "scattered"), 1)

        route()
        experts("main_", FIRST_EXPERT)
        pe.wait_ge(sem("over_known"), 1)
        more = pe.value_load(over_i[0:1, 0:1], min_val=0, max_val=1)
        with pe.If(more > 0):
            pend[0] = 1
            experts("over_", PIECES)

    @block.scalar
    def _(act_e):
        a = nc.scalar.activation
        done = [0]

        def link(ins):
            done[0] += 1
            ins.then_inc(sem("act_chain"), 1)
            act_e.wait_ge(sem("act_chain"), done[0])

        def norm_stats(l, j):
            if j:
                act_e.wait_ge(sem("x_done"), j)
            for tt in range(TT):
                ins = a(hT_flat[tt], x[:, tt, :], ACT.Square, accum_out=stat[:, tt:tt + 1])
            link(ins)
            a(stat[:, 2:4], stat[:, 0:2], ACT.Sqrt, bias=c_("eps"), scale=1.0 / D).then_inc(sem("norm_std"), 1)

        def evac_hT(l, step, gains):
            for b in range(2):
                full(act_e, l, f"{step}{b}")
                for kk in range(2):
                    k = 2 * b + kk
                    ins = a(hT[:, k, :], pb[b][:, kk * T:kk * T + T], ACT.Copy, scale=gains[:, k:k + 1] if gains is not None else 1.0)
                ins.then_inc(freed(f"{step}{b}"), 1)

        def softmax_exp(l, eps, max_sem, nmax, sums):
            for i, ep in enumerate(eps):
                tt = i // 2
                act_e.wait_ge(sem(max_sem), 4 * l + i + 1)
                for j in range(2):
                    h = 2 * (i % 2) + j if ep[0] == "d" else i % 2 + 2 * j
                    ns = P * (tt + 1)
                    col = 4 * tt + h
                    ins = a(probs[:, tt, h, 0:ns], bank2(ep)[:, j, 0:ns], ACT.Exp, bias=stat[:, nmax + col:nmax + col + 1],
                            accum_out=stat[:, sums + col:sums + col + 1])
                ins.then_inc(freed(ep), 1)

        def evac_probsT(l, eps):
            for i, ep in enumerate(eps):
                full(act_e, l, ep)
                a(probsT[:, 4 * i:4 * i + 4, :].rearrange("p a b -> p (a b)"), bank(ep)[:, :], ACT.Copy).then_inc(freed(ep), 1)

        def step_act(l, s):
            if s == "norm_mix":
                norm_stats(l, 2 * l)
                evac_hT(l, s, s_(l, "g_mix"))
            elif s == "norm_ffn":
                norm_stats(l, 2 * l + 1)
                if l == 0:
                    for b in range(4):
                        full(act_e, l, f"{s}{b}")
                        for kk in range(2):
                            k = 2 * b + kk
                            a(hT_h[:, k, :], pb[b][:, kk * T:kk * T + T], ACT.Copy, scale=s_(l, "g_ffn")[:, k:k + 1])\
                                .then_inc(sem("hT_high"), 1)
                else:
                    evac_hT(l, s, s_(l, "g_ffn"))
            elif s == "mrg_tr":
                evac_hT(l, s, None)
            elif s == "z_ml":
                full(act_e, l, s + "a")
                a(conv_in[:, :, 3:], bank2(s + "a"), ACT.Copy).then_inc(freed(s + "a"), 1)
            elif s == "z_lat":
                full(act_e, l, s + "a")
                a(z_lat[:, 0, :], bank(s + "a")[:, :], ACT.Copy).then_inc(freed(s + "a"), 1)
            elif s == "z_mvo":
                full(act_e, l, s + "a")
                a(z_mvo[:, 0, :], bank(s + "a")[:, :], ACT.Copy).then_inc(freed(s + "a"), 1)
            elif s == "z_fox":
                full(act_e, l, s + "a")
                a(foxq, bank2(s + "a"), ACT.Copy, scale=64 ** -0.5).then_inc(freed(s + "a"), 1)
            elif s == "z_rw0":
                full(act_e, l, s + "a")
                a(Zr[:, 0:2, 1:], bank2(s + "a"), ACT.Copy).then_inc(freed(s + "a"), 1)
            elif s == "z_rw1":
                full(act_e, l, s + "a")
                a(Zr[:, 4:6, 1:], bank2(s + "a"), ACT.Copy).then_inc(freed(s + "a"), 1)
            elif s[:4] == "gate":
                b, half = int(s[4]), int(s[5])
                if b >= 2:
                    drained(act_e, l, f"br{b - 2}1b")
                    drained(act_e, l, f"br{b - 2}1a")
                for tt, ep in ((0, s + "a"), (1, s + "b")):
                    full(act_e, l, ep)
                    a(gates[:, b % 2, tt, half * 512:half * 512 + 512], bank(ep)[:, :], ACT.Sigmoid).then_inc(freed(ep), 1)
            elif s == "ds_norm":
                act_e.wait_ge(sem("lat_ss"), l + 1)
                a(stat[:, 16:20], stat[:, 10:14], ACT.Sqrt, bias=c_("eps"), scale=1.0 / P)
                a(stat[:, 20:22], stat[:, 14:16], ACT.Sqrt, bias=c_("eps"), scale=1.0 / 32).then_inc(sem("lat_std"), 1)
            elif s == "ds_tr":
                full(act_e, l, "dT")
                a(latT, bank2("dT"), ACT.Copy).then_inc(freed("dT"), 1)
            elif s == "ds_q":
                for i in range(2):
                    full(act_e, l, f"dQ{i}")
                    a(dsq[:, 2 * i:2 * i + 2, :], bank2(f"dQ{i}"), ACT.Copy, scale=P ** -0.5).then_inc(freed(f"dQ{i}"), 1)
            elif s[:6] == "ds_dot":
                tt = int(s[6])
                if tt == 1:
                    act_e.wait_ge(sem("scored"), 2 * l + 1)
                for b in range(4):
                    ep = f"dD{tt}_{b}"
                    full(act_e, l, ep)
                    a(relu[:, 2 * b:2 * b + 2, 0:P * (tt + 1)], bank2(ep)[:, :, 0:P * (tt + 1)], ACT.Relu).then_inc(freed(ep), 1)
            elif s == "ds_L":
                full(act_e, l, "fT2")
                softmax_exp(l, [f"dL{i}" for i in range(4)], "ds_max", 40, 48)
            elif s == "ds_T":
                full(act_e, l, "mN")
                evac_probsT(l, ["dP0", "dP1", "dP2"])
            elif s == "ds_O":
                for i in range(2):
                    full(act_e, l, f"dO{i}")
                    a(dsO[:, 2 * i:2 * i + 2, :], bank2(f"dO{i}"), ACT.Copy).then_inc(freed(f"dO{i}"), 1)
            elif s == "ml_in":
                act_e.wait_ge(sem("conv_sum"), l + 1)
                a(conv_s, conv, ACT.Sigmoid).then_inc(sem("conv_sig"), 1)
            elif s == "ml_gate":
                drained(act_e, l, "z_mlb")
                a(g_tmp[0:64, :], g_pre[0:64, :], ACT.Tanh, scale=1.0 / 15).then_inc(sem("gates_tanh"), 1)
                act_e.wait_ge(sem("gates_abs"), l + 1)
                link(a(g_exp[0:96, :], g_tmp[0:96, :], ACT.Exp, scale=-1.0))
                a(g_tmp[0:96, :], g_exp[0:96, :], ACT.Ln, bias=const[0:96, CONST["one"][0]:CONST["one"][0] + 1]).then_inc(sem("gates_ln"), 1)
            elif s == "ml_D":
                for i in range(3):
                    tt = 0 if i == 0 else 1
                    ns = P * (tt + 1)
                    act_e.wait_ge(sem("ml_max"), 3 * l + i + 1)
                    for j in range(512 // ns):
                        h = j if i == 0 else 2 * (i - 1) + j
                        col = 80 + 4 * tt + h
                        ins = a(probs[:, tt, h, 0:ns], bank(f"mD{i}")[:, j * ns:j * ns + ns], ACT.Exp, bias=stat[:, col:col + 1])
                    ins.then_inc(freed(f"mD{i}"), 1)
                a(stat[:, 88:96], stat[:, 80:88], ACT.Exp).then_inc(sem("ml_floor"), 1)
            elif s == "ml_T":
                full(act_e, l, "fO")
                evac_probsT(l, ["mT0", "mT1", "mT2"])
                a(osig, z_mvo[:, :, 256:512], ACT.Sigmoid).then_inc(sem("ml_osig"), 1)
            elif s == "ml_N":
                act_e.wait_ge(sem("ml_ss"), l + 1)
                a(stat[:, 120:128], stat[:, 112:120], ACT.Sqrt, bias=c_("eps"), scale=1.0 / 64).then_inc(sem("ml_std"), 1)
            elif s == "fx_L":
                drained(act_e, l, "mQ3")
                softmax_exp(l, [f"fL{i}" for i in range(4)], "fx_max", 24, 32)
            elif s == "fx_T":
                evac_probsT(l, ["fT0", "fT1", "fT2"])
            elif s == "rw_mix":
                act_e.wait_ge(sem("rw_mixed"), l + 1)
                a(tanh_w[0:64, :], Zm[0:64, 6, :], ACT.Tanh)
                a(sig_g, Zm[:, 7, :], ACT.Sigmoid).then_inc(sem("rw_lora_in"), 1)
            elif s == "rw_lora":
                drained(act_e, l, "rKK")
                a(kkn_std, kkn_max, ACT.Sqrt).then_inc(sem("rw_kstd"), 1)
                full(act_e, l, "rW")
                for blk in range(2):
                    ins = a(lw[:, blk, :], bank2("rW")[:, blk, :], ACT.Sigmoid, bias=s_(l, "w0")[:, blk:blk + 1])
                ins.then_inc(freed("rW"), 1)
                full(act_e, l, "rA")
                for blk in range(2):
                    ins = a(sa[:, blk, :], bank2("rA")[:, blk, :], ACT.Sigmoid, bias=s_(l, "a0")[:, blk:blk + 1])
                ins.then_inc(freed("rA"), 1)
                full(act_e, l, "rG")
                a(gout, bank2("rG"), ACT.Copy).then_inc(freed("rG"), 1)
            elif s == "rw_fm":
                act_e.wait_ge(sem("rw_cum"), l + 1)
                a(Wf, cum, ACT.Exp)
                link(a(cml, cml, ACT.Exp))
                a(cum, cum, ACT.Exp, scale=-1.0).then_inc(sem("rw_exp"), 1)
            elif s == "rw_tr":
                for ep, dst in (("rtV", Vtm), ("rtA", Atm), ("rtB", Btm), ("rtK", Ktm)):
                    full(act_e, l, ep)
                    a(dst.rearrange("p a b -> p (a b)"), bank(ep)[:, :], ACT.Copy).then_inc(freed(ep), 1)
            elif s == "rw_x0":
                for i in range(2):
                    full(act_e, l, f"rX0_{i}")
                    a(X[:, 4 * i:4 * i + 4, :].rearrange("p a b -> p (a b)"), bank(f"rX0_{i}")[:, :], ACT.Copy).then_inc(freed(f"rX0_{i}"), 1)
            elif s[:4] == "rw_m" and s[4:].isdigit():
                j = int(s[4])
                for i in range(2):
                    full(act_e, l, f"rZ{j}_{i}")
                    a(Z[:, 4 * i:4 * i + 4, :].rearrange("p a b -> p (a b)"), bank(f"rZ{j}_{i}")[:, :], ACT.Copy).then_inc(freed(f"rZ{j}_{i}"), 1)
            elif s == "rw_app":
                full(act_e, l, "rLkV")
                a(ALV[:, :, 64:128], bank("rLkV")[:, :].rearrange("p (q v) -> p q v", q=8), ACT.Copy).then_inc(freed("rLkV"), 1)
                for i in range(2):
                    full(act_e, l, f"rXA{i}")
                    a(XALV[:, 4 * i:4 * i + 4, :].rearrange("p a b -> p (a b)"), bank(f"rXA{i}")[:, :], ACT.Copy).then_inc(freed(f"rXA{i}"), 1)
            elif s == "rw_Y":
                full(act_e, l, "rY")
                a(Ys.rearrange("p a b -> p (a b)"), bank("rY")[:, :], ACT.Copy).then_inc(freed("rY"), 1)
            elif s == "rw_gn":
                act_e.wait_ge(sem("rw_yc"), l + 1)
                a(Yq, Yc, ACT.Square).then_inc(sem("rw_ysq"), 1)
                full(act_e, l, "rVar")
                a(lw.rearrange("p a b -> p (a b)"), bank("rVar")[:, :], ACT.Sqrt, bias=c_("gn_eps")).then_inc(freed("rVar"), 1)

        def split_hi(count, n, e=None):
            turn = 0 if e is None else e * (16 * EXP_PIECES // RING)
            act_e.wait_ge(sem(f"piece{n % RING}_in"), turn + 16 * (n // RING + 1))
            act_e.wait_ge(sem("piece_used"), (0 if e is None else e * EXP_PIECES) + (n - SPLIT + 1))
            a(w_h[:, n % SPLIT, :], ring[:, n % RING, :], ACT.Copy).then_inc(sem("split_hi"), 1)

        hT_flat = [hT[:, 4 * tt:4 * tt + 4, :].rearrange("p a b -> p (a b)") for tt in range(TT)]
        kkn_std, kkn_max = cum, cml

        act_e.wait_ge(sem("const_in"), 16)
        act_e.wait_ge(sem("small_in"), 32 * LAYERS)
        act_e.wait_ge(sem("x_in"), 16)
        for l in range(LAYERS):
            for s in SCHEDULE:
                step_act(l, s)
            if l == 0:
                def dense_silu(g):
                    for b in range(4 * g, min(4 * g + 4, DENSE_BLOCKS)):
                        act_e.wait_ge(sem("dense_up"), b + 1)
                        if b >= 4:
                            act_e.wait_ge(sem("dense_act"), b - 3)
                        a(dsil[:, b % 4, :], pb[(0 if g % 2 else 4) + b % 4][:, 0:T], ACT.Silu).then_inc(sem("dense_silu"), 1)

                def dense_high(g):
                    for b in range(4 * g, min(4 * g + 4, DENSE_BLOCKS)):
                        act_e.wait_ge(sem("dense_mul"), b + 1)
                        a(denseT_h[:, b, :], dsil[:, b % 4, :], ACT.Copy).then_inc(sem("dense_high"), 1)

                for n in range(DENSE_PIECES):
                    split_hi(n, FIRST_DENSE + n)
                    g = n // 4
                    if 1 <= g <= DENSE_GROUPS and n % 4 == 0:
                        dense_silu(g - 1)
                    if 1 <= g <= DENSE_GROUPS and n % 4 == 1:
                        dense_high(g - 1)

        act_e.wait_ge(sem("top2_gap"), 1)
        a(rtmp[:, :, 34:35], rtmp[:, :, 33:34], ACT.Exp).then_inc(sem("top2_exp"), 1)

        def experts_act(tag, first):
            act_e.wait_ge(sem(tag + "ready"), 1)
            g_ffn = s_(1, "g_ffn")

            def hsel_high(count):
                for b in range(2):
                    act_e.wait_ge(sem(tag + "gathered"), count(b + 1))
                    for j in range(4):
                        k = 4 * b + j
                        a(hsel_h[:, k, :], pb[2 + b][:, j * P:j * P + P], ACT.Copy, scale=g_ffn[:, k:k + 1]).then_inc(sem(tag + "hsel_high"), 1)

            hsel_high(lambda n: n)
            with act_e.Fori(0, EXPERTS) as e:
                def hi(j):
                    split_hi(None, first + j, e)

                def silu(g):
                    act_e.wait_ge(sem(tag + "up"), e * EXP_GROUPS + (g + 1))
                    if g >= 2:
                        act_e.wait_ge(sem(tag + "act"), e * EXP_GROUPS + (g - 1))
                    a(sil[:, g % 2, :], pb[2 * (g % 2)][:, :], ACT.Silu).then_inc(sem(tag + "silu"), 1)

                def actT_high(g):
                    act_e.wait_ge(sem(tag + "turned"), e * EXP_GROUPS + (g + 1))
                    a(actT_h[:, 4 * g:4 * g + 4, :].rearrange("p a b -> p (a b)"), pb[6][:, :], ACT.Copy).then_inc(sem(tag + "actT_high"), 1)

                for g in range(EXP_GROUPS + 1):
                    hi(4 * g)
                    if g >= 1:
                        silu(g - 1)
                    if g >= 2:
                        actT_high(g - 2)
                    hi(4 * g + 1)
                    if g == 2:
                        act_e.wait_ge(sem(tag + "scattered"), e * 4 + 4)
                        act_e.wait_ge(sem(tag + "gathered"), e * 3 + 3)
                        a(pickT, pb[7][:, 0:T], ACT.Copy).then_inc(sem(tag + "pickT"), 1)
                    if g < EXP_GROUPS:
                        hi(4 * g + 2)
                        hi(4 * g + 3)
                hsel_high(lambda n: e * 3 + (3 + n))
                actT_high(EXP_GROUPS - 1)
                for j in range(4 * EXP_GROUPS + 2, EXP_PIECES):
                    hi(j)

        experts_act("main_", FIRST_EXPERT)
        act_e.wait_ge(sem("over_known"), 1)
        more = act_e.value_load(over_i[0:1, 0:1], min_val=0, max_val=1)
        with act_e.If(more > 0):
            experts_act("over_", PIECES)
        act_e.wait_ge(sem("x_done"), 2 * LAYERS)
        for tt in range(TT):
            ins = a(hT_flat[tt], x[:, tt, :], ACT.Square, accum_out=stat[:, tt:tt + 1])
        link(ins)
        a(stat[:, 2:4], stat[:, 0:2], ACT.Sqrt, bias=c_("eps"), scale=1.0 / D).then_inc(sem("norm_std"), 1)

    @block.vector
    def _(ve):
        v = nc.vector
        done = [0]

        def link(ins):
            done[0] += 1
            ins.then_inc(sem("vec_chain"), 1)
            ve.wait_ge(sem("vec_chain"), done[0])

        def tt_(o, i0, i1, op):
            return v.tensor_tensor(o, i0, i1, op)

        def ts(o, i0, s1, op0, s2=None, op1=ALU.bypass):
            return v.tensor_scalar(o, i0, s1, s2, op0, op1)

        def stt(o, i0, s, i1, op0, op1, **k):
            return v.scalar_tensor_tensor(out=o, in0=i0, scalar=s, in1=i1, op0=op0, op1=op1, **k)

        def split_lo(count, n, e=None):
            ve.wait_ge(sem("split_hi"), (0 if e is None else e * EXP_PIECES) + (count + 1))
            tt_(w_l[:, n % SPLIT, :], ring[:, n % RING, :], w_h[:, n % SPLIT, :].bitcast(F32), ALU.subtract).then_inc(sem("split_lo"), 1)

        def norm_rows(j):
            ve.wait_ge(sem("norm_std"), j + 1)
            link(v.reciprocal(stat[:, 4:6], stat[:, 2:4]))
            for tt in range(TT):
                ts(xn[:, tt, :], x[:, tt, :], stat[:, 4 + tt:5 + tt], ALU.mult).then_inc(sem("normed"), 1)

        def evac_hT(l, step, gains):
            for b in range(2, 4):
                full(ve, l, f"{step}{b}")
                for kk in range(2):
                    k = 2 * b + kk
                    if gains is None:
                        ins = v.tensor_copy(hT[:, k, :], pb[b][:, kk * T:kk * T + T])
                    else:
                        ins = ts(hT[:, k, :], pb[b][:, kk * T:kk * T + T], gains[:, k:k + 1], ALU.mult)
                ins.then_inc(freed(f"{step}{b}"), 1)

        def row_max(l, eps, max_sem, nmax):
            for i, ep in enumerate(eps):
                tt = i // 2
                full(ve, l, ep)
                first = 2 * (i % 2) if ep[0] == "d" else i % 2
                step = 1 if ep[0] == "d" else 2
                at = nmax + 4 * tt + first
                v.reduce_max(stat[:, at:at + step + 1:step], bank2(ep)[:, :, 0:P * (tt + 1)], AX.X, negate=True).then_inc(sem(max_sem), 1)

        def normalise(l, eps, sums, out_sem):
            for ep in eps:
                drained(ve, l, ep)
            link(v.reciprocal(stat[:, sums:sums + 8], stat[:, sums:sums + 8]))
            for tt in range(TT):
                ns = P * (tt + 1)
                ins = tt_(probs[:, tt, :, 0:ns], probs[:, tt, :, 0:ns],
                          stat[:, sums + 4 * tt:sums + 4 * tt + 4].unsqueeze(2).broadcast_to([P, 4, ns]), ALU.mult)
            ins.then_inc(sem(out_sem), 1)

        def step_vec(l, s):
            if s == "norm_mix":
                norm_rows(2 * l)
                evac_hT(l, s, s_(l, "g_mix"))
                v.memset(conv_in[:, :, 0:3], 0.0)
                v.memset(Zr[:, :, 0:1], 0.0)
            elif s == "norm_ffn":
                norm_rows(2 * l + 1)
                if l == 0:
                    for b in range(4):
                        for kk in range(2):
                            k = 2 * b + kk
                            if kk == 0:
                                ve.wait_ge(sem("hT_high"), k + 2)
                            ins = stt(hT_l[:, k, :], pb[b][:, kk * T:kk * T + T], s_(l, "g_ffn")[:, k:k + 1],
                                      hT_h[:, k, :].bitcast(F32), ALU.mult, ALU.subtract)
                        ins.then_inc(freed(f"{s}{b}"), 1)
                else:
                    evac_hT(l, s, s_(l, "g_ffn"))
            elif s == "mrg_tr":
                evac_hT(l, s, None)
            elif s == "z_ml":
                full(ve, l, s + "b")
                link(v.tensor_copy(z_idx, bank(s + "b")[:, T:T + 80].rearrange("p (a b) -> p a b", a=TT)))
                ts(g_pre[0:96, :], bank(s + "b")[0:96, 0:T], s_(l, "gate_b")[0:96, :], ALU.add).then_inc(freed(s + "b"), 1)
            elif s == "z_lat":
                full(ve, l, s + "b")
                v.tensor_copy(z_lat[:, 1, :], bank(s + "b")[:, :]).then_inc(freed(s + "b"), 1)
            elif s == "z_mvo":
                full(ve, l, s + "b")
                v.tensor_copy(z_mvo[:, 1, :], bank(s + "b")[:, :]).then_inc(freed(s + "b"), 1)
            elif s == "z_fox":
                full(ve, l, s + "b")
                v.tensor_copy(foxk, bank2(s + "b")).then_inc(freed(s + "b"), 1)
            elif s == "z_rw0":
                full(ve, l, s + "b")
                v.tensor_copy(Zr[:, 2:4, 1:], bank2(s + "b")).then_inc(freed(s + "b"), 1)
            elif s == "z_rw1":
                full(ve, l, s + "b")
                v.tensor_copy(Zr[:, 6:8, 1:], bank2(s + "b")).then_inc(freed(s + "b"), 1)
            elif s == "ml_in":
                drained(ve, l, "z_mla")
                cw = s_(l, "conv_w")
                for j in range(4):
                    for blk in range(2):
                        w = cw[:, 2 * j + blk:2 * j + blk + 1]
                        if j == 0:
                            ins = ts(conv[:, blk, :], conv_in[:, blk, 0:T], w, ALU.mult, s_(l, "conv_b")[:, blk:blk + 1], ALU.add)
                        else:
                            ins = stt(conv[:, blk, :], conv_in[:, blk, j:j + T], w, conv[:, blk, :], ALU.mult, ALU.add)
                    if j < 3:
                        link(ins)
                ins.then_inc(sem("conv_sum"), 1)
                ve.wait_ge(sem("conv_sig"), l + 1)
                stt(conv[:, 0, :], conv[:, 0, :], 32 ** -0.5, conv_s[:, 0, :], ALU.mult, ALU.mult)
                tt_(conv[:, 1, :], conv[:, 1, :], conv_s[:, 1, :], ALU.mult).then_inc(sem("conv_done"), 1)
            elif s == "ds_norm":
                drained(ve, l, "z_lata")
                drained(ve, l, "z_latb")
                lat = z_lat[:, :, 0:256].rearrange("p t (w c) -> p t w c", w=2)
                tt_(lat_sq, lat, lat, ALU.mult)
                link(tt_(ki_sq, z_idx[:, :, 0:32], z_idx[:, :, 0:32], ALU.mult))
                v.reduce_sum(stat[:, 10:14].rearrange("p (a b) -> p a b", a=2), lat_sq, AX.X)
                v.reduce_sum(stat[:, 14:16], ki_sq, AX.X).then_inc(sem("lat_ss"), 1)
                ve.wait_ge(sem("lat_std"), l + 1)
                link(v.reciprocal(stat[:, 16:22], stat[:, 16:22]))
                for tt in range(TT):
                    for w, g in ((0, "g_cq"), (1, "g_ckv")):
                        stt(lat_n[:, tt, w, :], z_lat[:, tt, w * P:w * P + P], stat[:, 16 + 2 * tt + w:17 + 2 * tt + w],
                            r_(l, g), ALU.mult, ALU.mult)
                    ins = stt(ki4[:, tt, :, :], z_idx[:, tt, 0:32].unsqueeze(1).broadcast_to([P, 4, 32]), stat[:, 20 + tt:21 + tt],
                              r_(l, "g_kidx").unsqueeze(1).broadcast_to([P, 4, 32]), ALU.mult, ALU.mult)
                ins.then_inc(sem("lat_normed"), 1)
                link(ts(z_idx[:, :, 32:40], z_idx[:, :, 32:40], 8 ** -0.5 * 32 ** -0.5, ALU.mult))
            elif s == "ds_tr":
                full(ve, l, "dTk")
                v.tensor_copy(kiT, bank("dTk")[:, 0:T]).then_inc(freed("dTk"), 1)
            elif s == "ds_q":
                full(ve, l, "dQi")
                v.tensor_copy(qiT, bank2("dQi")).then_inc(freed("dQi"), 1)
            elif s == "ml_gate":
                drained(ve, l, "z_mlb")
                ve.wait_ge(sem("gates_tanh"), l + 1)
                link(ts(g_pre[0:64, :], g_tmp[0:64, :], 15.0, ALU.mult))
                stt(g_tmp[0:96, :], g_pre[0:96, :], -1.0, g_pre[0:96, :], ALU.mult, ALU.max).then_inc(sem("gates_abs"), 1)
                ve.wait_ge(sem("gates_ln"), l + 1)
                link(stt(g_exp[0:96, :], g_pre[0:96, :], 0.0, g_tmp[0:96, :], ALU.min, ALU.subtract))
                link(v.tensor_tensor_scan(g_cum[0:96, :], c_("ones")[0:96, :], g_exp[0:96, :], 0.0, ALU.mult, ALU.add))
                is_f = const[0:96, CONST["is_f"][0]:CONST["is_f"][0] + 1]
                is_i = const[0:96, CONST["is_i"][0]:CONST["is_i"][0] + 1]
                ts(g_pos[0:96, :], g_cum[0:96, :], is_f, ALU.mult)
                link(ts(g_tmp[0:96, :], g_pre[0:96, :], is_i, ALU.mult))
                stt(g_key[0:96, :], g_pos[0:96, :], -1.0, g_tmp[0:96, :], ALU.mult, ALU.add).then_inc(sem("gate_sums"), 1)
            elif s[:6] == "ds_dot":
                tt = int(s[6])
                ns = P * (tt + 1)
                for h in range(8):
                    b, j = h % 4, h // 4
                    if h < 4:
                        drained(ve, l, f"dD{tt}_{b}")
                    r = relu[:, 2 * b + j, 0:ns]
                    w = z_idx[:, tt, 32 + h:33 + h]
                    if h == 0:
                        link(ts(score[:, tt, 0:ns], r, w, ALU.mult))
                    else:
                        ins = stt(score[:, tt, 0:ns], r, w, score[:, tt, 0:ns], ALU.mult, ALU.add)
                        if h == 7:
                            ins.then_inc(sem("scored"), 1)
                        else:
                            link(ins)
                ve.wait_ge(sem("scored"), 2 * l + tt + 1)
                link(tt_(score[:, tt, tsl(tt)], score[:, tt, tsl(tt)], c_("negtri"), ALU.add))
            elif s == "ds_topk":
                for r in range(TOPK // 8):
                    for tt in range(TT):
                        ins = v.max(best[:, tt, :], score[:, tt, 0:P * (tt + 1)])
                    link(ins)
                    for tt in range(TT):
                        ins = v.match_replace(score[:, tt, 0:P * (tt + 1)], best[:, tt, :], score[:, tt, 0:P * (tt + 1)], TAKEN)
                    link(ins)
                for tt in range(TT):
                    ns = P * (tt + 1)
                    ins = ts(score[:, tt, 0:ns], score[:, tt, 0:ns], TAKEN, ALU.not_equal, NEG, ALU.mult)
                link(ins)
                for tt in range(TT):
                    ins = tt_(score[:, tt, tsl(tt)], score[:, tt, tsl(tt)], c_("negtri"), ALU.add)
                ins.then_inc(sem("topk_mask"), 1)
            elif s == "ds_L":
                row_max(l, [f"dL{i}" for i in range(4)], "ds_max", 40)
                normalise(l, [f"dL{i}" for i in range(4)], 48, "ds_probs")
            elif s == "ds_Y":
                full(ve, l, "dY")
                v.tensor_copy(yT[:, 0, :, :], bank2("dY")).then_inc(freed("dY"), 1)
            elif s == "fx_L":
                row_max(l, [f"fL{i}" for i in range(4)], "fx_max", 24)
                normalise(l, [f"fL{i}" for i in range(4)], 32, "fx_probs")
            elif s == "fx_O":
                full(ve, l, "fO")
                v.tensor_copy(yT[:, 3, :, :], bank2("fO")).then_inc(freed("fO"), 1)
            elif s == "ml_D":
                for i in range(3):
                    tt = 0 if i == 0 else 1
                    ns = P * (tt + 1)
                    full(ve, l, f"mD{i}")
                    at = 80 + 4 * tt + (0 if i == 0 else 2 * (i - 1))
                    v.reduce_max(stat[:, at:at + 512 // ns], bank2(f"mD{i}", ns), AX.X, negate=True).then_inc(sem("ml_max"), 1)
            elif s == "ml_qk":
                for i in range(3):
                    drained(ve, l, f"mD{i}")
                for h in range(4):
                    full(ve, l, f"mQ{h}")
                    for tt in range(TT):
                        ns = P * (tt + 1)
                        ins = stt(mlP[:, tt, h, 0:ns], bank(f"mQ{h}")[:, tt * P:tt * P + ns], 1.0, probs[:, tt, h, 0:ns],
                                  ALU.mult, ALU.mult, accum_out=stat[:, 100 + 4 * tt + h:101 + 4 * tt + h])
                    ins.then_inc(freed(f"mQ{h}"), 1)
                ve.wait_ge(sem("ml_floor"), l + 1)
                drained(ve, l, "mQ3")
                link(stt(stat[:, 100:108], stat[:, 100:108], -1.0, stat[:, 100:108], ALU.mult, ALU.max))
                link(tt_(stat[:, 100:108], stat[:, 100:108], stat[:, 88:96], ALU.max))
                link(v.reciprocal(stat[:, 100:108], stat[:, 100:108]))
            elif s == "ml_N":
                full(ve, l, "mN")
                tt_(cell.rearrange("p t (h d) -> p (t h) d", h=4), bank2("mN", 64),
                    stat[:, 100:108].unsqueeze(2).broadcast_to([P, 8, 64]), ALU.mult).then_inc(freed("mN"), 1)
                drained(ve, l, "mN")
                link(tt_(cell_sq, cell, cell, ALU.mult))
                v.reduce_sum(stat[:, 112:120], cell_sq.rearrange("p t (h d) -> p (t h) d", h=4), AX.X).then_inc(sem("ml_ss"), 1)
                ve.wait_ge(sem("ml_std"), l + 1)
                link(v.reciprocal(stat[:, 120:128], stat[:, 120:128]))
                c3 = cell.rearrange("p t (h d) -> p (t h) d", h=4)
                link(tt_(c3, c3, stat[:, 120:128].unsqueeze(2).broadcast_to([P, 8, 64]), ALU.mult))
                link(tt_(cell, cell, r_(l, "ml_g").unsqueeze(1).broadcast_to([P, TT, 256]), ALU.mult))
                ve.wait_ge(sem("ml_osig"), l + 1)
                tt_(cell, cell, osig, ALU.mult).then_inc(sem("ml_cell"), 1)
            elif s == "ml_Y":
                full(ve, l, "mY")
                v.tensor_copy(yT[:, 2, :, :], bank2("mY")).then_inc(freed("mY"), 1)
            elif s == "rw_mix":
                drained(ve, l, "z_rw0a")
                drained(ve, l, "z_rw1a")
                drained(ve, l, "z_rw1b")
                full(ve, l, "dY")
                full(ve, l, "mY")
                drained(ve, l, "dO1")
                link(tt_(Zm, Zr[:, :, 0:T], Zr[:, :, 1:], ALU.subtract))
                for b in range(8):
                    ins = stt(Zm[:, b, :], Zm[:, b, :], s_(l, "mu")[:, b:b + 1], Zr[:, b, 1:], ALU.mult, ALU.add)
                ins.then_inc(sem("rw_mixed"), 1)
                ve.wait_ge(sem("rw_mixed"), l + 1)
                for blk in range(2):
                    ins = ts(kkn[:, blk, :], Zm[:, 2 + blk, :], s_(l, "k_k")[:, blk:blk + 1], ALU.mult)
                link(ins)
                tt_(t0, kkn, kkn, ALU.mult).then_inc(sem("rw_kksq"), 1)
            elif s == "rw_lora":
                full(ve, l, "rKK")
                ts(cml.rearrange("p a b -> p (a b)"), bank("rKK")[:, :], 1e-24, ALU.max).then_inc(freed("rKK"), 1)
                ve.wait_ge(sem("rw_kstd"), l + 1)
                link(v.reciprocal(cml, cum))
                link(tt_(kkn, kkn, cml, ALU.mult))
            elif s == "rw_fm":
                drained(ve, l, "rW")
                link(ts(lw, lw, -DECAY, ALU.mult))
                for blk in range(2):
                    ins = v.tensor_tensor_scan(cum[:, blk, :], c_("reset"), lw[:, blk, :], 0.0, ALU.mult, ALU.add)
                link(ins)
                tt_(cml, cum, lw, ALU.subtract).then_inc(sem("rw_cum"), 1)
                drained(ve, l, "rA")
                for blk in range(2):
                    ins = ts(k2[:, blk, :], sa[:, blk, :], 1.0, ALU.subtract, s_(l, "k_a")[:, blk:blk + 1], ALU.mult)
                link(ins)
                stt(k2, k2, 1.0, Zm[:, 2:4, :], ALU.add, ALU.mult)
                for blk in range(2):
                    ins = ts(t0[:, blk, :], Zm[:, blk, :], s_(l, "r_k")[:, blk:blk + 1], ALU.mult)
                link(ins)
                tt_(t0, t0, k2, ALU.mult)
                link(tt_(sa, kkn, sa, ALU.mult))
                ve.wait_ge(sem("rw_exp"), l + 1)
                stt(AR[:, :, 0, :], kkn, -1.0, cml, ALU.mult, ALU.mult)
                tt_(AR[:, :, 1, :], Zm[:, 0:2, :], Wf, ALU.mult)
                tt_(sa, sa, cum, ALU.mult)
                tt_(k2, k2, cum, ALU.mult).then_inc(sem("rw_fm_done"), 1)
            elif s == "rw_tr":
                full(ve, l, "rBon")
                tt_(bon, bank2("rBon"), Zm[:, 4:6, :], ALU.mult).then_inc(freed("rBon"), 1)
            elif s == "rw_prod":
                for pre, dst in (("rLT", LQ), ("rKT", KQ)):
                    for h in range(4):
                        full(ve, l, f"{pre}{h}")
                        ins = tt_(dst[:, h, :, :], bank2(f"{pre}{h}"), c_("masks").unsqueeze(1).broadcast_to([P, TT, 256]), ALU.mult)
                        ins.then_inc(freed(f"{pre}{h}"), 1)
                drained(ve, l, "rLT3")
                lt = LQ.rearrange("p h t n -> p (h t) n")[:, :, 0:P]
                lvl = c_("level").rearrange("p (a b) -> p a b", a=6)
                link(tt_(XT, lt, lvl[:, 0:1, :].broadcast_to([P, 8, P]), ALU.mult))
                tt_(XT, XT, c_("ident").unsqueeze(1).broadcast_to([P, 8, P]), ALU.add).then_inc(sem("rw_xt0"), 1)
            elif s == "rw_app":
                drained(ve, l, "rtA")
                v.tensor_copy(ALV[:, :, 0:64].rearrange("p (h t) d -> p h t d", t=TT),
                              Atm.rearrange("p t (h d) -> p h t d", h=4))
                drained(ve, l, "rLkV")
                v.tensor_copy(stat[:, 131:132], c_("one")).then_inc(sem("rw_alv"), 1)
            elif s[:4] == "rw_m" and s[4:].isdigit():
                j = int(s[4])
                for i in range(2):
                    for ep, dst in ((f"rX{j}_{i}", X), (f"rT{j}_{i}", XT)):
                        full(ve, l, ep)
                        d3 = dst[:, 4 * i:4 * i + 4, :]
                        tt_(d3, d3, bank2(ep, P), ALU.add).then_inc(freed(ep), 1)
            elif s == "rw_state":
                full(ve, l, "rRp")
                tt_(RpT, bank2("rRp"), AR[:, :, 1, :], ALU.add).then_inc(freed("rRp"), 1)
                for c in range(2):
                    full(ve, l, f"rP{c}")
                    tt_(PT[:, c, :, :, :].rearrange("p a b c -> p (a b) c"), bank(f"rP{c}")[:, 0:256].rearrange("p (a b) -> p a b", b=64),
                        c_("ident64").unsqueeze(1).broadcast_to([P, 4, 64]), ALU.add).then_inc(freed(f"rP{c}"), 1)
                last = Wf.rearrange("p a (n c) -> p a n c", c=64)[:, :, :, 63]
                for c in range(2):
                    full(ve, l, f"rG{c}")
                    for tt in range(TT):
                        ins = tt_(GW[:, c, :, tt, :], bank(f"rG{c}")[:, 0:256].rearrange("p (a t b) -> p a t b", t=TT, b=64)[:, :, tt, :],
                                  last[:, :, 2 * tt + c].unsqueeze(2).broadcast_to([P, 2, 64]), ALU.mult)
                    ins.then_inc(freed(f"rG{c}"), 1)
                drained(ve, l, "rG1")
                for ep, dst, c, tt in (("rS2", S2, 1, 0), ("rS3", S3, 0, 1)):
                    full(ve, l, ep)
                    for blk in range(2):
                        n = 2 * tt + c
                        ins = stt(dst[:, blk, :], bank(ep)[:, blk * 64:blk * 64 + 64], Wf[:, blk, 64 * n + 63:64 * n + 64],
                                  GW[:, c, blk, tt, :], ALU.mult, ALU.add)
                    ins.then_inc(freed(ep), 1)
            elif s == "rw_gn":
                full(ve, l, "rMean")
                drained(ve, l, "rY")
                tt_(Yc, Ys, bank2("rMean"), ALU.subtract).then_inc(freed("rMean"), 1)
                drained(ve, l, "rMean")
                v.tensor_copy(stat[:, 132:133], c_("one")).then_inc(sem("rw_yc"), 1)
                drained(ve, l, "rVar")
                link(v.reciprocal(lw, lw))
                link(tt_(Yc, Yc, lw, ALU.mult))
                for blk in range(2):
                    ins = ts(Yc[:, blk, :], Yc[:, blk, :], s_(l, "ln_g")[:, blk:blk + 1], ALU.mult, s_(l, "ln_b")[:, blk:blk + 1], ALU.add)
                link(ins)
                link(tt_(Yc, Yc, bon, ALU.add))
                tt_(yT[:, 1, :, :], Yc, gout, ALU.mult).then_inc(sem("rwkv_out"), 1)
            elif s[:2] == "br":
                bi = int(s[2])
                for half in range(2):
                    for tt, ep in ((0, f"br{bi}{half}a"), (1, f"br{bi}{half}b")):
                        cols = slice(half * 512, half * 512 + 512)
                        full(ve, l, ep)
                        if half == 0:
                            drained(ve, l, f"gate{bi}0b")
                            drained(ve, l, f"gate{bi}1b")
                        g = gates[:, bi % 2, tt, cols]
                        if bi == 0:
                            tt_(xn[:, tt, cols], bank(ep)[:, :], g, ALU.mult).then_inc(freed(ep), 1)
                        else:
                            tt_(mtmp, bank(ep)[:, :], g, ALU.mult).then_inc(freed(ep), 1)
                            drained(ve, l, ep)
                            ins = tt_(xn[:, tt, cols], xn[:, tt, cols], mtmp, ALU.add)
                            if half == 1 and tt == 1 and bi == 3:
                                ins.then_inc(sem("merged"), 1)
                            else:
                                link(ins)
            elif s[:3] == "out":
                half = int(s[3])
                for tt, ep in ((0, s + "a"), (1, s + "b")):
                    cols = slice(half * 512, half * 512 + 512)
                    full(ve, l, ep)
                    tt_(x[:, tt, cols], x[:, tt, cols], bank(ep)[:, :], ALU.add).then_inc(freed(ep), 1)
                if half == 1:
                    drained(ve, l, "out1b")
                    v.tensor_copy(stat[:, 133:134], c_("one")).then_inc(sem("x_done"), 1)

        ve.wait_ge(sem("const_in"), 16)
        ve.wait_ge(sem("small_in"), 32 * LAYERS)
        ve.wait_ge(sem("x_in"), 16)
        for l in range(LAYERS):
            for s in SCHEDULE:
                step_vec(l, s)
            if l == 0:
                def dense_mul(g):
                    for b in range(4 * g, min(4 * g + 4, DENSE_BLOCKS)):
                        ve.wait_ge(sem("dense_silu"), b + 1)
                        tt_(dsil[:, b % 4, :], dsil[:, b % 4, :], pb[(0 if g % 2 else 4) + b % 4][:, T:2 * T], ALU.mult)\
                            .then_inc(sem("dense_mul"), 1)

                def dense_low(g):
                    for b in range(4 * g, min(4 * g + 4, DENSE_BLOCKS)):
                        ve.wait_ge(sem("dense_high"), b + 1)
                        tt_(denseT_l[:, b, :], dsil[:, b % 4, :], denseT_h[:, b, :].bitcast(F32), ALU.subtract).then_inc(sem("dense_act"), 1)

                for n in range(DENSE_PIECES):
                    split_lo(n, FIRST_DENSE + n)
                    g = n // 4
                    if 1 <= g <= DENSE_GROUPS and n % 4 == 0:
                        dense_mul(g - 1)
                    if 1 <= g <= DENSE_GROUPS and n % 4 == 1:
                        dense_low(g - 1)
                ve.wait_ge(sem("dense_down"), 1)
                for tt in range(TT):
                    for half in range(2):
                        cols = slice(half * 512, half * 512 + 512)
                        ins = tt_(x[:, tt, cols], x[:, tt, cols], pb[4 + 2 * tt + half][:, :], ALU.add)
                ins.then_inc(sem("x_done"), 1)

        E1 = EXPERTS + 1
        v.memset(took[:, :, :], 0.0)
        v.memset(weight[:, :, :], 0.0)
        v.memset(rtmp[:, :, 8:24], ABSENT)
        link(v.memset(rank[:, :, :], 0.0))
        ve.wait_ge(sem("router_logits"), 1)
        link(v.tensor_copy(rtmp[:, :, 0:8], pb[4][:, 0:16].rearrange("p (t e) -> p t e", t=TT)))
        for tt in range(TT):
            ins = v.max(rtmp[:, tt, 24:32], rtmp[:, tt, 0:8])
        link(ins)
        v.tensor_copy(rtmp[:, :, 8:9], rtmp[:, :, 24:25])
        v.tensor_copy(rtmp[:, :, 16:17], rtmp[:, :, 25:26])
        link(tt_(rtmp[:, :, 33:34], rtmp[:, :, 25:26], rtmp[:, :, 24:25], ALU.subtract))
        for r in range(2):
            for tt in range(TT):
                ins = v.match_replace(rtmp[:, tt, 40 + 8 * r:48 + 8 * r], rtmp[:, tt, 8 + 8 * r:16 + 8 * r],
                                      rtmp[:, tt, 40:48] if r else rtmp[:, tt, 0:8], TAKEN)
            link(ins)
        v.tensor_copy(stat[:, 134:135], c_("one")).then_inc(sem("top2_gap"), 1)
        for tt in range(TT):
            ts(took[:, tt, 0:8], rtmp[:, tt, 48:56], TAKEN, ALU.is_equal)
            ins = ts(rtmp[:, tt, 56:64], rtmp[:, tt, 40:48], TAKEN, ALU.is_equal)
        ins.then_inc(sem("took_done"), 1)
        ve.wait_ge(sem("took_done"), 1)
        ve.wait_ge(sem("top2_exp"), 1)
        link(ts(rtmp[:, :, 35:36], rtmp[:, :, 34:35], 1.0, ALU.add))
        link(v.reciprocal(rtmp[:, :, 36:37], rtmp[:, :, 35:36]))
        link(tt_(rtmp[:, :, 37:38], rtmp[:, :, 34:35], rtmp[:, :, 36:37], ALU.mult))
        for tt in range(TT):
            ins = tt_(rtmp[:, tt, 0:8], took[:, tt, 0:8], rtmp[:, tt, 56:64], ALU.subtract)
        link(ins)
        for tt in range(TT):
            ins = ts(weight[:, tt, 0:8], rtmp[:, tt, 0:8], rtmp[:, tt, 37:38], ALU.mult)
        link(ins)
        for tt in range(TT):
            ins = stt(weight[:, tt, 0:8], rtmp[:, tt, 56:64], rtmp[:, tt, 36:37], weight[:, tt, 0:8], ALU.mult, ALU.add)
        link(ins)
        ve.wait_ge(sem("ranks"), 1)
        link(v.tensor_copy(rank[:, :, :], pb[5][:, 0:2 * E1].rearrange("p (t e) -> p t e", t=TT)))
        link(v.tensor_reduce(over[:, 0:1], pb[5][:, 2 * E1:3 * E1], AX.X, ALU.max))
        link(ts(over[:, 1:2], over[:, 0:1], float(P), ALU.is_gt))
        v.tensor_copy(over_i[:, 0:1], over[:, 1:2]).then_inc(sem("over_known"), 1)
        ve.wait_ge(sem("over_known"), 1)

        def experts_vec(tag, first_slot, first):
            iota = c_("iota")[:, first_slot:first_slot + P]

            def choose(e):
                for tt in range(TT):
                    ts(pick[:, tt, :], iota, rank[:, tt, bass.ds(e, 1)], ALU.is_equal, took[:, tt, bass.ds(e, 1)], ALU.mult)
                    ins = ts(pickg[:, tt, :], iota, rank[:, tt, bass.ds(e, 1)], ALU.is_equal, weight[:, tt, bass.ds(e, 1)], ALU.mult)
                ins.then_inc(sem(tag + "pick"), 1)

            if tag == "main_":
                v.memset(pickT[:, :], 0.0)
            v.memset(yexp[:, :], 0.0).then_inc(sem(tag + "ready"), 1)
            choose(0)
            g_ffn = s_(1, "g_ffn")

            def hsel_low(count):
                for k in range(KC):
                    if k % 4 == 0:
                        ve.wait_ge(sem(tag + "hsel_high"), count(k + 4))
                    ins = stt(hsel_l[:, k, :], pb[2 + k // 4][:, (k % 4) * P:(k % 4) * P + P], g_ffn[:, k:k + 1],
                              hsel_h[:, k, :].bitcast(F32), ALU.mult, ALU.subtract)
                ins.then_inc(sem(tag + "hsel"), 1)

            hsel_low(lambda k: k)
            with ve.Fori(0, EXPERTS) as e:
                def lo(j):
                    split_lo(DENSE_PIECES + first + j - FIRST_EXPERT, first + j, e)

                def yexp_in():
                    ve.wait_ge(sem(tag + "down"), e + 1)
                    v.tensor_copy(yexp[:, 0:512], pb[4][:, :])
                    v.tensor_copy(yexp[:, 512:1024], pb[5][:, :]).then_inc(sem(tag + "yexp"), 1)

                def add(tt):
                    for half in range(2):
                        cols = slice(half * 512, half * 512 + 512)
                        ve.wait_ge(sem(tag + "scattered"), e * 4 + (2 * tt + half + 1))
                        tt_(x[:, tt, cols], x[:, tt, cols], pb[4 + half][:, :], ALU.add).then_inc(sem(tag + "added"), 1)

                def gate_up(g):
                    ve.wait_ge(sem(tag + "silu"), e * EXP_GROUPS + (g + 1))
                    tt_(act[:, g % 2, :], sil[:, g % 2, :], pb[2 * (g % 2) + 1][:, :], ALU.mult).then_inc(sem(tag + "act"), 1)

                def actT_low(g):
                    ve.wait_ge(sem(tag + "actT_high"), e * EXP_GROUPS + (g + 1))
                    tt_(actT_l[:, 4 * g:4 * g + 4, :].rearrange("p a b -> p (a b)"), pb[6][:, :],
                        actT_h[:, 4 * g:4 * g + 4, :].rearrange("p a b -> p (a b)").bitcast(F32), ALU.subtract).then_inc(sem(tag + "actT"), 1)

                for g in range(EXP_GROUPS + 1):
                    lo(4 * g)
                    if g >= 1:
                        gate_up(g - 1)
                    if g >= 2:
                        actT_low(g - 2)
                    if g == 1:
                        add(0)
                    lo(4 * g + 1)
                    if g == 0:
                        yexp_in()
                    if g == 4:
                        choose(ve.snap(e + 1))
                    if g < EXP_GROUPS:
                        lo(4 * g + 2)
                        if g == 2:
                            add(1)
                        lo(4 * g + 3)
                hsel_low(lambda k: e * KC + (KC + k))
                actT_low(EXP_GROUPS - 1)
                for j in range(4 * EXP_GROUPS + 2, EXP_PIECES):
                    lo(j)
            ve.wait_ge(sem(tag + "down"), EXPERTS + 1)
            v.tensor_copy(yexp[:, 0:512], pb[4][:, :])
            v.tensor_copy(yexp[:, 512:1024], pb[5][:, :]).then_inc(sem(tag + "yexp"), 1)
            for tt in range(TT):
                for half in range(2):
                    cols = slice(half * 512, half * 512 + 512)
                    ve.wait_ge(sem(tag + "scattered"), EXPERTS * 4 + 2 * tt + half + 1)
                    tt_(x[:, tt, cols], x[:, tt, cols], pb[4 + half][:, :], ALU.add).then_inc(sem(tag + "added"), 1)

        experts_vec("main_", 0, FIRST_EXPERT)
        more = ve.value_load(over_i[0:1, 0:1], min_val=0, max_val=1)
        with ve.If(more > 0):
            ve.wait_ge(sem("main_added"), 4 * EXPERTS + 4)
            experts_vec("over_", P, PIECES)
        ve.wait_ge(sem("main_added"), 4 * EXPERTS + 4)
        v.tensor_copy(stat[:, 137:138], c_("one")).then_inc(sem("x_done"), 1)
        ve.wait_ge(sem("norm_std"), 2 * LAYERS + 1)
        link(v.reciprocal(stat[:, 4:6], stat[:, 2:4]))
        ve.wait_ge(sem("final_in"), 16)
        for tt in range(TT):
            ins = stt(xn[:, tt, :], x[:, tt, :], stat[:, 4 + tt:5 + tt], final_g, ALU.mult, ALU.mult)
        ins.then_inc(sem("out_ready"), 1)

    @block.gpsimd
    def _(gp):
        gp.dma_start(const[:, :], const_in).then_inc(sem("const_in"), 16)
        gp.dma_start(x[:, :, :], x_in.rearrange("b (t p) d -> p (b t) d", p=P)).then_inc(sem("x_in"), 16)
        for l in range(LAYERS):
            gp.dma_start(small[l][:, :], small_in[l]).then_inc(sem("small_in"), 16)
            gp.dma_start(row[l][:, :], row_in[l:l + 1, :].broadcast_to([P, N_ROW])).then_inc(sem("small_in"), 16)
        gp.wait_ge(sem("const_in"), 16)
        lt = LQ.rearrange("p h t n -> p (h t) n")[:, :, 0:P]
        lvl = c_("level").rearrange("p (a b) -> p a b", a=6)
        for l in range(LAYERS):
            drained(gp, l, "rLT3")
            for j in range(1, 6):
                if j >= 3:
                    full(gp, l, f"rZ{j - 2}_1")
                nc.gpsimd.tensor_tensor(lev[:, j % 2, :, :], lt, lvl[:, j:j + 1, :].broadcast_to([P, 8, P]), ALU.mult)\
                  .then_inc(sem("rw_level"), 1)
        gp.wait_ge(sem("x_done"), 2 * LAYERS - 1)
        gp.dma_start(final_g, final_in.broadcast_to([P, D])).then_inc(sem("final_in"), 16)

    ctx_block.__exit__(None, None, None)


def lay_out(inputs):
    f = {k: np.ascontiguousarray(a) for k, a in inputs.items()}
    pieces = np.zeros((PIECES, P, PIECE), np.float32)

    def columns(n, w):
        v = w.reshape(2, 4, P, w.shape[1]).transpose(0, 2, 1, 3)
        pieces[n:n + 2].reshape(2, P, 4, 512)[:, :, :, :w.shape[1]] = v
        return n + 2

    def rows(n, w):
        m = w.shape[0] // 256
        pieces[n:n + m].reshape(m, P, 2, D)[...] = w.reshape(m, 2, P, D).transpose(0, 2, 1, 3)
        return n + m

    n = 0
    for l in range(LAYERS):
        for s in SCHEDULE:
            if s in GROUPS:
                w = np.zeros((D, 512), np.float32)
                for src, width, dst in GROUPS[s]:
                    w[:, dst:dst + width] = f["w_in"][l][:, src:src + width]
                n = columns(n, w)
            elif s[:2] == "br":
                n = rows(n, f["w_branch"][l, BRANCH_ORDER[int(s[2])]])
            elif s[:3] == "out":
                h = int(s[3])
                n = columns(n, f["w_out"][l][:, 512 * h:512 * h + 512])
        if l == 0:
            for g in range(DENSE_GROUPS):
                for w in (f["ffn_w1"][0], f["ffn_w3"][0]):
                    n = columns(n, w[:, 512 * g:512 * g + 512])
            n = rows(n, f["ffn_w2"][0])
    for e in range(EXPERTS):
        for g in range(EXP_GROUPS):
            for w in (f["moe_w1"][0, e], f["moe_w3"][0, e]):
                n = columns(n, w[:, 512 * g:512 * g + 512])
        n = rows(n, f["moe_w2"][0, e])
    assert n == PIECES

    small = np.zeros((LAYERS, P, N_SMALL), np.float32)

    def put(l, name, value, rows_=slice(None)):
        at, width = SMALL[name]
        small[l, rows_, at:at + width] = value

    for l in range(LAYERS):
        put(l, "w_uq", f["dsa_w_uq"][l].reshape(P, 512))
        put(l, "w_qidx", f["dsa_w_qidx"][l].reshape(P, 256))
        put(l, "w_uv", f["dsa_w_uv"][l].transpose(1, 0, 2).reshape(P, 256))
        put(l, "wa_up", f["rwkv_w_up"][l], slice(0, 64))
        put(l, "wa_up", f["rwkv_a_up"][l], slice(64, 128))
        put(l, "g_up", f["rwkv_g_up"][l])
        put(l, "g_mix", f["norm_mix_g"][l].reshape(KC, P).T)
        put(l, "g_ffn", f["norm_ffn_g"][l].reshape(KC, P).T)
        put(l, "mu", f["rwkv_mu"][l].reshape(8, P).T)
        for name, src in (("w0", "rwkv_w0"), ("a0", "rwkv_a0"), ("k_k", "rwkv_k_k"), ("k_a", "rwkv_k_a"),
                          ("r_k", "rwkv_r_k"), ("ln_g", "rwkv_ln_g"), ("ln_b", "rwkv_ln_b"), ("conv_b", "mlstm_conv_b")):
            put(l, name, f[src][l].reshape(2, P).T)
        put(l, "conv_w", f["mlstm_conv_w"][l].reshape(8, P).T)
        for at, src in ((0, "mlstm_b_i"), (32, "mlstm_b_f"), (64, "fox_b_f")):
            put(l, "gate_b", f[src][l].reshape(4, 1), slice(at, at + 4))
    put(1, "router", f["moe_router"][0].reshape(KC, P, EXPERTS).transpose(1, 0, 2).reshape(P, 64))
    row = np.concatenate([f[k] for k in ("dsa_g_cq", "dsa_g_ckv", "dsa_g_kidx", "mlstm_norm_g")], axis=1)
    return {"x": f["x"], "stream": pieces, "small": small, "row": row, "const": constants(),
            "final_g": f["final_norm_g"].reshape(1, D)}


def kernel(**inputs):
    import concourse.bacc as bacc
    from concourse.bass_utils import run_bass_kernel_spmd

    arrays = lay_out(inputs)
    nc = bacc.Bacc("TRN2", target_bir_lowering=False, num_devices=1)
    args = [nc.dram_tensor(k, a.shape, F32, kind="ExternalInput").ap() for k, a in arrays.items()]
    out = nc.dram_tensor("y", (1, T, D), F32, kind="ExternalOutput").ap()
    build(nc, *args, out)
    r = run_bass_kernel_spmd(nc, [arrays], core_ids=[0])
    return r.results[0]["y"]
```

```python
import numpy as np

import concourse.bass as bass
import concourse.mybir as mybir

F32 = mybir.dt.float32
F32R = mybir.dt.float32r
ALU = mybir.AluOpType
ACT = mybir.ActivationFunctionType
AX = mybir.AxisListType

P = 128
D = 1024
T = 256
TT = T // P
KC = D // P
LAYERS = 2
FF_DENSE = 2816
FF_EXPERT = 3584
EXPERTS = 8
TOPK = 64
EPS = 1e-6
GN_EPS = 64e-5
NEG = -1e30
TAKEN = -3e38
ABSENT = -3.2e38
DECAY = float(np.exp(-0.5))

Z_RWKV, Z_ML, Z_FOX, Z_GATE = 296, 1320, 2096, 2868
GROUPS = {
    "z_ml": [(Z_ML, 256, 0), (Z_ML + 768, 4, 256), (Z_ML + 772, 4, 288), (Z_FOX + 768, 4, 320), (256, 40, 352)],
    "z_lat": [(0, 256, 0), (Z_FOX + 512, 256, 256)],
    "z_mvo": [(Z_ML + 256, 512, 0)],
    "z_fox": [(Z_FOX, 512, 0)],
    "z_rw0": [(Z_RWKV, 512, 0)],
    "z_rw1": [(Z_RWKV + 512, 512, 0)],
}
BRANCH_ORDER = [3, 2, 0, 1]
for _b, _n in enumerate(BRANCH_ORDER):
    for _h in range(2):
        GROUPS[f"gate{_b}{_h}"] = [(Z_GATE + _n * D + _h * 512, 512, 0)]

SCHEDULE = [
    "norm_mix", "z_ml", "z_lat", "z_mvo", "ds_norm", "z_fox", "ds_tr", "ml_gate", "part:z_rw0", "part:z_rw0", "ds_q",
    "z_rw0", "ds_dot0", "part:z_rw1", "ml_D", "ml_in", "z_rw1", "ds_dot1", "part:gate00", "ml_qk", "part:gate00",
    "fx_L", "part:gate00", "gate00", "ds_topk", "fx_T", "part:gate01", "part:gate01", "fx_O", "ml_T", "gate01", "br0",
    "ml_N", "ds_L", "gate10", "ml_Y", "part:gate11", "part:gate11", "ds_T", "gate11", "ds_O", "part:gate20", "ds_Y",
    "part:gate20", "rw_mix", "gate20", "rw_lora", "part:gate21", "rw_fm", "part:gate21", "rw_tr", "rw_prod", "gate21",
    "br1", "rw_x0", "rw_m1", "br2", "rw_m2", "rw_m3", "rw_m4", "rw_m5", "rw_app", "rw_state", "gate30", "rw_Y",
    "rw_gn", "gate31", "br3", "mrg_tr", "out0", "out1", "norm_ffn",
]

def _episodes():
    eps, alt = [], 0
    own = {
        "ds_tr": [("dT", 4), ("dTk", 5)],
        "ds_q": [("dQ0", 6), ("dQ1", 7), ("dQi", 4)],
        "ds_dot0": [("dD0_%d" % b, 4 + b) for b in range(4)],
        "ds_dot1": [("dD1_%d" % b, 4 + b) for b in range(4)],
        "ml_D": [("mD0", 4), ("mD1", 5), ("mD2", 6)],
        "ml_qk": [("mQ%d" % h, 4 + h) for h in range(4)],
        "fx_L": [("fL%d" % i, 4 + i) for i in range(4)],
        "fx_T": [("fT%d" % i, 4 + i) for i in range(3)],
        "fx_O": [("fO", 7)],
        "ml_T": [("mT%d" % i, 4 + i) for i in range(3)],
        "ml_N": [("mN", 7)],
        "ml_Y": [("mY", 4)],
        "ds_L": [("dL%d" % i, 4 + i) for i in range(4)],
        "ds_T": [("dP%d" % i, 4 + i) for i in range(3)],
        "ds_O": [("dO0", 7), ("dO1", 4)],
        "ds_Y": [("dY", 5)],
        "rw_lora": [("rKK", 7), ("rW", 4), ("rA", 5), ("rG", 6)],
        "rw_tr": [("rtV", 4), ("rtA", 5), ("rtB", 6), ("rtK", 7), ("rBon", 4)],
        "rw_prod": [("rLT%d" % h, 4 + (1 + h) % 4) for h in range(4)] + [("rKT%d" % h, 4 + (1 + h) % 4) for h in range(4)],
        "rw_x0": [("rX0_0", 4), ("rX0_1", 5)],
        "rw_app": [("rLkV", 4), ("rXA0", 5), ("rXA1", 6)],
        "rw_state": [("rRp", 7), ("rP0", 4), ("rP1", 5), ("rG0", 6), ("rG1", 7), ("rS2", 4), ("rS3", 5)],
        "rw_Y": [("rY", 6)],
        "rw_gn": [("rMean", 7), ("rVar", 4)],
    }
    for j in range(1, 6):
        own["rw_m%d" % j] = [(f"rZ{j}_0", 4), (f"rZ{j}_1", 5), (f"rX{j}_0", 6), (f"rT{j}_0", 7), (f"rX{j}_1", 4), (f"rT{j}_1", 5)]
    own["rw_m5"] = [e for e in own["rw_m5"] if e[0][:2] != "rX"]
    for s in SCHEDULE:
        if s in ("norm_mix", "norm_ffn", "mrg_tr"):
            eps += [(f"{s}{b}", b) for b in range(4)]
        elif s in GROUPS or s.startswith("out"):
            eps += [(s + "a", alt), (s + "b", alt + 1)]
            alt = 2 - alt
        elif s.startswith("br"):
            for h in range(2):
                eps += [(f"{s}{h}a", alt), (f"{s}{h}b", alt + 1)]
                alt = 2 - alt
        else:
            eps += own.get(s, [])
    return eps

EPISODES = _episodes()
EP_BANK = dict(EPISODES)
EP_IN_BANK = [[n for n, b in EPISODES if b == k] for k in range(8)]
EP_NO = {n: EP_IN_BANK[b].index(n) for n, b in EPISODES}

PIECE = 2048
MIX_PIECES = sum(2 if (s in GROUPS or s.startswith("out")) else 1 if s.startswith("br") else 0 for s in SCHEDULE)
DENSE_BLOCKS = FF_DENSE // P
DENSE_GROUPS = -(-DENSE_BLOCKS // 4)
DENSE_PIECES = 4 * DENSE_GROUPS + DENSE_BLOCKS // 2
EXP_GROUPS = FF_EXPERT // 512
EXP_BLOCKS = FF_EXPERT // P
EXP_PIECES = 4 * EXP_GROUPS + EXP_BLOCKS // 2
FIRST_DENSE = MIX_PIECES
FIRST_EXPERT = 2 * MIX_PIECES + DENSE_PIECES
PIECES = FIRST_EXPERT + EXPERTS * EXP_PIECES

RING, RING_EXPERT = 5, 7
HIGH_MIX, HIGH_DENSE, HIGH_EXPERT = 2, 4, 7
assert EXP_PIECES % RING_EXPERT == 0 and EXP_PIECES % HIGH_EXPERT == 0
EXPERT_SLOTS = [(FIRST_EXPERT + i) % RING for i in range(RING)] + list(range(RING, RING_EXPERT))


def ring_slot(n):
    return n % RING if n < FIRST_EXPERT else EXPERT_SLOTS[(n - FIRST_EXPERT) % RING_EXPERT]


RING_USES = []
for _n in range(PIECES + EXP_PIECES):
    RING_USES.append(1 + sum(ring_slot(_m) == ring_slot(_n) for _m in range(_n)))

SPLIT_GROUPS = [s for s in SCHEDULE if s in GROUPS or s.startswith("out")]
FIRST_OF = {}
HIGH_SLOT, SPLIT_NO = [], []
for _l in range(LAYERS):
    for _s in SCHEDULE:
        if _s in SPLIT_GROUPS:
            FIRST_OF[_l, _s] = len(HIGH_SLOT)
            HIGH_SLOT += [0, 1]
        elif _s.startswith("br"):
            FIRST_OF[_l, _s] = len(HIGH_SLOT)
            HIGH_SLOT += [None]
    if _l == 0:
        HIGH_SLOT += [n % HIGH_DENSE for n in range(DENSE_PIECES)]
HIGH_SLOT += [n % HIGH_EXPERT for n in range((EXPERTS + 1) * EXP_PIECES)]
for _h in HIGH_SLOT:
    SPLIT_NO.append((SPLIT_NO[-1] if SPLIT_NO else 0) + (_h is not None))


SPLIT_LATER = {"gate31": "mrg_tr"}


def next_split(l, s):
    i = SPLIT_GROUPS.index(s) + 1
    if i < len(SPLIT_GROUPS):
        return FIRST_OF[l, SPLIT_GROUPS[i]]
    return FIRST_DENSE if l == 0 else None


def _columns(spec):
    at, out = 0, {}
    for name, n in spec:
        out[name] = (at, n)
        at += n
    return out, at

CONST, N_CONST = _columns([("ident", 128), ("pair_ones", 128), ("pair_mean", 128), ("negtri", 128), ("masks", 256),
                           ("level", 768), ("ident64", 64), ("reset", 256), ("ones", 256), ("before", 128),
                           ("iota", 256), ("pick", 8), ("eps", 1), ("gn_eps", 1), ("one", 1), ("is_f", 1), ("is_i", 1)])
SMALL, N_SMALL = _columns([("w_uq", 512), ("w_qidx", 256), ("w_uv", 256), ("wa_up", 256), ("g_up", 256), ("router", 64),
                           ("g_mix", 8), ("g_ffn", 8), ("mu", 8), ("w0", 2), ("a0", 2), ("k_k", 2), ("k_a", 2), ("r_k", 2),
                           ("ln_g", 2), ("ln_b", 2), ("conv_w", 8), ("conv_b", 2), ("gate_b", 1)])
ROW, N_ROW = _columns([("g_cq", 128), ("g_ckv", 128), ("g_kidx", 32), ("ml_g", 256)])


def constants():
    c = np.zeros((P, N_CONST), np.float32)
    i, j = np.arange(P)[:, None], np.arange(P)[None, :]

    def put(name, value):
        at, n = CONST[name]
        c[:, at:at + n] = value

    put("ident", i == j)
    put("pair_ones", i // 64 == j // 64)
    put("pair_mean", (i // 64 == j // 64) / 64.0)
    put("negtri", np.where(j <= i, 0.0, NEG))
    chunk = i // 64 == j // 64
    put("masks", np.concatenate([(i < j) & chunk, (i <= j) & chunk], 1))
    put("level", np.concatenate([(i < j) & (i // 2 ** (n + 1) == j // 2 ** (n + 1)) & (i // 2 ** n != j // 2 ** n)
                                 for n in range(6)], 1))
    put("ident64", (i % 64) == np.arange(64)[None, :])
    put("reset", (np.arange(256) % 64 != 0)[None, :])
    put("ones", 1.0)
    put("before", i < j)
    put("iota", np.arange(256)[None, :])
    for h in range(4):
        c[[h, 32 + h], CONST["pick"][0] + h] = 1.0
        c[64 + h, CONST["pick"][0] + 4 + h] = 1.0
    put("eps", EPS)
    put("gn_eps", GN_EPS)
    put("one", 1.0)
    put("is_f", i >= 32)
    put("is_i", i < 32)
    return c


def build(nc, x_in, stream, small_in, row_in, const_in, final_in, out):
    sems = {}

    def sem(name):
        if name not in sems:
            sems[name] = nc.alloc_semaphore(name)
        return sems[name]

    def sb(name, shape):
        return nc.alloc_sbuf_tensor(name, shape, F32)

    x = sb("resid", [P, TT, D])
    xn = sb("xn", [P, TT, D])
    small = sb("smalls", [P, N_SMALL])
    row = sb("rows", [P, N_ROW])
    stat = sb("stat", [P, 144])
    over_i = nc.alloc_sbuf_tensor("over_i", [P, 1], mybir.dt.int32)
    slab_at = -(-nc.sbuf_base // 32) * 32
    SLAB = (nc.sbuf_top - slab_at) // 32 * 8
    nc.alloc_sbuf_tensor("slab", [P, SLAB], F32)
    placed = [0]

    def place(name, shape, dtype):
        n = int(np.prod(shape[1:]))
        t = nc.alloc_sbuf_tensor_at(name, shape, dtype, offset=slab_at + 4 * placed[0])
        placed[0] += -(-n // 8) * 8
        assert placed[0] <= SLAB, (name, placed[0], SLAB)
        return t

    def both(name, shape):
        at = placed[0]
        plain = place(name, shape, F32)
        placed[0] = at
        return plain, place(name + "_r", shape, F32R)

    const, const_r = both("consts", [P, N_CONST])
    ring_a, ring_a_r = both("ring_a", [P, RING, PIECE])
    high_a = place("high_a", [P, HIGH_MIX, PIECE], F32R)
    placed_hT = placed[0]
    hT_h = place("hT_h", [P, KC, T], F32R)
    hT_l = place("hT_l", [P, KC, T], F32R)
    arena_at = placed[0]
    ARENA = SLAB - arena_at
    arena, arena_r = both("arena", [P, ARENA])
    placed[0] = placed_hT
    hT = place("hT", [P, KC, T], F32)
    hsel_h = place("hsel_h", [P, KC, P], F32R)
    hsel_l = place("hsel_l", [P, KC, P], F32R)
    assert placed[0] == arena_at
    high_dense = place("high_dense", [P, HIGH_DENSE - HIGH_MIX, PIECE], F32R)
    denseT_h = place("denseT_h", [P, DENSE_BLOCKS, T], F32R)
    denseT_l = place("denseT_l", [P, DENSE_BLOCKS, T], F32R)
    dsil = place("dsil", [P, 4, T], F32)
    placed[0] = arena_at
    ring_b, ring_b_r = both("ring_b", [P, RING_EXPERT - RING, PIECE])
    high_expert = place("high_expert", [P, HIGH_EXPERT - HIGH_MIX, PIECE], F32R)
    actT_h = place("actT_h", [P, EXP_BLOCKS, P], F32R)
    actT_l = place("actT_l", [P, EXP_BLOCKS, P], F32R)
    experts_at = placed[0] - arena_at

    def raw(n):
        i = ring_slot(n)
        return ring_a[:, i, :] if i < RING else ring_b[:, i - RING, :]

    def low(n):
        i = ring_slot(n)
        return ring_a_r[:, i, :] if i < RING else ring_b_r[:, i - RING, :]

    def high(n):
        i = HIGH_SLOT[n]
        more = high_expert if n >= FIRST_EXPERT else high_dense
        return high_a[:, i, :] if i < HIGH_MIX else more[:, i - HIGH_MIX, :]

    def piece_in(n):
        return sem(f"piece{ring_slot(n)}_in")

    pb = [nc.alloc_psum_tensor(f"bank{i}", [P, 512], F32) for i in range(8)]

    ROUNDED = ("negtri", "pick", "ident")

    def c_(name):
        at, n = CONST[name]
        return const_r[:, at:at + n].bitcast(F32) if name in ROUNDED else const[:, at:at + n]

    def exact(name):
        at, n = CONST[name]
        return const_r[:, at:at + n]

    def s_(l, name):
        at, n = SMALL[name]
        return small[:, at:at + n]

    def r_(l, name):
        at, n = ROW[name]
        return row[:, at:at + n]

    top = [0]

    def area(*shape):
        n = int(np.prod(shape))
        a = arena[:, top[0]:top[0] + n]
        top[0] += n
        assert top[0] <= ARENA, top[0]
        if len(shape) == 2:
            a = a.rearrange("p (a b) -> p a b", a=shape[0])
        if len(shape) == 3:
            a = a.rearrange("p (a b c) -> p a b c", a=shape[0], b=shape[1])
        if len(shape) == 4:
            a = a.rearrange("p (a b c d) -> p a b c d", a=shape[0], b=shape[1], c=shape[2])
        return a

    yT = area(4, 2, T)
    gates = area(2, TT, D)
    Zr = area(8, T + 1)
    shared = top[0]
    z_lat = area(TT, 512)
    z_mvo = area(TT, 512)
    z_idx = area(TT, 40)
    conv_in = area(2, T + 3)
    conv = area(2, T)
    conv_s = area(2, T)
    g_pre, g_tmp, g_exp, g_cum, g_pos, g_key = (area(T) for _ in range(6))
    g_pos_h, g_key_h, g_pos_l, g_key_l = (arena_r[:, top[0] - n * T:top[0] - n * T + T] for n in (6, 4, 2, 1))
    foxq, foxk = area(2, T), area(2, T)
    probs = area(TT, 4, T)
    probsT = area(12, P)
    relu = area(8, T)
    mlP = relu.rearrange("p a b -> p (a b)").rearrange("p (a b c) -> p a b c", a=TT, b=4)
    lat_n = area(TT, 2, P)
    lat_sq = area(TT, 2, P)
    ki4 = area(TT, 4, 32)
    ki_sq = area(TT, 32)
    latT = area(2, T)
    kiT = area(T)
    dsq = area(4, T)
    qiT = area(2, T)
    score_r = arena_r[:, top[0]:top[0] + TT * T].rearrange("p (a b) -> p a b", a=TT)
    score = area(TT, T)
    best = area(TT, 8)
    dsO = relu[:, 0:4, :]
    cell = area(TT, 256)
    cell_sq = lat_sq.rearrange("p a b c -> p a (b c)")
    osig = conv_s
    attn_top = top[0]
    top[0] = shared
    kkn, t0, lw, cum, cml, Wf, sa, k2 = (area(2, T) for _ in range(8))
    AR = area(2, 2, T)
    tanh_w = area(T)
    sig_g = area(T)
    gout = area(2, T)
    Vtm, Atm, Btm, Ktm = (Zr.rearrange("p a b -> p (a b)")[:, 512 * n:512 * n + 512].rearrange("p (a b) -> p a b", a=TT) for n in range(4))
    LQ = area(4, TT, 256)
    KQ = area(4, TT, 256)
    lev = area(2, 8, P)
    X, Z = area(8, P), area(8, P)
    Xf, Zf = X.rearrange("p a b -> p (a b)"), Z.rearrange("p a b -> p (a b)")
    RpT = Xf[:, 0:512].rearrange("p (a b) -> p a b", a=2)
    PT = Xf[:, 512:1024].rearrange("p (c a t k) -> p c a t k", c=2, a=2, t=TT)
    GW = Zf[:, 0:512].rearrange("p (c a t k) -> p c a t k", c=2, a=2, t=TT)
    S2, S3 = (Zf[:, 512 + 128 * n:640 + 128 * n].rearrange("p (a b) -> p a b", a=2) for n in range(2))
    ALV, XALV = lev[:, 0, :, :], lev[:, 1, :, :]
    Zm = area(8, T)
    XT = Zm.rearrange("p a b -> p (a b)")[:, 0:8 * P].rearrange("p (a b) -> p a b", a=8)
    bon = area(2, T)
    Ys, Yc, Yq = Wf, t0, cml
    rwkv_top = top[0]
    top[0] = max(attn_top, rwkv_top)
    mtmp = area(512)
    top[0] = experts_at
    hT_rows = hT[:, :, :].rearrange("p a b -> p (a b)")
    sil, act = (hT_rows[:, 1024 * n:1024 * n + 1024].rearrange("p (a b) -> p a b", a=2) for n in range(2))
    pickT = area(T)
    pick = area(TT, P)
    pickg = area(TT, P)
    yexp = area(D)
    rank = area(TT, EXPERTS + 1)
    took = area(TT, EXPERTS + 1)
    weight = area(TT, EXPERTS + 1)
    rtmp = area(TT, 64)
    over = area(8)
    assert top[0] < ARENA - D
    final_g = arena[:, ARENA - D:ARENA]

    def bank2(name, n=T):
        return pb[EP_BANK[name]][:, :].rearrange("p (a b) -> p a b", a=512 // n)

    def bank(name):
        return pb[EP_BANK[name]]

    def full(eng, l, name):
        b = EP_BANK[name]
        eng.wait_ge(sem(f"bank{b}_full"), l * len(EP_IN_BANK[b]) + EP_NO[name] + 1)

    def drained(eng, l, name):
        b = EP_BANK[name]
        eng.wait_ge(sem(f"bank{b}_free"), l * len(EP_IN_BANK[b]) + EP_NO[name] + 1)

    def freed(name):
        return sem(f"bank{EP_BANK[name]}_free")

    def begin(eng, l, name):
        b = EP_BANK[name]
        before = l * len(EP_IN_BANK[b]) + EP_NO[name]
        if before:
            eng.wait_ge(sem(f"bank{b}_free"), before)

    def filled(name):
        return sem(f"bank{EP_BANK[name]}_full")

    HEADS = [(h, h // 2, slice(64 * (h % 2), 64 * (h % 2) + 64)) for h in range(4)]

    def tsl(tt):
        return slice(tt * P, tt * P + P)

    ctx_block = nc.Block()
    block = ctx_block.__enter__()

    @block.sync
    def _(sp):
        sp.dma_start(x[:, :, :], x_in.rearrange("b (t p) d -> p (b t) d", p=P)).then_inc(sem("x_in"), 16)
        sp.dma_start(const[:, :], const_in).then_inc(sem("const_in"), 16)

        def load(n, before, i=None, step=0):
            src = stream[n] if i is None else stream[bass.ds(i * step + n, 1)].rearrange("a p n -> (a p) n")
            if before is not None:
                sp.wait_ge(sem("piece_used"), before + 1 if i is None else i * step + (before + 1))
            sp.dma_start(raw(n), src).then_inc(piece_in(n), 16)

        load(0, None)
        sp.dma_start(small[:, :], small_in[0]).then_inc(sem("small0_in"), 16)
        load(1, None)
        sp.dma_start(row[:, :], row_in[0:1, :].broadcast_to([P, N_ROW])).then_inc(sem("row0_in"), 16)
        for n in range(2, RING):
            load(n, None)
        rounds = FIRST_EXPERT // RING - 1
        with sp.Fori(0, rounds) as i:
            for s in range(RING):
                load(RING + s, s, i, RING)
        for n in range(RING * (rounds + 1), FIRST_EXPERT + RING):
            load(n, n - RING)
        drained(sp, 1, "out1b")
        for n in range(FIRST_EXPERT + RING, FIRST_EXPERT + RING_EXPERT):
            load(n, None)
        with sp.Fori(0, EXPERTS * EXP_PIECES // RING_EXPERT - 1) as i:
            for s in range(RING_EXPERT):
                load(FIRST_EXPERT + RING_EXPERT + s, FIRST_EXPERT + s, i, RING_EXPERT)

        sp.wait_ge(sem("over_known"), 1)
        more = sp.value_load(over_i[0:1, 0:1], min_val=0, max_val=1)
        with sp.If(more > 0):
            with sp.Fori(0, EXPERTS) as e:
                for j in range(EXP_PIECES):
                    sp.wait_ge(sem("piece_used"), e * EXP_PIECES + (PIECES + j - RING_EXPERT + 1))
                    sp.dma_start(raw(PIECES + j),
                                 stream[bass.ds(e * EXP_PIECES + (FIRST_EXPERT + j), 1)].rearrange("a p n -> (a p) n"))\
                      .then_inc(piece_in(PIECES + j), 16)
        for tt in range(TT):
            sp.wait_ge(sem("out_ready"), tt + 1)
            sp.dma_start(out.rearrange("b (t p) d -> p (b t) d", p=P)[:, tt, :], xn[:, tt, :]).then_inc(sem("out_stored"), 16)
        sp.wait_ge(sem("out_stored"), 16 * TT)

    @block.tensor
    def _(pe):
        mm = nc.tensor.matmul
        pend = [0]
        ident = c_("ident")

        def smm(o, lhsT, rhs, start, stop):
            ins = mm(o, lhsT, rhs, start=start, stop=stop)
            if pend[0]:
                ins.then_inc(sem("piece_used"), pend[0])
                pend[0] = 0
            return ins

        def arrived(n):
            pe.wait_ge(piece_in(n), 16 * RING_USES[n])

        def is_split(n):
            pe.wait_ge(sem("split_lo"), SPLIT_NO[n])

        def parts(o, lhs, rhs, first, last):
            (lh, ll), (rh, rl) = lhs, rhs
            a = smm(o, lh, rh, first, False)
            smm(o, lh, rl, False, False)
            return a, smm(o, ll, rh, False, last)

        def wparts(n, k, width, cols):
            return tuple(w.rearrange("p (k n) -> p k n", n=width)[:, k, cols] for w in (high(n), low(n)))

        def hparts(k, cols=slice(0, T)):
            return hT_h[:, k, cols], hT_l[:, k, cols]

        def fm_part(o, n0, kk, at, width, first=True, last=True):
            is_split(n0 + kk)
            for k in range(4):
                _, ins = parts(o, wparts(n0 + kk, k, 512, slice(at, at + width)), hparts(4 * kk + k),
                               first and kk == 0 and k == 0, last and kk == 1 and k == 3)
            return ins

        def tm_part(o, n0, kk, tt, at=0, width=512, first=True, last=True):
            is_split(n0 + kk)
            for k in range(4):
                _, ins = parts(o, hparts(4 * kk + k, tsl(tt)), wparts(n0 + kk, k, 512, slice(at, at + width)),
                               first and kk == 0 and k == 0, last and kk == 1 and k == 3)
            return ins

        quarters = {}

        def quarter(l, step):
            q = quarters.get((l, step), 0)
            quarters[l, step] = q + 1
            n0 = FIRST_OF[l, step]
            kk, side = divmod(q, 2)
            ep = step + "ab"[side]
            if kk == 0:
                begin(pe, l, ep)
            if step == "z_ml" or step == "out0":
                drained(pe, l, ("norm_mix" if step == "z_ml" else "mrg_tr") + ("3" if kk else "1"))
            if step not in ("z_ml", "z_fox", "z_rw0", "z_rw1"):
                ins = tm_part(bank(ep)[:, :], n0, kk, side)
            elif step == "z_ml" and side:
                fm_part(bank(ep)[0:96, 0:T], n0, kk, 256, 96, last=False)
                for tt in range(TT):
                    ins = tm_part(bank(ep)[:, T + 40 * tt:T + 40 * tt + 40], n0, kk, tt, 352, 40, first=False, last=tt == 1)
            else:
                for i in range(2):
                    ins = fm_part(bank2(ep)[:, i, :], n0, kk, 2 * side * P + i * P, P, first=i == 0, last=i == 1)
            if kk:
                ins.then_inc(filled(ep), 1)
            elif side:
                ins.then_inc(sem("piece_used"), 1)
            if q == 3:
                pend[0] = 1

        def group(l, step):
            while quarters.get((l, step), 0) < 4:
                quarter(l, step)

        def norm_transposes(l, step, j):
            for b in range(4):
                begin(pe, l, f"{step}{b}")
                for kk in range(2):
                    for tt in range(TT):
                        if b == 0 and kk == 0:
                            pe.wait_ge(sem("normed"), TT * j + tt + 1)
                        ins = nc.tensor.transpose(pb[b][:, kk * T + tt * P:kk * T + tt * P + P],
                                                  xn[:, tt, (2 * b + kk) * P:(2 * b + kk + 1) * P], ident)
                ins.then_inc(filled(f"{step}{b}"), 1)

        def branch_half(l, bi):
            half = quarters.get((l, bi), 0)
            quarters[l, bi] = half + 1
            n = FIRST_OF[l, f"br{bi}"]
            yi = BRANCH_ORDER[bi]
            if half == 0:
                arrived(n)
                drained(pe, l, {3: "fO", 2: "mY", 0: "dY", 1: "rVar"}[yi])
                if yi == 1:
                    pe.wait_ge(sem("rwkv_out"), l + 1)
            for tt, ep in ((0, f"br{bi}{half}a"), (1, f"br{bi}{half}b")):
                begin(pe, l, ep)
                for k in range(2):
                    ins = smm(bank(ep)[:, :], yT[:, yi, k, tsl(tt)],
                              raw(n).rearrange("p (k n) -> p k n", k=2)[:, k, half * 512:half * 512 + 512], k == 0, k == 1)
                ins.then_inc(filled(ep), 1)
            if half:
                pend[0] = 1

        def branch(l, bi):
            while quarters.get((l, bi), 0) < 2:
                branch_half(l, bi)

        def merged_transposes(l):
            for b in range(4):
                pe.wait_ge(sem("merged"), 2 * l + b // 2 + 1)
                begin(pe, l, f"mrg_tr{b}")
                for kk in range(2):
                    for tt in range(TT):
                        ins = nc.tensor.transpose(pb[b][:, kk * T + tt * P:kk * T + tt * P + P],
                                                  xn[:, tt, (2 * b + kk) * P:(2 * b + kk + 1) * P], ident)
                ins.then_inc(filled(f"mrg_tr{b}"), 1)

        def ds_tr(l):
            pe.wait_ge(sem("lat_normed"), l + 1)
            begin(pe, l, "dT")
            for w in range(2):
                for tt in range(TT):
                    ins = nc.tensor.transpose(bank("dT")[:, w * T + tt * P:w * T + tt * P + P], lat_n[:, tt, w, :], ident)
            ins.then_inc(filled("dT"), 1)
            begin(pe, l, "dTk")
            for tt in range(TT):
                ins = nc.tensor.transpose(bank("dTk")[:, tsl(tt)], ki4[:, tt, :, :].rearrange("p a b -> p (a b)"), ident)
            ins.then_inc(filled("dTk"), 1)

        def ds_q(l):
            drained(pe, l, "dT")
            for i in range(2):
                begin(pe, l, f"dQ{i}")
                for j in range(2):
                    h = 2 * i + j
                    ins = mm(bank2(f"dQ{i}")[:, j, :], s_(l, "w_uq")[:, h * P:h * P + P], latT[:, 0, :], start=True, stop=True)
                ins.then_inc(filled(f"dQ{i}"), 1)
            begin(pe, l, "dQi")
            for j in range(2):
                ins = mm(bank2("dQi")[:, j, :], s_(l, "w_qidx")[:, j * P:j * P + P], latT[:, 0, :], start=True, stop=True)
            ins.then_inc(filled("dQi"), 1)

        def ds_dot(l, tt):
            drained(pe, l, "dQi")
            drained(pe, l, "dTk")
            for b in range(4):
                ep = f"dD{tt}_{b}"
                begin(pe, l, ep)
                for j in range(2):
                    ins = mm(bank2(ep)[:, j, 0:P * (tt + 1)], qiT[32 * b:32 * b + 32, j, tsl(tt)],
                             kiT[32 * b:32 * b + 32, 0:P * (tt + 1)], start=True, stop=True, tile_position=(32 * b, 0))
                ins.then_inc(filled(ep), 1)

        def causal(o, tt):
            return mm(o[:, tt * P:tt * P + P], exact("ident"), exact("negtri"), start=False, stop=True)

        def ds_L(l):
            pe.wait_ge(sem("topk_mask"), l + 1)
            drained(pe, l, "dQ1")
            for i in range(4):
                tt, ns = i // 2, P * (i // 2 + 1)
                begin(pe, l, f"dL{i}")
                for j in range(2):
                    h = 2 * (i % 2) + j
                    o = bank2(f"dL{i}")[:, j, 0:ns]
                    mm(o, dsq[:, h, tsl(tt)], latT[:, 1, 0:ns], start=True, stop=False)
                    ins = mm(o, exact("ident"), score_r[:, tt, 0:ns], start=False, stop=True)
                ins.then_inc(filled(f"dL{i}"), 1)

        def probs_transposes(l, eps, src):
            for i, ep in enumerate(eps):
                begin(pe, l, ep)
                for j in range(4):
                    h, tt, sblk = (j, 0, 0) if i == 0 else (2 * (i - 1) + j // 2, 1, j % 2)
                    ins = nc.tensor.transpose(bank(ep)[:, j * P:j * P + P], src[:, tt, h, sblk * P:sblk * P + P], ident)
                ins.then_inc(filled(ep), 1)

        def pT(h, tt, sblk):
            return probsT[:, h if tt == 0 else 4 + 2 * h + sblk, :]

        def ds_O(l):
            drained(pe, l, "dP0")
            drained(pe, l, "dP1")
            drained(pe, l, "dP2")
            for i in range(2):
                begin(pe, l, f"dO{i}")
                for j in range(2):
                    h = 2 * i + j
                    for tt in range(TT):
                        for sblk in range(tt + 1):
                            ins = mm(bank2(f"dO{i}")[:, j, tsl(tt)], lat_n[:, sblk, 1, :], pT(h, tt, sblk),
                                     start=sblk == 0, stop=sblk == tt)
                ins.then_inc(filled(f"dO{i}"), 1)

        def ds_Y(l):
            drained(pe, l, "dO0")
            drained(pe, l, "dO1")
            begin(pe, l, "dY")
            for h, blk, ps in HEADS:
                ins = mm(bank2("dY")[ps, blk, :], s_(l, "w_uv")[:, h * 64:h * 64 + 64], dsO[:, h, :], start=True, stop=True)
            ins.then_inc(filled("dY"), 1)

        def decay_logits(o, row_, tt, ns, start):
            pk = exact("pick")[0:96, row_:row_ + 1]
            for n, part in enumerate((g_pos_h, g_pos_l)):
                mm(o, part[0:96, tsl(tt)], pk.broadcast_to([96, ns]), start=start and n == 0, stop=False)
            for part in (g_key_h, g_key_l):
                mm(o, pk.broadcast_to([96, P]), part[0:96, 0:ns], start=False, stop=False)

        def ml_D(l):
            pe.wait_ge(sem("gate_sums"), l + 1)
            for i in range(3):
                tt = 0 if i == 0 else 1
                ns = P * (tt + 1)
                begin(pe, l, f"mD{i}")
                for j in range(512 // ns):
                    h = j if i == 0 else 2 * (i - 1) + j
                    o = bank(f"mD{i}")[:, j * ns:j * ns + ns]
                    decay_logits(o, h, tt, ns, True)
                    ins = causal(o, tt)
                ins.then_inc(filled(f"mD{i}"), 1)

        def ml_qk(l):
            pe.wait_ge(sem("conv_done"), l + 1)
            for h in range(4):
                ep = f"mQ{h}"
                begin(pe, l, ep)
                hs = slice(32 * h, 32 * h + 32)
                mm(bank(ep)[:, 0:P], conv[hs, 0, 0:P], conv[hs, 1, 0:P], start=True, stop=True, tile_position=(32 * h, 0))
                mm(bank(ep)[:, P:P + T], conv[hs, 0, P:T], conv[hs, 1, :], start=True, stop=True, tile_position=(32 * h, 0))\
                    .then_inc(filled(ep), 1)

        def ml_N(l):
            for i in range(3):
                drained(pe, l, f"mT{i}")
            begin(pe, l, "mN")
            for tt in range(TT):
                for h in range(4):
                    for sblk in range(tt + 1):
                        ins = mm(bank("mN")[:, tt * 256 + h * 64:tt * 256 + h * 64 + 64], pT(h, tt, sblk),
                                 z_mvo[:, sblk, h * 64:h * 64 + 64], start=sblk == 0, stop=sblk == tt)
            ins.then_inc(filled("mN"), 1)

        def ml_Y(l):
            pe.wait_ge(sem("ml_cell"), l + 1)
            begin(pe, l, "mY")
            for blk in range(2):
                for tt in range(TT):
                    ins = nc.tensor.transpose(bank2("mY")[:, blk, tsl(tt)], cell[:, tt, blk * P:blk * P + P], ident)
            ins.then_inc(filled("mY"), 1)

        def fx_L(l):
            pe.wait_ge(sem("gate_sums"), l + 1)
            drained(pe, l, "z_foxa")
            drained(pe, l, "z_foxb")
            for i in range(4):
                tt, ns = i // 2, P * (i // 2 + 1)
                begin(pe, l, f"fL{i}")
                for j in range(2):
                    h = i % 2 + 2 * j
                    ps = HEADS[h][2]
                    o = bank2(f"fL{i}")[:, j, 0:ns]
                    mm(o, foxq[ps, j, tsl(tt)], foxk[ps, j, 0:ns], start=True, stop=False)
                    decay_logits(o, 4 + h, tt, ns, False)
                    ins = causal(o, tt)
                ins.then_inc(filled(f"fL{i}"), 1)

        def fx_O(l):
            for i in range(3):
                drained(pe, l, f"fT{i}")
            begin(pe, l, "fO")
            for h, blk, ps in HEADS:
                for tt in range(TT):
                    for sblk in range(tt + 1):
                        ins = mm(bank2("fO")[ps, blk, tsl(tt)], z_lat[:, sblk, 256 + h * 64:256 + h * 64 + 64], pT(h, tt, sblk),
                                 start=sblk == 0, stop=sblk == tt)
            ins.then_inc(filled("fO"), 1)

        def rw_lora(l):
            pe.wait_ge(sem("rw_kksq"), l + 1)
            begin(pe, l, "rKK")
            mm(bank("rKK")[:, :], c_("pair_ones"), t0.rearrange("p a b -> p (a b)"), start=True, stop=True)\
                .then_inc(filled("rKK"), 1)
            pe.wait_ge(sem("rw_lora_in"), l + 1)
            for ep, w, rhs in (("rW", s_(l, "wa_up")[0:64, :], tanh_w[0:64, :]),
                               ("rA", s_(l, "wa_up")[64:128, :], Zm[64:128, 6, :]),
                               ("rG", s_(l, "g_up"), sig_g)):
                begin(pe, l, ep)
                for blk in range(2):
                    ins = mm(bank2(ep)[:, blk, :], w[:, blk * P:blk * P + P], rhs, start=True, stop=True)
                ins.then_inc(filled(ep), 1)

        def rw_tr(l):
            def turn(ep, src):
                begin(pe, l, ep)
                for tt in range(TT):
                    for blk in range(2):
                        ins = nc.tensor.transpose(bank(ep)[:, tt * 256 + blk * P:tt * 256 + blk * P + P], src(blk, tt), ident)
                ins.then_inc(filled(ep), 1)
            turn("rtV", lambda blk, tt: Zm[:, 4 + blk, tsl(tt)])
            quarter(l, "gate21")
            quarter(l, "gate21")
            branch_half(l, 1)
            pe.wait_ge(sem("rw_fm_done"), l + 1)
            turn("rtA", lambda blk, tt: AR[:, blk, 0, tsl(tt)])
            turn("rtB", lambda blk, tt: sa[:, blk, tsl(tt)])
            turn("rtK", lambda blk, tt: k2[:, blk, tsl(tt)])
            begin(pe, l, "rBon")
            mm(bank("rBon")[:, :], c_("pair_ones"), t0.rearrange("p a b -> p (a b)"), start=True, stop=True)\
                .then_inc(filled("rBon"), 1)

        def rw_prod(l):
            for pre, src in (("rLT", sa), ("rKT", k2)):
                for h, blk, ps in HEADS:
                    ep = f"{pre}{h}"
                    begin(pe, l, ep)
                    for tt in range(TT):
                        ins = mm(bank2(ep)[:, tt, :].rearrange("p (a b) -> p a b", a=2), src[ps, blk, tsl(tt)],
                                 AR[ps, blk, :, tsl(tt)], start=True, stop=True)
                    ins.then_inc(filled(ep), 1)

        def rw_x0(l):
            pe.wait_ge(sem("rw_xt0"), l + 1)
            for i in range(2):
                begin(pe, l, f"rX0_{i}")
                for j in range(4):
                    ins = nc.tensor.transpose(bank(f"rX0_{i}")[:, j * P:j * P + P], XT[:, 4 * i + j, :], ident)
                ins.then_inc(filled(f"rX0_{i}"), 1)

        def rw_merge(l, j):
            pe.wait_ge(sem("rw_level"), 5 * l + j)
            for i in range(2):
                drained(pe, l, f"rX{j - 1}_{i}")
                if j > 1:
                    drained(pe, l, f"rT{j - 1}_{i}")
                ep = f"rZ{j}_{i}"
                begin(pe, l, ep)
                for q in range(4 * i, 4 * i + 4):
                    ins = mm(bank(ep)[:, (q % 4) * P:(q % 4) * P + P], lev[:, j % 2, q, :], X[:, q, :], start=True, stop=True)
                ins.then_inc(filled(ep), 1)
            for i in range(2):
                drained(pe, l, f"rZ{j}_{i}")
                for ep, lhs, rhs in ((f"rX{j}_{i}", XT, Z), (f"rT{j}_{i}", Z, XT))[j == 5:]:
                    begin(pe, l, ep)
                    for q in range(4 * i, 4 * i + 4):
                        ins = mm(bank(ep)[:, (q % 4) * P:(q % 4) * P + P], lhs[:, q, :], rhs[:, q, :], start=True, stop=True)
                    ins.then_inc(filled(ep), 1)

        def rw_app(l):
            drained(pe, l, "rtV")
            drained(pe, l, "rKT3")
            begin(pe, l, "rLkV")
            for h in range(4):
                for tt in range(TT):
                    q = 2 * h + tt
                    ins = mm(bank("rLkV")[:, q * 64:q * 64 + 64], KQ[:, h, tt, 0:P], Vtm[:, tt, h * 64:h * 64 + 64],
                             start=True, stop=True)
            ins.then_inc(filled("rLkV"), 1)
            quarter(l, "gate30")
            pe.wait_ge(sem("rw_alv"), l + 1)
            for i in range(2):
                drained(pe, l, f"rT5_{i}")
                begin(pe, l, f"rXA{i}")
                for q in range(4 * i, 4 * i + 4):
                    ins = mm(bank(f"rXA{i}")[:, (q % 4) * P:(q % 4) * P + P], XT[:, q, :], ALV[:, q, :], start=True, stop=True)
                ins.then_inc(filled(f"rXA{i}"), 1)

        def rw_state(l):
            quarter(l, "gate30")
            drained(pe, l, "rtB")
            drained(pe, l, "rtK")
            drained(pe, l, "rXA0")
            drained(pe, l, "rXA1")
            begin(pe, l, "rRp")
            for h, blk, ps in HEADS:
                for tt in range(TT):
                    ins = mm(bank2("rRp")[ps, blk, tsl(tt)], XALV[:, 2 * h + tt, 0:64], LQ[:, h, tt, P:2 * P], start=True, stop=True)
            ins.then_inc(filled("rRp"), 1)
            for c in range(2):
                cs = slice(64 * c, 64 * c + 64)
                begin(pe, l, f"rP{c}")
                for h, blk, ps in HEADS:
                    for tt in range(TT):
                        at = (blk * 2 + tt) * 64
                        ins = mm(bank(f"rP{c}")[ps, at:at + 64], XALV[cs, 2 * h + tt, 0:64], Btm[cs, tt, h * 64:h * 64 + 64],
                                 start=True, stop=True)
                ins.then_inc(filled(f"rP{c}"), 1)
            for c in range(2):
                cs = slice(64 * c, 64 * c + 64)
                begin(pe, l, f"rG{c}")
                for h, blk, ps in HEADS:
                    for tt in range(TT):
                        at = (blk * 2 + tt) * 64
                        o = bank(f"rG{c}")[ps, at:at + 64]
                        mm(o, Btm[cs, tt, h * 64:h * 64 + 64], XALV[cs, 2 * h + tt, 64:128], start=True, stop=False)
                        ins = mm(o, Ktm[cs, tt, h * 64:h * 64 + 64], Vtm[cs, tt, h * 64:h * 64 + 64], start=False, stop=True)
                ins.then_inc(filled(f"rG{c}"), 1)
            quarter(l, "gate30")
            drained(pe, l, "rP1")
            drained(pe, l, "rG0")
            drained(pe, l, "rG1")
            for ep, c, tt, prev in (("rS2", 1, 0, lambda blk: GW[:, 0, blk, 0, :]), ("rS3", 0, 1, lambda blk: S2[:, blk, :])):
                if ep == "rS3":
                    quarter(l, "gate30")
                    drained(pe, l, "rS2")
                begin(pe, l, ep)
                for h, blk, ps in HEADS:
                    ins = mm(bank(ep)[ps, blk * 64:blk * 64 + 64], PT[ps, c, blk, tt, :], prev(blk)[ps, :], start=True, stop=True)
                ins.then_inc(filled(ep), 1)

        def rw_Y(l):
            drained(pe, l, "rRp")
            drained(pe, l, "rS3")
            begin(pe, l, "rY")
            entering = {1: lambda blk: GW[:, 0, blk, 0, :], 2: lambda blk: S2[:, blk, :], 3: lambda blk: S3[:, blk, :]}
            for h, blk, ps in HEADS:
                for tt in range(TT):
                    q = 2 * h + tt
                    o = bank2("rY")[ps, blk, tsl(tt)]
                    mm(o, XALV[:, q, 64:128], LQ[:, h, tt, P:2 * P], start=True, stop=False)
                    mm(o, Vtm[:, tt, h * 64:h * 64 + 64], KQ[:, h, tt, P:2 * P], start=False, stop=False)
                    for c in range(2):
                        n = 2 * tt + c
                        if n:
                            ins = mm(bank2("rY")[ps, blk, n * 64:n * 64 + 64], entering[n](blk)[ps, :],
                                     RpT[ps, blk, n * 64:n * 64 + 64], start=False, stop=c == 1)
            ins.then_inc(filled("rY"), 1)

        def rw_gn(l):
            quarter(l, "gate31")
            drained(pe, l, "rY")
            begin(pe, l, "rMean")
            mm(bank("rMean")[:, :], c_("pair_mean"), Ys.rearrange("p a b -> p (a b)"), start=True, stop=True)\
                .then_inc(filled("rMean"), 1)
            quarter(l, "gate31")
            pe.wait_ge(sem("rw_ysq"), l + 1)
            begin(pe, l, "rVar")
            mm(bank("rVar")[:, :], c_("pair_mean"), Yq.rearrange("p a b -> p (a b)"), start=True, stop=True)\
                .then_inc(filled("rVar"), 1)

        def mixer(l):
            for step in SCHEDULE:
                if step == "norm_mix":
                    norm_transposes(l, step, 2 * l)
                elif step == "norm_ffn":
                    norm_transposes(l, step, 2 * l + 1)
                elif step in SPLIT_GROUPS:
                    group(l, step)
                elif step[:5] == "part:":
                    quarter(l, step[5:])
                elif step[:2] == "br":
                    branch(l, int(step[2]))
                elif step == "mrg_tr":
                    merged_transposes(l)
                elif step == "ds_tr":
                    ds_tr(l)
                elif step == "ds_q":
                    ds_q(l)
                elif step[:6] == "ds_dot":
                    ds_dot(l, int(step[6]))
                elif step == "ds_L":
                    ds_L(l)
                elif step == "ds_T":
                    pe.wait_ge(sem("ds_probs"), l + 1)
                    probs_transposes(l, ["dP0", "dP1", "dP2"], probs)
                elif step == "ds_O":
                    ds_O(l)
                elif step == "ds_Y":
                    ds_Y(l)
                elif step == "ml_D":
                    ml_D(l)
                elif step == "ml_qk":
                    ml_qk(l)
                elif step == "ml_T":
                    drained(pe, l, "mQ3")
                    probs_transposes(l, ["mT0", "mT1", "mT2"], mlP)
                elif step == "ml_N":
                    ml_N(l)
                elif step == "ml_Y":
                    ml_Y(l)
                elif step == "fx_L":
                    fx_L(l)
                elif step == "fx_T":
                    pe.wait_ge(sem("fx_probs"), l + 1)
                    probs_transposes(l, ["fT0", "fT1", "fT2"], probs)
                elif step == "fx_O":
                    fx_O(l)
                elif step == "rw_lora":
                    rw_lora(l)
                elif step == "rw_tr":
                    rw_tr(l)
                elif step == "rw_prod":
                    rw_prod(l)
                elif step == "rw_x0":
                    rw_x0(l)
                elif step[:4] == "rw_m" and step[4:].isdigit():
                    rw_merge(l, int(step[4]))
                elif step == "rw_app":
                    rw_app(l)
                elif step == "rw_state":
                    rw_state(l)
                elif step == "rw_Y":
                    rw_Y(l)
                elif step == "rw_gn":
                    rw_gn(l)

        def dense():
            drained(pe, 0, "norm_ffn1")
            for g in range(DENSE_GROUPS):
                base = 0 if g % 2 else 4
                blocks = range(4 * g, min(4 * g + 4, DENSE_BLOCKS))
                for w in range(2):
                    n0 = FIRST_DENSE + 4 * g + 2 * w
                    for b in blocks:
                        if w == 0 and b >= 8:
                            pe.wait_ge(sem("dense_mul"), b - 7)
                        for k in range(KC):
                            if b == 0 and w == 0 and k == 4:
                                drained(pe, 0, "norm_ffn3")
                            if b == blocks[0] and k % 4 == 0:
                                is_split(n0 + k // 4)
                            c = (b - 4 * g) * P
                            first, last = parts(pb[base + b % 4][:, w * T:w * T + T], wparts(n0 + k // 4, k % 4, 512, slice(c, c + P)),
                                                (hT_h[:, k, :], hT_l[:, k, :]), k == 0, k == KC - 1)
                            if b == blocks[-1] and k == 4:
                                first.then_inc(sem("piece_used"), 1)
                        if w == 1:
                            last.then_inc(sem("dense_up"), 1)
                    pend[0] = 1
            for c in range(DENSE_BLOCKS // 2):
                n = FIRST_DENSE + 4 * DENSE_GROUPS + c
                is_split(n)
                if c == 0:
                    pe.wait_ge(sem("dense_mul"), 4 * (DENSE_GROUPS - 1))
                pe.wait_ge(sem("dense_act"), 2 * c + 2)
                for tt in range(TT):
                    for k in range(2):
                        b = 2 * c + k
                        for half in range(2):
                            _, last = parts(pb[4 + 2 * tt + half][:, :], (denseT_h[:, b, tsl(tt)], denseT_l[:, b, tsl(tt)]),
                                            wparts(n, k, D, slice(half * 512, half * 512 + 512)), b == 0, b == DENSE_BLOCKS - 1)
                    if c == DENSE_BLOCKS // 2 - 1:
                        last.then_inc(sem("dense_down"), 1)
                pend[0] = 1

        pe.wait_ge(sem("const_ready"), 1)
        pe.wait_ge(sem("small0_in"), 16)
        mixer(0)
        dense()
        pe.wait_ge(sem("small1_in"), 16)
        mixer(1)

        def route():
            drained(pe, 1, "norm_ffn1")
            drained(pe, 1, "norm_ffn3")
            for tt in range(TT):
                for k in range(KC):
                    ins = mm(pb[4][:, tt * 8:tt * 8 + 8], hT[:, k, tsl(tt)], s_(1, "router")[:, k * 8:k * 8 + 8], start=k == 0, stop=k == KC - 1)
            ins.then_inc(sem("router_logits"), 1)
            pe.wait_ge(sem("took_done"), 1)
            E1 = EXPERTS + 1
            mm(pb[5][:, 0:E1], c_("before"), took[:, 0, :], start=True, stop=True)
            mm(pb[5][:, E1:2 * E1], c_("ones")[:, 0:P], took[:, 0, :], start=True, stop=False)
            mm(pb[5][:, E1:2 * E1], c_("before"), took[:, 1, :], start=False, stop=True)
            mm(pb[5][:, 2 * E1:3 * E1], c_("ones")[:, 0:P], took[:, 0, :], start=True, stop=False)
            mm(pb[5][:, 2 * E1:3 * E1], c_("ones")[:, 0:P], took[:, 1, :], start=False, stop=True).then_inc(sem("ranks"), 1)

        def gather(tag):
            for b in range(2):
                for j in range(4):
                    k = 4 * b + j
                    for tt in range(TT):
                        ins = mm(pb[2 + b][:, j * P:j * P + P], xn[:, tt, k * P:k * P + P], pick[:, tt, :], start=tt == 0, stop=tt == 1)
                ins.then_inc(sem(tag + "gathered"), 1)
            for tt in range(TT):
                ins = nc.tensor.transpose(pb[7][:, tsl(tt)], pickg[:, tt, :], ident)
            ins.then_inc(sem(tag + "gathered"), 1)

        def experts(tag, first):
            pe.wait_ge(sem(tag + "ready"), 1)
            pe.wait_ge(sem(tag + "pick"), 1)
            gather(tag)
            for half in range(2):
                ins = mm(pb[4 + half][:, :], yexp[:, 0:P], yexp[:, 0:512], start=True, stop=True)
            ins.then_inc(sem(tag + "down"), 1)
            with pe.Fori(0, EXPERTS) as e:
                def up(g):
                    for w in range(2):
                        n0 = first + 4 * g + 2 * w
                        b = 2 * (g % 2) + w
                        if w == 0 and g >= 2:
                            pe.wait_ge(sem(tag + "act"), e * EXP_GROUPS + (g - 1))
                        for k in range(KC):
                            if k % 4 == 0:
                                pe.wait_ge(sem("split_lo"), e * EXP_PIECES + SPLIT_NO[n0 + k // 4])
                            a, last = parts(pb[b][:, :], (hsel_h[:, k, :], hsel_l[:, k, :]),
                                            wparts(n0 + k // 4, k % 4, 512, slice(0, 512)), k == 0, k == KC - 1)
                            if k == 4:
                                a.then_inc(sem("piece_used"), 1)
                        if w == 1:
                            last.then_inc(sem(tag + "up"), 1)
                        pend[0] = 1

                def turn(g):
                    pe.wait_ge(sem(tag + "act"), e * EXP_GROUPS + (g + 1))
                    if g >= 1:
                        pe.wait_ge(sem(tag + "actT"), e * EXP_GROUPS + g)
                    for j in range(4):
                        ins = nc.tensor.transpose(pb[6][:, j * P:j * P + P], act[:, g % 2, j * P:j * P + P], ident)
                    ins.then_inc(sem(tag + "turned"), 1)

                def scatter(tt):
                    for half in range(2):
                        if tt == 1:
                            pe.wait_ge(sem(tag + "added"), e * 4 + (half + 1))
                        mm(pb[4 + half][:, :], pickT[:, tsl(tt)], yexp[:, half * 512:half * 512 + 512], start=True, stop=True)\
                            .then_inc(sem(tag + "scattered"), 1)

                pend[0] = 1
                pe.wait_ge(sem(tag + "hsel"), e + 1)
                up(0)
                pe.wait_ge(sem(tag + "yexp"), e + 1)
                scatter(0)
                up(1)
                turn(0)
                scatter(1)
                for g in range(2, EXP_GROUPS):
                    up(g)
                    turn(g - 1)
                pe.wait_ge(sem(tag + "pick"), e + 2)
                pe.wait_ge(sem(tag + "pickT"), e + 1)
                gather(tag)
                turn(EXP_GROUPS - 1)
                pe.wait_ge(sem(tag + "added"), e * 4 + 4)
                for c in range(EXP_BLOCKS // 2):
                    n = first + 4 * EXP_GROUPS + c
                    pe.wait_ge(sem("split_lo"), e * EXP_PIECES + SPLIT_NO[n])
                    if c % 2 == 0:
                        pe.wait_ge(sem(tag + "actT"), e * EXP_GROUPS + (c // 2 + 1))
                    for k in range(2):
                        b = 2 * c + k
                        for half in range(2):
                            _, last = parts(pb[4 + half][:, :], (actT_h[:, b, :], actT_l[:, b, :]),
                                            wparts(n, k, D, slice(half * 512, half * 512 + 512)), b == 0, b == EXP_BLOCKS - 1)
                    pend[0] = 1
                last.then_inc(sem(tag + "down"), 1)
            pend[0] = 0
            pe.wait_ge(sem(tag + "yexp"), EXPERTS + 1)
            for tt in range(TT):
                for half in range(2):
                    if tt == 1:
                        pe.wait_ge(sem(tag + "added"), EXPERTS * 4 + half + 1)
                    mm(pb[4 + half][:, :], pickT[:, tsl(tt)], yexp[:, half * 512:half * 512 + 512], start=True, stop=True)\
                        .then_inc(sem(tag + "scattered"), 1)

        route()
        experts("main_", FIRST_EXPERT)
        pe.wait_ge(sem("over_known"), 1)
        more = pe.value_load(over_i[0:1, 0:1], min_val=0, max_val=1)
        with pe.If(more > 0):
            pend[0] = 1
            experts("over_", PIECES)

    @block.scalar
    def _(act_e):
        a = nc.scalar.activation
        done = [0]

        def link(ins):
            done[0] += 1
            ins.then_inc(sem("act_chain"), 1)
            act_e.wait_ge(sem("act_chain"), done[0])

        def split_hi(n, used=None, e=None):
            act_e.wait_ge(piece_in(n), 16 * RING_USES[n] if e is None else e * (16 * EXP_PIECES // RING_EXPERT) + 16 * RING_USES[n])
            if used is not None:
                act_e.wait_ge(sem("piece_used"), used + 1 if e is None else e * EXP_PIECES + (used + 1))
            a(high(n), raw(n), ACT.Copy).then_inc(sem("split_hi"), 1)

        def norm_stats(l, j):
            for tt in range(TT):
                if j % 2:
                    drained(act_e, l, "out1" + "ab"[tt])
                elif j:
                    act_e.wait_ge(sem("x_fed"), tt + 1)
                link(a(hT_flat[tt], x[:, tt, :], ACT.Square, accum_out=stat[:, tt:tt + 1]))
                if j == 0 and tt == 0:
                    act_e.wait_ge(sem("const_in"), 16)
                a(stat[:, 2 + tt:3 + tt], stat[:, tt:tt + 1], ACT.Sqrt, bias=c_("eps"), scale=1.0 / D).then_inc(sem("norm_std"), 1)

        def evac_hT_high(l, step, gains):
            for b in range(4):
                full(act_e, l, f"{step}{b}")
                for kk in range(2):
                    k = 2 * b + kk
                    a(hT_h[:, k, :], pb[b][:, kk * T:kk * T + T], ACT.Copy, scale=gains[:, k:k + 1] if gains is not None else 1.0)\
                        .then_inc(sem("hT_high"), 1)

        def evac_hT(l, step, gains):
            for b in range(2):
                full(act_e, l, f"{step}{b}")
                for kk in range(2):
                    k = 2 * b + kk
                    ins = a(hT[:, k, :], pb[b][:, kk * T:kk * T + T], ACT.Copy, scale=gains[:, k:k + 1] if gains is not None else 1.0)
                ins.then_inc(freed(f"{step}{b}"), 1)

        def softmax_exp(l, eps, max_sem, nmax, sums):
            for i, ep in enumerate(eps):
                tt = i // 2
                act_e.wait_ge(sem(max_sem), 4 * l + i + 1)
                for j in range(2):
                    h = 2 * (i % 2) + j if ep[0] == "d" else i % 2 + 2 * j
                    ns = P * (tt + 1)
                    col = 4 * tt + h
                    ins = a(probs[:, tt, h, 0:ns], bank2(ep)[:, j, 0:ns], ACT.Exp, bias=stat[:, nmax + col:nmax + col + 1],
                            accum_out=stat[:, sums + col:sums + col + 1])
                ins.then_inc(freed(ep), 1)

        def evac_probsT(l, eps):
            for i, ep in enumerate(eps):
                full(act_e, l, ep)
                a(probsT[:, 4 * i:4 * i + 4, :].rearrange("p a b -> p (a b)"), bank(ep)[:, :], ACT.Copy).then_inc(freed(ep), 1)

        def step_act(l, s):
            if s == "norm_mix":
                norm_stats(l, 2 * l)
                split_hi(FIRST_OF[l, SPLIT_GROUPS[0]])
                act_e.wait_ge(sem(f"small{l}_in"), 16)
                evac_hT_high(l, s, s_(l, "g_mix"))
                split_hi(FIRST_OF[l, SPLIT_GROUPS[0]] + 1)
            elif s == "norm_ffn":
                norm_stats(l, 2 * l + 1)
                if l == 0:
                    split_hi(FIRST_DENSE + 1)
                    evac_hT_high(l, s, s_(l, "g_ffn"))
                else:
                    evac_hT(l, s, s_(l, "g_ffn"))
            elif s == "mrg_tr":
                evac_hT_high(l, s, None)
            elif s == "z_ml":
                full(act_e, l, s + "a")
                a(conv_in[:, :, 3:], bank2(s + "a"), ACT.Copy).then_inc(freed(s + "a"), 1)
            elif s == "z_lat":
                full(act_e, l, s + "a")
                a(z_lat[:, 0, :], bank(s + "a")[:, :], ACT.Copy).then_inc(freed(s + "a"), 1)
            elif s == "z_mvo":
                full(act_e, l, s + "a")
                a(z_mvo[:, 0, :], bank(s + "a")[:, :], ACT.Copy).then_inc(freed(s + "a"), 1)
            elif s == "z_fox":
                full(act_e, l, s + "a")
                a(foxq, bank2(s + "a"), ACT.Copy, scale=64 ** -0.5).then_inc(freed(s + "a"), 1)
            elif s == "z_rw0":
                full(act_e, l, s + "a")
                a(Zr[:, 0:2, 1:], bank2(s + "a"), ACT.Copy).then_inc(freed(s + "a"), 1)
            elif s == "z_rw1":
                full(act_e, l, s + "a")
                a(Zr[:, 4:6, 1:], bank2(s + "a"), ACT.Copy).then_inc(freed(s + "a"), 1)
            elif s[:4] == "gate":
                b, half = int(s[4]), int(s[5])
                if b >= 2:
                    drained(act_e, l, f"br{b - 2}1b")
                    drained(act_e, l, f"br{b - 2}1a")
                for tt, ep in ((0, s + "a"), (1, s + "b")):
                    full(act_e, l, ep)
                    a(gates[:, b % 2, tt, half * 512:half * 512 + 512], bank(ep)[:, :], ACT.Sigmoid).then_inc(freed(ep), 1)
            elif s == "ds_norm":
                act_e.wait_ge(sem("lat_ss"), l + 1)
                a(stat[:, 16:20], stat[:, 10:14], ACT.Sqrt, bias=c_("eps"), scale=1.0 / P)
                a(stat[:, 20:22], stat[:, 14:16], ACT.Sqrt, bias=c_("eps"), scale=1.0 / 32).then_inc(sem("lat_std"), 1)
            elif s == "ds_tr":
                full(act_e, l, "dT")
                a(latT, bank2("dT"), ACT.Copy).then_inc(freed("dT"), 1)
            elif s == "ds_q":
                for i in range(2):
                    full(act_e, l, f"dQ{i}")
                    a(dsq[:, 2 * i:2 * i + 2, :], bank2(f"dQ{i}"), ACT.Copy, scale=P ** -0.5).then_inc(freed(f"dQ{i}"), 1)
            elif s[:6] == "ds_dot":
                tt = int(s[6])
                if tt == 1:
                    act_e.wait_ge(sem("scored"), 2 * l + 1)
                for b in range(4):
                    ep = f"dD{tt}_{b}"
                    full(act_e, l, ep)
                    a(relu[:, 2 * b:2 * b + 2, 0:P * (tt + 1)], bank2(ep)[:, :, 0:P * (tt + 1)], ACT.Relu).then_inc(freed(ep), 1)
            elif s == "ds_L":
                full(act_e, l, "fT2")
                softmax_exp(l, [f"dL{i}" for i in range(4)], "ds_max", 40, 48)
            elif s == "ds_T":
                full(act_e, l, "mN")
                evac_probsT(l, ["dP0", "dP1", "dP2"])
            elif s == "ds_O":
                for i in range(2):
                    full(act_e, l, f"dO{i}")
                    a(dsO[:, 2 * i:2 * i + 2, :], bank2(f"dO{i}"), ACT.Copy).then_inc(freed(f"dO{i}"), 1)
            elif s == "ml_in":
                act_e.wait_ge(sem("conv_sum"), l + 1)
                a(conv_s, conv, ACT.Sigmoid).then_inc(sem("conv_sig"), 1)
            elif s == "ml_gate":
                drained(act_e, l, "z_mlb")
                a(g_tmp[0:64, :], g_pre[0:64, :], ACT.Tanh, scale=1.0 / 15).then_inc(sem("gates_tanh"), 1)
                act_e.wait_ge(sem("gates_abs"), l + 1)
                link(a(g_exp[0:96, :], g_tmp[0:96, :], ACT.Exp, scale=-1.0))
                a(g_tmp[0:96, :], g_exp[0:96, :], ACT.Ln, bias=const[0:96, CONST["one"][0]:CONST["one"][0] + 1]).then_inc(sem("gates_ln"), 1)
            elif s == "ml_D":
                for i in range(3):
                    tt = 0 if i == 0 else 1
                    ns = P * (tt + 1)
                    act_e.wait_ge(sem("ml_max"), 3 * l + i + 1)
                    for j in range(512 // ns):
                        h = j if i == 0 else 2 * (i - 1) + j
                        col = 80 + 4 * tt + h
                        ins = a(probs[:, tt, h, 0:ns], bank(f"mD{i}")[:, j * ns:j * ns + ns], ACT.Exp, bias=stat[:, col:col + 1])
                    ins.then_inc(freed(f"mD{i}"), 1)
                a(stat[:, 88:96], stat[:, 80:88], ACT.Exp).then_inc(sem("ml_floor"), 1)
            elif s == "ml_T":
                full(act_e, l, "fO")
                evac_probsT(l, ["mT0", "mT1", "mT2"])
                a(osig, z_mvo[:, :, 256:512], ACT.Sigmoid).then_inc(sem("ml_osig"), 1)
            elif s == "ml_N":
                act_e.wait_ge(sem("ml_ss"), l + 1)
                a(stat[:, 120:128], stat[:, 112:120], ACT.Sqrt, bias=c_("eps"), scale=1.0 / 64).then_inc(sem("ml_std"), 1)
            elif s == "fx_L":
                drained(act_e, l, "mQ3")
                softmax_exp(l, [f"fL{i}" for i in range(4)], "fx_max", 24, 32)
            elif s == "fx_T":
                evac_probsT(l, ["fT0", "fT1", "fT2"])
            elif s == "rw_mix":
                act_e.wait_ge(sem("rw_mixed"), l + 1)
                a(tanh_w[0:64, :], Zm[0:64, 6, :], ACT.Tanh)
                a(sig_g, Zm[:, 7, :], ACT.Sigmoid).then_inc(sem("rw_lora_in"), 1)
            elif s == "rw_lora":
                drained(act_e, l, "rKK")
                a(kkn_std, kkn_max, ACT.Sqrt).then_inc(sem("rw_kstd"), 1)
                full(act_e, l, "rW")
                for blk in range(2):
                    ins = a(lw[:, blk, :], bank2("rW")[:, blk, :], ACT.Sigmoid, bias=s_(l, "w0")[:, blk:blk + 1])
                ins.then_inc(freed("rW"), 1)
                full(act_e, l, "rA")
                for blk in range(2):
                    ins = a(sa[:, blk, :], bank2("rA")[:, blk, :], ACT.Sigmoid, bias=s_(l, "a0")[:, blk:blk + 1])
                ins.then_inc(freed("rA"), 1)
                full(act_e, l, "rG")
                a(gout, bank2("rG"), ACT.Copy).then_inc(freed("rG"), 1)
            elif s == "rw_fm":
                act_e.wait_ge(sem("rw_cum"), l + 1)
                a(Wf, cum, ACT.Exp)
                link(a(cml, cml, ACT.Exp))
                a(cum, cum, ACT.Exp, scale=-1.0).then_inc(sem("rw_exp"), 1)
            elif s == "rw_tr":
                for ep, dst in (("rtV", Vtm), ("rtA", Atm), ("rtB", Btm), ("rtK", Ktm)):
                    full(act_e, l, ep)
                    a(dst.rearrange("p a b -> p (a b)"), bank(ep)[:, :], ACT.Copy).then_inc(freed(ep), 1)
            elif s == "rw_x0":
                for i in range(2):
                    full(act_e, l, f"rX0_{i}")
                    a(X[:, 4 * i:4 * i + 4, :].rearrange("p a b -> p (a b)"), bank(f"rX0_{i}")[:, :], ACT.Copy).then_inc(freed(f"rX0_{i}"), 1)
            elif s[:4] == "rw_m" and s[4:].isdigit():
                j = int(s[4])
                for i in range(2):
                    full(act_e, l, f"rZ{j}_{i}")
                    a(Z[:, 4 * i:4 * i + 4, :].rearrange("p a b -> p (a b)"), bank(f"rZ{j}_{i}")[:, :], ACT.Copy).then_inc(freed(f"rZ{j}_{i}"), 1)
            elif s == "rw_app":
                full(act_e, l, "rLkV")
                a(ALV[:, :, 64:128], bank("rLkV")[:, :].rearrange("p (q v) -> p q v", q=8), ACT.Copy).then_inc(freed("rLkV"), 1)
                for i in range(2):
                    full(act_e, l, f"rXA{i}")
                    a(XALV[:, 4 * i:4 * i + 4, :].rearrange("p a b -> p (a b)"), bank(f"rXA{i}")[:, :], ACT.Copy).then_inc(freed(f"rXA{i}"), 1)
            elif s == "rw_Y":
                full(act_e, l, "rY")
                a(Ys.rearrange("p a b -> p (a b)"), bank("rY")[:, :], ACT.Copy).then_inc(freed("rY"), 1)
            elif s == "rw_gn":
                act_e.wait_ge(sem("rw_yc"), l + 1)
                a(Yq, Yc, ACT.Square).then_inc(sem("rw_ysq"), 1)
                full(act_e, l, "rVar")
                a(lw.rearrange("p a b -> p (a b)"), bank("rVar")[:, :], ACT.Sqrt, bias=c_("gn_eps")).then_inc(freed("rVar"), 1)

        hT_flat = [hT[:, 4 * tt:4 * tt + 4, :].rearrange("p a b -> p (a b)") for tt in range(TT)]
        kkn_std, kkn_max = cum, cml

        act_e.wait_ge(sem("x_in"), 16)
        for l in range(LAYERS):
            for s in SCHEDULE:
                following = next_split(l, s) if s in SPLIT_GROUPS else None
                if following is not None:
                    split_hi(following, FIRST_OF[l, s])
                step_act(l, s)
                for group_, at in SPLIT_LATER.items():
                    if s == at:
                        split_hi(next_split(l, group_) + 1)
                if following not in (None, FIRST_DENSE) and s not in SPLIT_LATER:
                    full(act_e, l, s + "b")
                    split_hi(following + 1)
            if l == 0:
                def dense_silu(g):
                    for b in range(4 * g, min(4 * g + 4, DENSE_BLOCKS)):
                        act_e.wait_ge(sem("dense_up"), b + 1)
                        if b >= 4:
                            act_e.wait_ge(sem("dense_act"), b - 3)
                        a(dsil[:, b % 4, :], pb[(0 if g % 2 else 4) + b % 4][:, 0:T], ACT.Silu).then_inc(sem("dense_silu"), 1)

                def dense_high(g):
                    for b in range(4 * g, min(4 * g + 4, DENSE_BLOCKS)):
                        act_e.wait_ge(sem("dense_mul"), b + 1)
                        a(denseT_h[:, b, :], dsil[:, b % 4, :], ACT.Copy).then_inc(sem("dense_high"), 1)

                for n in range(DENSE_PIECES):
                    if n >= HIGH_MIX:
                        split_hi(FIRST_DENSE + n, FIRST_DENSE + n - HIGH_DENSE if n >= HIGH_DENSE else None)
                    g = n // 4
                    if 1 <= g <= DENSE_GROUPS and n % 4 == 1:
                        dense_silu(g - 1)
                    if 1 <= g <= DENSE_GROUPS and n % 4 == 2:
                        dense_high(g - 1)

        act_e.wait_ge(sem("top2_gap"), 1)
        a(rtmp[:, :, 34:35], rtmp[:, :, 33:34], ACT.Exp).then_inc(sem("top2_exp"), 1)

        def experts_act(tag, first):
            act_e.wait_ge(sem(tag + "ready"), 1)
            g_ffn = s_(1, "g_ffn")

            def hsel_high(count):
                for b in range(2):
                    act_e.wait_ge(sem(tag + "gathered"), count(b + 1))
                    for j in range(4):
                        k = 4 * b + j
                        a(hsel_h[:, k, :], pb[2 + b][:, j * P:j * P + P], ACT.Copy, scale=g_ffn[:, k:k + 1]).then_inc(sem(tag + "hsel_high"), 1)

            with act_e.Fori(0, EXPERTS) as e:
                def hi(j):
                    split_hi(first + j, first + j - HIGH_EXPERT, e)

                def silu(g):
                    act_e.wait_ge(sem(tag + "up"), e * EXP_GROUPS + (g + 1))
                    if g >= 2:
                        act_e.wait_ge(sem(tag + "act"), e * EXP_GROUPS + (g - 1))
                    a(sil[:, g % 2, :], pb[2 * (g % 2)][:, :], ACT.Silu).then_inc(sem(tag + "silu"), 1)

                def actT_high(g):
                    act_e.wait_ge(sem(tag + "turned"), e * EXP_GROUPS + (g + 1))
                    a(actT_h[:, 4 * g:4 * g + 4, :].rearrange("p a b -> p (a b)"), pb[6][:, :], ACT.Copy).then_inc(sem(tag + "actT_high"), 1)

                for g in range(EXP_GROUPS + 1):
                    hi(4 * g)
                    if g == 0:
                        hsel_high(lambda n: e * 3 + n)
                    hi(4 * g + 1)
                    if g >= 1:
                        silu(g - 1)
                    if g >= 2:
                        actT_high(g - 2)
                    if g == 2:
                        act_e.wait_ge(sem(tag + "scattered"), e * 4 + 4)
                        act_e.wait_ge(sem(tag + "gathered"), e * 3 + 3)
                        a(pickT, pb[7][:, 0:T], ACT.Copy).then_inc(sem(tag + "pickT"), 1)
                    if g < EXP_GROUPS:
                        hi(4 * g + 2)
                        hi(4 * g + 3)
                actT_high(EXP_GROUPS - 1)
                for j in range(4 * EXP_GROUPS + 2, EXP_PIECES):
                    hi(j)

        experts_act("main_", FIRST_EXPERT)
        act_e.wait_ge(sem("over_known"), 1)
        more = act_e.value_load(over_i[0:1, 0:1], min_val=0, max_val=1)
        with act_e.If(more > 0):
            experts_act("over_", PIECES)
        for tt in range(TT):
            act_e.wait_ge(sem("x_fed"), TT + tt + 1)
            link(a(hT_flat[tt], x[:, tt, :], ACT.Square, accum_out=stat[:, tt:tt + 1]))
            a(stat[:, 2 + tt:3 + tt], stat[:, tt:tt + 1], ACT.Sqrt, bias=c_("eps"), scale=1.0 / D).then_inc(sem("norm_std"), 1)

    @block.vector
    def _(ve):
        v = nc.vector
        done = [0]

        def link(ins):
            done[0] += 1
            ins.then_inc(sem("vec_chain"), 1)
            ve.wait_ge(sem("vec_chain"), done[0])

        def tt_(o, i0, i1, op):
            return v.tensor_tensor(o, i0, i1, op)

        def ts(o, i0, s1, op0, s2=None, op1=ALU.bypass):
            return v.tensor_scalar(o, i0, s1, s2, op0, op1)

        def stt(o, i0, s, i1, op0, op1, **k):
            return v.scalar_tensor_tensor(out=o, in0=i0, scalar=s, in1=i1, op0=op0, op1=op1, **k)

        def split_lo(n, e=None):
            ve.wait_ge(sem("split_hi"), SPLIT_NO[n] if e is None else e * EXP_PIECES + SPLIT_NO[n])
            tt_(low(n), raw(n), high(n).bitcast(F32), ALU.subtract).then_inc(sem("split_lo"), 1)

        def norm_rows(j):
            for tt in range(TT):
                ve.wait_ge(sem("norm_std"), 2 * j + tt + 1)
                link(v.reciprocal(stat[:, 4 + tt:5 + tt], stat[:, 2 + tt:3 + tt]))
                ts(xn[:, tt, :], x[:, tt, :], stat[:, 4 + tt:5 + tt], ALU.mult).then_inc(sem("normed"), 1)

        def evac_hT_low(l, step, gains, before):
            for b in range(4):
                for kk in range(2):
                    k = 2 * b + kk
                    if kk == 0:
                        ve.wait_ge(sem("hT_high"), before + k + 2)
                    hi = hT_h[:, k, :].bitcast(F32)
                    if gains is None:
                        ins = tt_(hT_l[:, k, :], pb[b][:, kk * T:kk * T + T], hi, ALU.subtract)
                    else:
                        ins = stt(hT_l[:, k, :], pb[b][:, kk * T:kk * T + T], gains[:, k:k + 1], hi, ALU.mult, ALU.subtract)
                ins.then_inc(freed(f"{step}{b}"), 1)

        def evac_hT(l, step, gains):
            for b in range(2, 4):
                full(ve, l, f"{step}{b}")
                for kk in range(2):
                    k = 2 * b + kk
                    if gains is None:
                        ins = v.tensor_copy(hT[:, k, :], pb[b][:, kk * T:kk * T + T])
                    else:
                        ins = ts(hT[:, k, :], pb[b][:, kk * T:kk * T + T], gains[:, k:k + 1], ALU.mult)
                ins.then_inc(freed(f"{step}{b}"), 1)

        def row_max(l, eps, max_sem, nmax):
            for i, ep in enumerate(eps):
                tt = i // 2
                full(ve, l, ep)
                first = 2 * (i % 2) if ep[0] == "d" else i % 2
                step = 1 if ep[0] == "d" else 2
                at = nmax + 4 * tt + first
                v.reduce_max(stat[:, at:at + step + 1:step], bank2(ep)[:, :, 0:P * (tt + 1)], AX.X, negate=True).then_inc(sem(max_sem), 1)

        def normalise(l, eps, sums, out_sem):
            for ep in eps:
                drained(ve, l, ep)
            link(v.reciprocal(stat[:, sums:sums + 8], stat[:, sums:sums + 8]))
            for tt in range(TT):
                ns = P * (tt + 1)
                ins = tt_(probs[:, tt, :, 0:ns], probs[:, tt, :, 0:ns],
                          stat[:, sums + 4 * tt:sums + 4 * tt + 4].unsqueeze(2).broadcast_to([P, 4, ns]), ALU.mult)
            ins.then_inc(sem(out_sem), 1)

        def step_vec(l, s):
            if s == "norm_mix":
                norm_rows(2 * l)
                split_lo(FIRST_OF[l, SPLIT_GROUPS[0]])
                ve.wait_ge(sem(f"small{l}_in"), 16)
                evac_hT_low(l, s, s_(l, "g_mix"), 3 * KC * l)
                split_lo(FIRST_OF[l, SPLIT_GROUPS[0]] + 1)
                v.memset(conv_in[:, :, 0:3], 0.0)
                v.memset(Zr[:, :, 0:1], 0.0)
            elif s == "norm_ffn":
                norm_rows(2 * l + 1)
                if l == 0:
                    split_lo(FIRST_DENSE + 1)
                    evac_hT_low(l, s, s_(l, "g_ffn"), 2 * KC)
                else:
                    evac_hT(l, s, s_(l, "g_ffn"))
            elif s == "mrg_tr":
                evac_hT_low(l, s, None, (3 * l + 1) * KC)
            elif s == "z_ml":
                full(ve, l, s + "b")
                link(v.tensor_copy(z_idx, bank(s + "b")[:, T:T + 80].rearrange("p (a b) -> p a b", a=TT)))
                ts(g_pre[0:96, :], bank(s + "b")[0:96, 0:T], s_(l, "gate_b")[0:96, :], ALU.add).then_inc(freed(s + "b"), 1)
            elif s == "z_lat":
                full(ve, l, s + "b")
                v.tensor_copy(z_lat[:, 1, :], bank(s + "b")[:, :]).then_inc(freed(s + "b"), 1)
            elif s == "z_mvo":
                full(ve, l, s + "b")
                v.tensor_copy(z_mvo[:, 1, :], bank(s + "b")[:, :]).then_inc(freed(s + "b"), 1)
            elif s == "z_fox":
                full(ve, l, s + "b")
                v.tensor_copy(foxk, bank2(s + "b")).then_inc(freed(s + "b"), 1)
            elif s == "z_rw0":
                full(ve, l, s + "b")
                v.tensor_copy(Zr[:, 2:4, 1:], bank2(s + "b")).then_inc(freed(s + "b"), 1)
            elif s == "z_rw1":
                full(ve, l, s + "b")
                v.tensor_copy(Zr[:, 6:8, 1:], bank2(s + "b")).then_inc(freed(s + "b"), 1)
            elif s == "ml_in":
                drained(ve, l, "z_mla")
                cw = s_(l, "conv_w")
                for j in range(4):
                    for blk in range(2):
                        w = cw[:, 2 * j + blk:2 * j + blk + 1]
                        if j == 0:
                            ins = ts(conv[:, blk, :], conv_in[:, blk, 0:T], w, ALU.mult, s_(l, "conv_b")[:, blk:blk + 1], ALU.add)
                        else:
                            ins = stt(conv[:, blk, :], conv_in[:, blk, j:j + T], w, conv[:, blk, :], ALU.mult, ALU.add)
                    if j < 3:
                        link(ins)
                ins.then_inc(sem("conv_sum"), 1)
                ve.wait_ge(sem("conv_sig"), l + 1)
                stt(conv[:, 0, :], conv[:, 0, :], 32 ** -0.5, conv_s[:, 0, :], ALU.mult, ALU.mult)
                tt_(conv[:, 1, :], conv[:, 1, :], conv_s[:, 1, :], ALU.mult).then_inc(sem("conv_done"), 1)
            elif s == "ds_norm":
                drained(ve, l, "z_lata")
                drained(ve, l, "z_latb")
                ve.wait_ge(sem(f"row{l}_in"), 16)
                lat = z_lat[:, :, 0:256].rearrange("p t (w c) -> p t w c", w=2)
                tt_(lat_sq, lat, lat, ALU.mult)
                link(tt_(ki_sq, z_idx[:, :, 0:32], z_idx[:, :, 0:32], ALU.mult))
                v.reduce_sum(stat[:, 10:14].rearrange("p (a b) -> p a b", a=2), lat_sq, AX.X)
                v.reduce_sum(stat[:, 14:16], ki_sq, AX.X).then_inc(sem("lat_ss"), 1)
                ve.wait_ge(sem("lat_std"), l + 1)
                link(v.reciprocal(stat[:, 16:22], stat[:, 16:22]))
                for tt in range(TT):
                    for w, g in ((0, "g_cq"), (1, "g_ckv")):
                        stt(lat_n[:, tt, w, :], z_lat[:, tt, w * P:w * P + P], stat[:, 16 + 2 * tt + w:17 + 2 * tt + w],
                            r_(l, g), ALU.mult, ALU.mult)
                    ins = stt(ki4[:, tt, :, :], z_idx[:, tt, 0:32].unsqueeze(1).broadcast_to([P, 4, 32]), stat[:, 20 + tt:21 + tt],
                              r_(l, "g_kidx").unsqueeze(1).broadcast_to([P, 4, 32]), ALU.mult, ALU.mult)
                ins.then_inc(sem("lat_normed"), 1)
                link(ts(z_idx[:, :, 32:40], z_idx[:, :, 32:40], 8 ** -0.5 * 32 ** -0.5, ALU.mult))
            elif s == "ds_tr":
                full(ve, l, "dTk")
                v.tensor_copy(kiT, bank("dTk")[:, 0:T]).then_inc(freed("dTk"), 1)
            elif s == "ds_q":
                full(ve, l, "dQi")
                v.tensor_copy(qiT, bank2("dQi")).then_inc(freed("dQi"), 1)
            elif s == "ml_gate":
                drained(ve, l, "z_mlb")
                ve.wait_ge(sem("gates_tanh"), l + 1)
                link(ts(g_pre[0:64, :], g_tmp[0:64, :], 15.0, ALU.mult))
                stt(g_tmp[0:96, :], g_pre[0:96, :], -1.0, g_pre[0:96, :], ALU.mult, ALU.max).then_inc(sem("gates_abs"), 1)
                ve.wait_ge(sem("gates_ln"), l + 1)
                link(stt(g_exp[0:96, :], g_pre[0:96, :], 0.0, g_tmp[0:96, :], ALU.min, ALU.subtract))
                link(v.tensor_tensor_scan(g_cum[0:96, :], c_("ones")[0:96, :], g_exp[0:96, :], 0.0, ALU.mult, ALU.add))
                is_f = const[0:96, CONST["is_f"][0]:CONST["is_f"][0] + 1]
                is_i = const[0:96, CONST["is_i"][0]:CONST["is_i"][0] + 1]
                ts(g_pos[0:96, :], g_cum[0:96, :], is_f, ALU.mult)
                link(ts(g_tmp[0:96, :], g_pre[0:96, :], is_i, ALU.mult))
                v.tensor_copy(g_pos_h[0:96, :], g_pos[0:96, :])
                link(stt(g_key[0:96, :], g_pos[0:96, :], -1.0, g_tmp[0:96, :], ALU.mult, ALU.add))
                link(v.tensor_copy(g_key_h[0:96, :], g_key[0:96, :]))
                tt_(g_pos_l[0:96, :], g_pos[0:96, :], g_pos_h[0:96, :].bitcast(F32), ALU.subtract)
                tt_(g_key_l[0:96, :], g_key[0:96, :], g_key_h[0:96, :].bitcast(F32), ALU.subtract).then_inc(sem("gate_sums"), 1)
            elif s[:6] == "ds_dot":
                tt = int(s[6])
                ns = P * (tt + 1)
                for h in range(8):
                    b, j = h % 4, h // 4
                    if h < 4:
                        drained(ve, l, f"dD{tt}_{b}")
                    r = relu[:, 2 * b + j, 0:ns]
                    w = z_idx[:, tt, 32 + h:33 + h]
                    if h == 0:
                        link(ts(score[:, tt, 0:ns], r, w, ALU.mult))
                    else:
                        ins = stt(score[:, tt, 0:ns], r, w, score[:, tt, 0:ns], ALU.mult, ALU.add)
                        if h == 7:
                            ins.then_inc(sem("scored"), 1)
                        else:
                            link(ins)
                ve.wait_ge(sem("scored"), 2 * l + tt + 1)
                link(tt_(score[:, tt, tsl(tt)], score[:, tt, tsl(tt)], c_("negtri"), ALU.add))
            elif s == "ds_topk":
                for r in range(TOPK // 8):
                    for tt in range(TT):
                        ins = v.max(best[:, tt, :], score[:, tt, 0:P * (tt + 1)])
                    link(ins)
                    for tt in range(TT):
                        ins = v.match_replace(score[:, tt, 0:P * (tt + 1)], best[:, tt, :], score[:, tt, 0:P * (tt + 1)], TAKEN)
                    link(ins)
                for tt in range(TT):
                    ns = P * (tt + 1)
                    ins = ts(score_r[:, tt, 0:ns], score[:, tt, 0:ns], TAKEN, ALU.not_equal, NEG, ALU.mult)
                link(ins)
                for tt in range(TT):
                    ins = tt_(score_r[:, tt, tsl(tt)], score_r[:, tt, tsl(tt)].bitcast(F32), c_("negtri"), ALU.add)
                ins.then_inc(sem("topk_mask"), 1)
            elif s == "ds_L":
                row_max(l, [f"dL{i}" for i in range(4)], "ds_max", 40)
                normalise(l, [f"dL{i}" for i in range(4)], 48, "ds_probs")
            elif s == "ds_Y":
                full(ve, l, "dY")
                v.tensor_copy(yT[:, 0, :, :], bank2("dY")).then_inc(freed("dY"), 1)
            elif s == "fx_L":
                row_max(l, [f"fL{i}" for i in range(4)], "fx_max", 24)
                normalise(l, [f"fL{i}" for i in range(4)], 32, "fx_probs")
            elif s == "fx_O":
                full(ve, l, "fO")
                v.tensor_copy(yT[:, 3, :, :], bank2("fO")).then_inc(freed("fO"), 1)
            elif s == "ml_D":
                for i in range(3):
                    tt = 0 if i == 0 else 1
                    ns = P * (tt + 1)
                    full(ve, l, f"mD{i}")
                    at = 80 + 4 * tt + (0 if i == 0 else 2 * (i - 1))
                    v.reduce_max(stat[:, at:at + 512 // ns], bank2(f"mD{i}", ns), AX.X, negate=True).then_inc(sem("ml_max"), 1)
            elif s == "ml_qk":
                for i in range(3):
                    drained(ve, l, f"mD{i}")
                for h in range(4):
                    full(ve, l, f"mQ{h}")
                    for tt in range(TT):
                        ns = P * (tt + 1)
                        ins = stt(mlP[:, tt, h, 0:ns], bank(f"mQ{h}")[:, tt * P:tt * P + ns], 1.0, probs[:, tt, h, 0:ns],
                                  ALU.mult, ALU.mult, accum_out=stat[:, 100 + 4 * tt + h:101 + 4 * tt + h])
                    ins.then_inc(freed(f"mQ{h}"), 1)
                ve.wait_ge(sem("ml_floor"), l + 1)
                drained(ve, l, "mQ3")
                link(stt(stat[:, 100:108], stat[:, 100:108], -1.0, stat[:, 100:108], ALU.mult, ALU.max))
                link(tt_(stat[:, 100:108], stat[:, 100:108], stat[:, 88:96], ALU.max))
                link(v.reciprocal(stat[:, 100:108], stat[:, 100:108]))
            elif s == "ml_N":
                full(ve, l, "mN")
                tt_(cell.rearrange("p t (h d) -> p (t h) d", h=4), bank2("mN", 64),
                    stat[:, 100:108].unsqueeze(2).broadcast_to([P, 8, 64]), ALU.mult).then_inc(freed("mN"), 1)
                drained(ve, l, "mN")
                link(tt_(cell_sq, cell, cell, ALU.mult))
                v.reduce_sum(stat[:, 112:120], cell_sq.rearrange("p t (h d) -> p (t h) d", h=4), AX.X).then_inc(sem("ml_ss"), 1)
                ve.wait_ge(sem("ml_std"), l + 1)
                link(v.reciprocal(stat[:, 120:128], stat[:, 120:128]))
                c3 = cell.rearrange("p t (h d) -> p (t h) d", h=4)
                link(tt_(c3, c3, stat[:, 120:128].unsqueeze(2).broadcast_to([P, 8, 64]), ALU.mult))
                link(tt_(cell, cell, r_(l, "ml_g").unsqueeze(1).broadcast_to([P, TT, 256]), ALU.mult))
                ve.wait_ge(sem("ml_osig"), l + 1)
                tt_(cell, cell, osig, ALU.mult).then_inc(sem("ml_cell"), 1)
            elif s == "ml_Y":
                full(ve, l, "mY")
                v.tensor_copy(yT[:, 2, :, :], bank2("mY")).then_inc(freed("mY"), 1)
            elif s == "rw_mix":
                drained(ve, l, "z_rw0a")
                drained(ve, l, "z_rw1a")
                drained(ve, l, "z_rw1b")
                full(ve, l, "dY")
                full(ve, l, "mY")
                drained(ve, l, "dO1")
                link(tt_(Zm, Zr[:, :, 0:T], Zr[:, :, 1:], ALU.subtract))
                for b in range(8):
                    ins = stt(Zm[:, b, :], Zm[:, b, :], s_(l, "mu")[:, b:b + 1], Zr[:, b, 1:], ALU.mult, ALU.add)
                ins.then_inc(sem("rw_mixed"), 1)
                ve.wait_ge(sem("rw_mixed"), l + 1)
                for blk in range(2):
                    ins = ts(kkn[:, blk, :], Zm[:, 2 + blk, :], s_(l, "k_k")[:, blk:blk + 1], ALU.mult)
                link(ins)
                tt_(t0, kkn, kkn, ALU.mult).then_inc(sem("rw_kksq"), 1)
            elif s == "rw_lora":
                full(ve, l, "rKK")
                ts(cml.rearrange("p a b -> p (a b)"), bank("rKK")[:, :], 1e-24, ALU.max).then_inc(freed("rKK"), 1)
                ve.wait_ge(sem("rw_kstd"), l + 1)
                link(v.reciprocal(cml, cum))
                link(tt_(kkn, kkn, cml, ALU.mult))
            elif s == "rw_fm":
                drained(ve, l, "rW")
                link(ts(lw, lw, -DECAY, ALU.mult))
                for blk in range(2):
                    ins = v.tensor_tensor_scan(cum[:, blk, :], c_("reset"), lw[:, blk, :], 0.0, ALU.mult, ALU.add)
                link(ins)
                tt_(cml, cum, lw, ALU.subtract).then_inc(sem("rw_cum"), 1)
                drained(ve, l, "rA")
                for blk in range(2):
                    ins = ts(k2[:, blk, :], sa[:, blk, :], 1.0, ALU.subtract, s_(l, "k_a")[:, blk:blk + 1], ALU.mult)
                link(ins)
                stt(k2, k2, 1.0, Zm[:, 2:4, :], ALU.add, ALU.mult)
                for blk in range(2):
                    ins = ts(t0[:, blk, :], Zm[:, blk, :], s_(l, "r_k")[:, blk:blk + 1], ALU.mult)
                link(ins)
                tt_(t0, t0, k2, ALU.mult)
                link(tt_(sa, kkn, sa, ALU.mult))
                ve.wait_ge(sem("rw_exp"), l + 1)
                stt(AR[:, :, 0, :], kkn, -1.0, cml, ALU.mult, ALU.mult)
                tt_(AR[:, :, 1, :], Zm[:, 0:2, :], Wf, ALU.mult)
                tt_(sa, sa, cum, ALU.mult)
                tt_(k2, k2, cum, ALU.mult).then_inc(sem("rw_fm_done"), 1)
            elif s == "rw_tr":
                full(ve, l, "rBon")
                tt_(bon, bank2("rBon"), Zm[:, 4:6, :], ALU.mult).then_inc(freed("rBon"), 1)
            elif s == "rw_prod":
                for pre, dst in (("rLT", LQ), ("rKT", KQ)):
                    for h in range(4):
                        full(ve, l, f"{pre}{h}")
                        ins = tt_(dst[:, h, :, :], bank2(f"{pre}{h}"), c_("masks").unsqueeze(1).broadcast_to([P, TT, 256]), ALU.mult)
                        ins.then_inc(freed(f"{pre}{h}"), 1)
                drained(ve, l, "rLT3")
                lt = LQ.rearrange("p h t n -> p (h t) n")[:, :, 0:P]
                lvl = c_("level").rearrange("p (a b) -> p a b", a=6)
                link(tt_(XT, lt, lvl[:, 0:1, :].broadcast_to([P, 8, P]), ALU.mult))
                tt_(XT, XT, c_("ident").unsqueeze(1).broadcast_to([P, 8, P]), ALU.add).then_inc(sem("rw_xt0"), 1)
            elif s == "rw_app":
                drained(ve, l, "rtA")
                v.tensor_copy(ALV[:, :, 0:64].rearrange("p (h t) d -> p h t d", t=TT),
                              Atm.rearrange("p t (h d) -> p h t d", h=4))
                drained(ve, l, "rLkV")
                v.tensor_copy(stat[:, 131:132], c_("one")).then_inc(sem("rw_alv"), 1)
            elif s[:4] == "rw_m" and s[4:].isdigit():
                j = int(s[4])
                for i in range(2):
                    for ep, dst in ((f"rX{j}_{i}", X), (f"rT{j}_{i}", XT))[j == 5:]:
                        full(ve, l, ep)
                        d3 = dst[:, 4 * i:4 * i + 4, :]
                        tt_(d3, d3, bank2(ep, P), ALU.add).then_inc(freed(ep), 1)
            elif s == "rw_state":
                full(ve, l, "rRp")
                tt_(RpT, bank2("rRp"), AR[:, :, 1, :], ALU.add).then_inc(freed("rRp"), 1)
                for c in range(2):
                    full(ve, l, f"rP{c}")
                    tt_(PT[:, c, :, :, :].rearrange("p a b c -> p (a b) c"), bank(f"rP{c}")[:, 0:256].rearrange("p (a b) -> p a b", b=64),
                        c_("ident64").unsqueeze(1).broadcast_to([P, 4, 64]), ALU.add).then_inc(freed(f"rP{c}"), 1)
                last = Wf.rearrange("p a (n c) -> p a n c", c=64)[:, :, :, 63]
                for c in range(2):
                    full(ve, l, f"rG{c}")
                    for tt in range(TT):
                        ins = tt_(GW[:, c, :, tt, :], bank(f"rG{c}")[:, 0:256].rearrange("p (a t b) -> p a t b", t=TT, b=64)[:, :, tt, :],
                                  last[:, :, 2 * tt + c].unsqueeze(2).broadcast_to([P, 2, 64]), ALU.mult)
                    ins.then_inc(freed(f"rG{c}"), 1)
                drained(ve, l, "rG1")
                for ep, dst, c, tt in (("rS2", S2, 1, 0), ("rS3", S3, 0, 1)):
                    full(ve, l, ep)
                    for blk in range(2):
                        n = 2 * tt + c
                        ins = stt(dst[:, blk, :], bank(ep)[:, blk * 64:blk * 64 + 64], Wf[:, blk, 64 * n + 63:64 * n + 64],
                                  GW[:, c, blk, tt, :], ALU.mult, ALU.add)
                    ins.then_inc(freed(ep), 1)
            elif s == "rw_gn":
                full(ve, l, "rMean")
                drained(ve, l, "rY")
                tt_(Yc, Ys, bank2("rMean"), ALU.subtract).then_inc(freed("rMean"), 1)
                drained(ve, l, "rMean")
                v.tensor_copy(stat[:, 132:133], c_("one")).then_inc(sem("rw_yc"), 1)
                drained(ve, l, "rVar")
                link(v.reciprocal(lw, lw))
                link(tt_(Yc, Yc, lw, ALU.mult))
                for blk in range(2):
                    ins = ts(Yc[:, blk, :], Yc[:, blk, :], s_(l, "ln_g")[:, blk:blk + 1], ALU.mult, s_(l, "ln_b")[:, blk:blk + 1], ALU.add)
                link(ins)
                link(tt_(Yc, Yc, bon, ALU.add))
                tt_(yT[:, 1, :, :], Yc, gout, ALU.mult).then_inc(sem("rwkv_out"), 1)
            elif s[:2] == "br":
                bi = int(s[2])
                for half in range(2):
                    for tt, ep in ((0, f"br{bi}{half}a"), (1, f"br{bi}{half}b")):
                        cols = slice(half * 512, half * 512 + 512)
                        full(ve, l, ep)
                        if half == 0:
                            drained(ve, l, f"gate{bi}0b")
                            drained(ve, l, f"gate{bi}1b")
                        g = gates[:, bi % 2, tt, cols]
                        if bi == 0:
                            tt_(xn[:, tt, cols], bank(ep)[:, :], g, ALU.mult).then_inc(freed(ep), 1)
                        else:
                            tt_(mtmp, bank(ep)[:, :], g, ALU.mult).then_inc(freed(ep), 1)
                            drained(ve, l, ep)
                            ins = tt_(xn[:, tt, cols], xn[:, tt, cols], mtmp, ALU.add)
                            if tt == 1 and bi == 3:
                                ins.then_inc(sem("merged"), 1)
                                ve.wait_ge(sem("merged"), 2 * l + half + 1)
                            else:
                                link(ins)
            elif s[:3] == "out":
                half = int(s[3])
                for tt, ep in ((0, s + "a"), (1, s + "b")):
                    cols = slice(half * 512, half * 512 + 512)
                    full(ve, l, ep)
                    tt_(x[:, tt, cols], x[:, tt, cols], bank(ep)[:, :], ALU.add).then_inc(freed(ep), 1)

        ve.wait_ge(sem("const_in"), 16)
        for name in ROUNDED:
            at, n = CONST[name]
            ins = v.tensor_copy(exact(name), const[:, at:at + n])
        ins.then_inc(sem("const_ready"), 1)
        ve.wait_ge(sem("const_ready"), 1)
        ve.wait_ge(sem("x_in"), 16)
        for l in range(LAYERS):
            for s in SCHEDULE:
                following = next_split(l, s) if s in SPLIT_GROUPS else None
                if following is not None:
                    split_lo(following)
                step_vec(l, s)
                for group_, at in SPLIT_LATER.items():
                    if s == at:
                        split_lo(next_split(l, group_) + 1)
                if following not in (None, FIRST_DENSE) and s not in SPLIT_LATER:
                    split_lo(following + 1)
            if l == 0:
                def dense_mul(g):
                    for b in range(4 * g, min(4 * g + 4, DENSE_BLOCKS)):
                        ve.wait_ge(sem("dense_silu"), b + 1)
                        tt_(dsil[:, b % 4, :], dsil[:, b % 4, :], pb[(0 if g % 2 else 4) + b % 4][:, T:2 * T], ALU.mult)\
                            .then_inc(sem("dense_mul"), 1)

                def dense_low(g):
                    for b in range(4 * g, min(4 * g + 4, DENSE_BLOCKS)):
                        ve.wait_ge(sem("dense_high"), b + 1)
                        tt_(denseT_l[:, b, :], dsil[:, b % 4, :], denseT_h[:, b, :].bitcast(F32), ALU.subtract).then_inc(sem("dense_act"), 1)

                for n in range(DENSE_PIECES):
                    if n >= HIGH_MIX:
                        split_lo(FIRST_DENSE + n)
                    g = n // 4
                    if 1 <= g <= DENSE_GROUPS and n % 4 == 1:
                        dense_mul(g - 1)
                    if 1 <= g <= DENSE_GROUPS and n % 4 == 2:
                        dense_low(g - 1)
                for tt in range(TT):
                    ve.wait_ge(sem("dense_down"), tt + 1)
                    for half in range(2):
                        cols = slice(half * 512, half * 512 + 512)
                        ins = tt_(x[:, tt, cols], x[:, tt, cols], pb[4 + 2 * tt + half][:, :], ALU.add)
                    ins.then_inc(sem("x_fed"), 1)

        E1 = EXPERTS + 1
        v.memset(took[:, :, :], 0.0)
        v.memset(weight[:, :, :], 0.0)
        v.memset(rtmp[:, :, 8:24], ABSENT)
        link(v.memset(rank[:, :, :], 0.0))
        v.memset(pickT[:, :], 0.0)
        v.memset(yexp[:, :], 0.0).then_inc(sem("main_ready"), 1)
        ve.wait_ge(sem("router_logits"), 1)
        link(v.tensor_copy(rtmp[:, :, 0:8], pb[4][:, 0:16].rearrange("p (t e) -> p t e", t=TT)))
        for tt in range(TT):
            ins = v.max(rtmp[:, tt, 24:32], rtmp[:, tt, 0:8])
        link(ins)
        v.tensor_copy(rtmp[:, :, 8:9], rtmp[:, :, 24:25])
        v.tensor_copy(rtmp[:, :, 16:17], rtmp[:, :, 25:26])
        link(tt_(rtmp[:, :, 33:34], rtmp[:, :, 25:26], rtmp[:, :, 24:25], ALU.subtract))
        for r in range(2):
            for tt in range(TT):
                ins = v.match_replace(rtmp[:, tt, 40 + 8 * r:48 + 8 * r], rtmp[:, tt, 8 + 8 * r:16 + 8 * r],
                                      rtmp[:, tt, 40:48] if r else rtmp[:, tt, 0:8], TAKEN)
            link(ins)
        v.tensor_copy(stat[:, 134:135], c_("one")).then_inc(sem("top2_gap"), 1)
        for tt in range(TT):
            ts(took[:, tt, 0:8], rtmp[:, tt, 48:56], TAKEN, ALU.is_equal)
            ins = ts(rtmp[:, tt, 56:64], rtmp[:, tt, 40:48], TAKEN, ALU.is_equal)
        ins.then_inc(sem("took_done"), 1)
        ve.wait_ge(sem("took_done"), 1)
        ve.wait_ge(sem("top2_exp"), 1)
        link(ts(rtmp[:, :, 35:36], rtmp[:, :, 34:35], 1.0, ALU.add))
        link(v.reciprocal(rtmp[:, :, 36:37], rtmp[:, :, 35:36]))
        link(tt_(rtmp[:, :, 37:38], rtmp[:, :, 34:35], rtmp[:, :, 36:37], ALU.mult))
        for tt in range(TT):
            ins = tt_(rtmp[:, tt, 0:8], took[:, tt, 0:8], rtmp[:, tt, 56:64], ALU.subtract)
        link(ins)
        for tt in range(TT):
            ins = ts(weight[:, tt, 0:8], rtmp[:, tt, 0:8], rtmp[:, tt, 37:38], ALU.mult)
        link(ins)
        for tt in range(TT):
            ins = stt(weight[:, tt, 0:8], rtmp[:, tt, 56:64], rtmp[:, tt, 36:37], weight[:, tt, 0:8], ALU.mult, ALU.add)
        link(ins)
        ve.wait_ge(sem("ranks"), 1)
        link(v.tensor_copy(rank[:, :, :], pb[5][:, 0:2 * E1].rearrange("p (t e) -> p t e", t=TT)))
        link(v.tensor_reduce(over[:, 0:1], pb[5][:, 2 * E1:3 * E1], AX.X, ALU.max))
        link(ts(over[:, 1:2], over[:, 0:1], float(P), ALU.is_gt))
        v.tensor_copy(over_i[:, 0:1], over[:, 1:2]).then_inc(sem("over_known"), 1)
        ve.wait_ge(sem("over_known"), 1)

        def experts_vec(tag, first_slot, first):
            iota = c_("iota")[:, first_slot:first_slot + P]

            def choose(e):
                for tt in range(TT):
                    ts(pick[:, tt, :], iota, rank[:, tt, bass.ds(e, 1)], ALU.is_equal, took[:, tt, bass.ds(e, 1)], ALU.mult)
                    ins = ts(pickg[:, tt, :], iota, rank[:, tt, bass.ds(e, 1)], ALU.is_equal, weight[:, tt, bass.ds(e, 1)], ALU.mult)
                ins.then_inc(sem(tag + "pick"), 1)

            if tag == "over_":
                v.memset(yexp[:, :], 0.0).then_inc(sem("over_ready"), 1)
            choose(0)
            g_ffn = s_(1, "g_ffn")

            def hsel_low(count):
                for k in range(KC):
                    if k % 4 == 0:
                        ve.wait_ge(sem(tag + "hsel_high"), count(k + 4))
                    ins = stt(hsel_l[:, k, :], pb[2 + k // 4][:, (k % 4) * P:(k % 4) * P + P], g_ffn[:, k:k + 1],
                              hsel_h[:, k, :].bitcast(F32), ALU.mult, ALU.subtract)
                ins.then_inc(sem(tag + "hsel"), 1)

            with ve.Fori(0, EXPERTS) as e:
                def lo(j):
                    split_lo(first + j, e)

                def yexp_in():
                    ve.wait_ge(sem(tag + "down"), e + 1)
                    v.tensor_copy(yexp[:, 0:512], pb[4][:, :])
                    v.tensor_copy(yexp[:, 512:1024], pb[5][:, :]).then_inc(sem(tag + "yexp"), 1)

                def add(tt):
                    for half in range(2):
                        cols = slice(half * 512, half * 512 + 512)
                        ve.wait_ge(sem(tag + "scattered"), e * 4 + (2 * tt + half + 1))
                        tt_(x[:, tt, cols], x[:, tt, cols], pb[4 + half][:, :], ALU.add).then_inc(sem(tag + "added"), 1)

                def gate_up(g):
                    ve.wait_ge(sem(tag + "silu"), e * EXP_GROUPS + (g + 1))
                    tt_(act[:, g % 2, :], sil[:, g % 2, :], pb[2 * (g % 2) + 1][:, :], ALU.mult).then_inc(sem(tag + "act"), 1)

                def actT_low(g):
                    ve.wait_ge(sem(tag + "actT_high"), e * EXP_GROUPS + (g + 1))
                    tt_(actT_l[:, 4 * g:4 * g + 4, :].rearrange("p a b -> p (a b)"), pb[6][:, :],
                        actT_h[:, 4 * g:4 * g + 4, :].rearrange("p a b -> p (a b)").bitcast(F32), ALU.subtract).then_inc(sem(tag + "actT"), 1)

                for g in range(EXP_GROUPS + 1):
                    lo(4 * g)
                    if g == 0:
                        hsel_low(lambda k: e * KC + k)
                    lo(4 * g + 1)
                    if g >= 1:
                        gate_up(g - 1)
                    if g >= 2:
                        actT_low(g - 2)
                    if g == 1:
                        add(0)
                    if g == 0:
                        yexp_in()
                    if g == 4:
                        choose(ve.snap(e + 1))
                    if g < EXP_GROUPS:
                        lo(4 * g + 2)
                        if g == 2:
                            add(1)
                        lo(4 * g + 3)
                actT_low(EXP_GROUPS - 1)
                for j in range(4 * EXP_GROUPS + 2, EXP_PIECES):
                    lo(j)
            ve.wait_ge(sem(tag + "down"), EXPERTS + 1)
            v.tensor_copy(yexp[:, 0:512], pb[4][:, :])
            v.tensor_copy(yexp[:, 512:1024], pb[5][:, :]).then_inc(sem(tag + "yexp"), 1)
            for tt in range(TT):
                for half in range(2):
                    cols = slice(half * 512, half * 512 + 512)
                    ve.wait_ge(sem(tag + "scattered"), EXPERTS * 4 + 2 * tt + half + 1)
                    tt_(x[:, tt, cols], x[:, tt, cols], pb[4 + half][:, :], ALU.add).then_inc(sem(tag + "added"), 1)

        experts_vec("main_", 0, FIRST_EXPERT)
        more = ve.value_load(over_i[0:1, 0:1], min_val=0, max_val=1)
        with ve.If(more > 0):
            ve.wait_ge(sem("main_added"), 4 * EXPERTS + 4)
            experts_vec("over_", P, PIECES)
        ve.wait_ge(sem("main_added"), 4 * EXPERTS + 4)
        for tt in range(TT):
            v.tensor_copy(stat[:, 136 + tt:137 + tt], c_("one")).then_inc(sem("x_fed"), 1)
        ve.wait_ge(sem("final_in"), 16)
        for tt in range(TT):
            ve.wait_ge(sem("norm_std"), TT * 2 * LAYERS + tt + 1)
            link(v.reciprocal(stat[:, 4 + tt:5 + tt], stat[:, 2 + tt:3 + tt]))
            stt(xn[:, tt, :], x[:, tt, :], stat[:, 4 + tt:5 + tt], final_g, ALU.mult, ALU.mult).then_inc(sem("out_ready"), 1)

    @block.gpsimd
    def _(gp):
        lt = LQ.rearrange("p h t n -> p (h t) n")[:, :, 0:P]
        lvl = c_("level").rearrange("p (a b) -> p a b", a=6)
        for l in range(LAYERS):
            if l == 0:
                gp.wait_ge(sem("const_in"), 16)
            else:
                drained(gp, l - 1, "norm_ffn3")
                gp.dma_start(small[:, :], small_in[l]).then_inc(sem(f"small{l}_in"), 16)
                gp.dma_start(row[:, :], row_in[l:l + 1, :].broadcast_to([P, N_ROW])).then_inc(sem(f"row{l}_in"), 16)
            drained(gp, l, "rLT3")
            for j in range(1, 6):
                if j >= 3:
                    full(gp, l, f"rZ{j - 2}_1")
                nc.gpsimd.tensor_tensor(lev[:, j % 2, :, :], lt, lvl[:, j:j + 1, :].broadcast_to([P, 8, P]), ALU.mult)\
                  .then_inc(sem("rw_level"), 1)
        drained(gp, 1, "out1b")
        gp.dma_start(final_g, final_in.broadcast_to([P, D])).then_inc(sem("final_in"), 16)

    ctx_block.__exit__(None, None, None)


def lay_out(inputs):
    f = {k: np.ascontiguousarray(a) for k, a in inputs.items()}
    pieces = np.zeros((PIECES, P, PIECE), np.float32)

    def columns(n, w):
        v = w.reshape(2, 4, P, w.shape[1]).transpose(0, 2, 1, 3)
        pieces[n:n + 2].reshape(2, P, 4, 512)[:, :, :, :w.shape[1]] = v
        return n + 2

    def rows(n, w):
        m = w.shape[0] // 256
        pieces[n:n + m].reshape(m, P, 2, D)[...] = w.reshape(m, 2, P, D).transpose(0, 2, 1, 3)
        return n + m

    n = 0
    for l in range(LAYERS):
        for s in SCHEDULE:
            if s in GROUPS:
                w = np.zeros((D, 512), np.float32)
                for src, width, dst in GROUPS[s]:
                    w[:, dst:dst + width] = f["w_in"][l][:, src:src + width]
                n = columns(n, w)
            elif s[:2] == "br":
                n = rows(n, f["w_branch"][l, BRANCH_ORDER[int(s[2])]])
            elif s[:3] == "out":
                h = int(s[3])
                n = columns(n, f["w_out"][l][:, 512 * h:512 * h + 512])
        if l == 0:
            for g in range(DENSE_GROUPS):
                for w in (f["ffn_w1"][0], f["ffn_w3"][0]):
                    n = columns(n, w[:, 512 * g:512 * g + 512])
            n = rows(n, f["ffn_w2"][0])
    for e in range(EXPERTS):
        for g in range(EXP_GROUPS):
            for w in (f["moe_w1"][0, e], f["moe_w3"][0, e]):
                n = columns(n, w[:, 512 * g:512 * g + 512])
        n = rows(n, f["moe_w2"][0, e])
    assert n == PIECES

    small = np.zeros((LAYERS, P, N_SMALL), np.float32)

    def put(l, name, value, rows_=slice(None)):
        at, width = SMALL[name]
        small[l, rows_, at:at + width] = value

    for l in range(LAYERS):
        put(l, "w_uq", f["dsa_w_uq"][l].reshape(P, 512))
        put(l, "w_qidx", f["dsa_w_qidx"][l].reshape(P, 256))
        put(l, "w_uv", f["dsa_w_uv"][l].transpose(1, 0, 2).reshape(P, 256))
        put(l, "wa_up", f["rwkv_w_up"][l], slice(0, 64))
        put(l, "wa_up", f["rwkv_a_up"][l], slice(64, 128))
        put(l, "g_up", f["rwkv_g_up"][l])
        put(l, "g_mix", f["norm_mix_g"][l].reshape(KC, P).T)
        put(l, "g_ffn", f["norm_ffn_g"][l].reshape(KC, P).T)
        put(l, "mu", f["rwkv_mu"][l].reshape(8, P).T)
        for name, src in (("w0", "rwkv_w0"), ("a0", "rwkv_a0"), ("k_k", "rwkv_k_k"), ("k_a", "rwkv_k_a"),
                          ("r_k", "rwkv_r_k"), ("ln_g", "rwkv_ln_g"), ("ln_b", "rwkv_ln_b"), ("conv_b", "mlstm_conv_b")):
            put(l, name, f[src][l].reshape(2, P).T)
        put(l, "conv_w", f["mlstm_conv_w"][l].reshape(8, P).T)
        for at, src in ((0, "mlstm_b_i"), (32, "mlstm_b_f"), (64, "fox_b_f")):
            put(l, "gate_b", f[src][l].reshape(4, 1), slice(at, at + 4))
    put(1, "router", f["moe_router"][0].reshape(KC, P, EXPERTS).transpose(1, 0, 2).reshape(P, 64))
    row = np.concatenate([f[k] for k in ("dsa_g_cq", "dsa_g_ckv", "dsa_g_kidx", "mlstm_norm_g")], axis=1)
    return {"x": f["x"], "stream": pieces, "small": small, "row": row, "const": constants(),
            "final_g": f["final_norm_g"].reshape(1, D)}


def kernel(**inputs):
    import concourse.bacc as bacc
    from concourse.bass_utils import run_bass_kernel_spmd

    arrays = lay_out(inputs)
    nc = bacc.Bacc("TRN2", target_bir_lowering=False, num_devices=1)
    args = [nc.dram_tensor(k, a.shape, F32, kind="ExternalInput").ap() for k, a in arrays.items()]
    out = nc.dram_tensor("y", (1, T, D), F32, kind="ExternalOutput").ap()
    build(nc, *args, out)
    r = run_bass_kernel_spmd(nc, [arrays], core_ids=[0])
    return r.results[0]["y"]
```
